# Optimizing a Trainium2 kernel written in Bass

```python
import math
import jax, jax.numpy as jnp
from jax import lax
import numpy as np

D_MODEL = 1024
BATCH = 1
SEQ = 1024
DEPTH = 1

HEAD_DIM = 64
N_HEADS_DIL = D_MODEL // (2 * HEAD_DIM)
N_HEADS_NA = D_MODEL // (2 * HEAD_DIM)
WIDTH_DIL = N_HEADS_DIL * HEAD_DIM
WIDTH_NA = N_HEADS_NA * HEAD_DIM
MIX_WIDTH = WIDTH_DIL + WIDTH_NA
DIL_PATTERNS = ((128, 1), (512, 4), (2048, 16))
DIL_BLOCK = 64
GRID_W = 64
NA_WIN_ROWS = 8
NA_WIN_COLS = 16
NA_Q_ROWS = 4
NA_Q_COLS = 16
NA_K_COLS = 32
N_GROUPS = 4
EXPERTS_PER_GROUP = 4
N_EXPERTS = N_GROUPS * EXPERTS_PER_GROUP
TOP_K_EXPERT = 2
D_EXPERT = 256
RMS_EPS = 1e-6
NEG_INF = -1e30


def rms_norm(x, gain):
    xf = x.astype(jnp.float32)
    xf = xf * lax.rsqrt(jnp.mean(xf * xf, axis=-1, keepdims=True) + RMS_EPS)
    return (xf * gain.astype(jnp.float32)).astype(x.dtype)

def alibi_slopes(n_heads):
    return jnp.exp2(-8.0 * jnp.arange(1, n_heads + 1, dtype=jnp.float32) / n_heads)

def dilated_window_attention(q, k, v, slopes, window, dilation):
    B, H, S, Dh = q.shape
    L = S // dilation
    radius = (window // 2) // dilation
    blk = DIL_BLOCK
    n_blk = -(-L // blk)
    Lp = n_blk * blk

    def residue_major(t, lo, hi):
        t = t.reshape(B, H, L, dilation, Dh).transpose(0, 1, 3, 2, 4)
        return jnp.pad(t, ((0, 0), (0, 0), (0, 0), (lo, hi), (0, 0)))

    def key_blocks(t):
        tp = residue_major(t, blk, Lp - L + blk).reshape(B, H, dilation, n_blk + 2, blk, Dh)
        return jnp.concatenate([tp[:, :, :, i:i + n_blk] for i in range(3)], axis=4)

    qb = residue_major(q, 0, Lp - L).reshape(B, H, dilation, n_blk, blk, Dh)
    kb = key_blocks(k)
    vb = key_blocks(v)

    q_pos = jnp.arange(Lp).reshape(n_blk, blk)
    k_pos = (jnp.arange(n_blk)[:, None] - 1) * blk + jnp.arange(3 * blk)[None, :]
    off = jnp.abs(k_pos[:, None, :] - q_pos[:, :, None])
    valid = ((off <= radius) & (k_pos[:, None, :] >= 0) & (k_pos[:, None, :] < L)
             & (q_pos[:, :, None] < L))
    dist = (off * dilation).astype(jnp.float32)

    s = jnp.einsum('bhrnqd,bhrnkd->bhrnqk', qb, kb).astype(jnp.float32) * (HEAD_DIM ** -0.5)
    s = s - slopes[None, :, None, None, None, None] * dist
    s = jnp.where(valid, s, NEG_INF)
    mx = jnp.max(s, axis=-1, keepdims=True)
    p = jnp.exp(s - mx)
    den = jnp.sum(p, axis=-1)
    o = jnp.einsum('bhrnqk,bhrnkd->bhrnqd', p, vb.astype(jnp.float32)) / den[..., None]
    lse = mx[..., 0] + jnp.log(den)

    o = o.reshape(B, H, dilation, Lp, Dh)[:, :, :, :L].transpose(0, 1, 3, 2, 4).reshape(B, H, S, Dh)
    lse = lse.reshape(B, H, dilation, Lp)[..., :L].transpose(0, 1, 3, 2).reshape(B, H, S)
    return o, lse

def dilated_mixture_attention(q, k, v, slopes):
    results = [dilated_window_attention(q, k, v, slopes, w, d) for (w, d) in DIL_PATTERNS]
    outs = jnp.stack([r[0] for r in results])
    lses = jnp.stack([r[1] for r in results])
    weights = jax.nn.softmax(lses, axis=0)
    return jnp.sum(weights[..., None] * outs, axis=0).astype(q.dtype)

def neighbourhood_attention(q, k, v, rpb):
    B, H, S, Dh = q.shape
    rows = S // GRID_W
    wh = min(NA_WIN_ROWS, rows)
    q_rows = math.gcd(rows, NA_Q_ROWS)
    k_rows = min(wh + q_rows - 1, rows)
    n_rb = rows // q_rows
    n_cb = GRID_W // NA_Q_COLS

    r = jnp.arange(rows)
    c = jnp.arange(GRID_W)
    row_start = jnp.clip(r - wh // 2, 0, rows - wh)
    col_start = jnp.clip(c - NA_WIN_COLS // 2, 0, GRID_W - NA_WIN_COLS)
    key_row = jnp.clip(row_start[::q_rows], 0, rows - k_rows)[:, None] + jnp.arange(k_rows)
    key_col = (jnp.clip(jnp.arange(n_cb) * NA_Q_COLS - NA_WIN_COLS // 2, 0, GRID_W - NA_K_COLS)[:, None]
               + jnp.arange(NA_K_COLS))

    q_row = r.reshape(n_rb, q_rows)
    q_col = c.reshape(n_cb, NA_Q_COLS)
    rs = row_start.reshape(n_rb, q_rows)[:, :, None]
    cs = col_start.reshape(n_cb, NA_Q_COLS)[:, :, None]
    row_ok = (key_row[:, None, :] >= rs) & (key_row[:, None, :] < rs + wh)
    col_ok = (key_col[:, None, :] >= cs) & (key_col[:, None, :] < cs + NA_WIN_COLS)
    mask = row_ok[:, None, :, None, :, None] & col_ok[None, :, None, :, None, :]
    dr = jnp.clip(key_row[:, None, :] - q_row[:, :, None] + NA_WIN_ROWS - 1, 0, 2 * NA_WIN_ROWS - 2)
    dc = jnp.clip(key_col[:, None, :] - q_col[:, :, None] + NA_WIN_COLS - 1, 0, 2 * NA_WIN_COLS - 2)
    bias = rpb[:, dr[:, None, :, None, :, None], dc[None, :, None, :, None, :]].astype(jnp.float32)

    def grid(t):
        return t.reshape(B, H, rows, GRID_W, Dh)

    qb = grid(q).reshape(B, H, n_rb, q_rows, n_cb, NA_Q_COLS, Dh).transpose(0, 1, 2, 4, 3, 5, 6)
    ridx = key_row[:, None, :, None]
    cidx = key_col[None, :, None, :]
    kg = grid(k)[:, :, ridx, cidx]
    vg = grid(v)[:, :, ridx, cidx]

    s = jnp.einsum('bhijqcd,bhijkld->bhijqckl', qb, kg).astype(jnp.float32) * (HEAD_DIM ** -0.5)
    s = jnp.where(mask, s + bias[None], NEG_INF)
    p = jax.nn.softmax(s, axis=(-2, -1))
    o = jnp.einsum('bhijqckl,bhijkld->bhijqcd', p, vg.astype(jnp.float32))
    o = o.transpose(0, 1, 2, 4, 3, 5, 6).reshape(B, H, S, Dh)
    return o.astype(q.dtype)

def hierarchical_moe(x, w_group, b_group, w_router, b_router, w_gate, w_up, w_down):
    B, S, D = x.shape
    n_tok = B * S
    xf = x.reshape(n_tok, D)
    g_logits = (xf @ w_group).astype(jnp.float32) + b_group.astype(jnp.float32)
    g_weight, g_idx = lax.top_k(jax.nn.softmax(g_logits, axis=-1), 1)
    e_logits = ((xf @ w_router).astype(jnp.float32) + b_router.astype(jnp.float32)
                ).reshape(n_tok, N_GROUPS, EXPERTS_PER_GROUP)
    e_in_group = jnp.take_along_axis(e_logits, g_idx[:, :, None], axis=1)[:, 0]
    e_val, e_idx = lax.top_k(e_in_group, TOP_K_EXPERT)
    e_weight = jax.nn.softmax(e_val, axis=-1) * g_weight
    expert_id = g_idx * EXPERTS_PER_GROUP + e_idx
    combine = jnp.sum(jax.nn.one_hot(expert_id, N_EXPERTS, dtype=jnp.float32) * e_weight[..., None], axis=1)
    gate = jnp.einsum('nd,edf->nef', xf, w_gate)
    up = jnp.einsum('nd,edf->nef', xf, w_up)
    act = jax.nn.silu(gate) * up * combine[:, :, None].astype(x.dtype)
    out = jnp.einsum('nef,efd->nd', act, w_down)
    return out.reshape(B, S, D).astype(x.dtype)

def first_inputs(seed: int = 0) -> dict:
    key = jax.random.key(seed)
    ks = jax.random.split(key, 17)
    f32 = jnp.float32

    def nrm(k, shape, scale):
        return jax.random.normal(k, shape, f32) * scale

    return {
        'x': nrm(ks[0], (BATCH, SEQ, D_MODEL), 1.0),
        'norm_mix_g': 1.0 + nrm(ks[1], (DEPTH, D_MODEL), 0.02),
        'w_in': nrm(ks[2], (DEPTH, D_MODEL, 3 * MIX_WIDTH), D_MODEL ** -0.5),
        'rpb': nrm(ks[3], (DEPTH, N_HEADS_NA, 2 * NA_WIN_ROWS - 1, 2 * NA_WIN_COLS - 1), 0.1),
        'g_out_dil': 1.0 + nrm(ks[4], (DEPTH, WIDTH_DIL), 0.02),
        'g_out_na': 1.0 + nrm(ks[5], (DEPTH, WIDTH_NA), 0.02),
        'w_out': nrm(ks[6], (DEPTH, MIX_WIDTH, D_MODEL), MIX_WIDTH ** -0.5),
        'norm_ffn_g': 1.0 + nrm(ks[7], (DEPTH, D_MODEL), 0.02),
        'w_group': nrm(ks[8], (DEPTH, D_MODEL, N_GROUPS), D_MODEL ** -0.5),
        'b_group': nrm(ks[9], (DEPTH, N_GROUPS), 0.01),
        'w_router': nrm(ks[10], (DEPTH, D_MODEL, N_EXPERTS), D_MODEL ** -0.5),
        'b_router': nrm(ks[11], (DEPTH, N_EXPERTS), 0.01),
        'w_gate': nrm(ks[12], (DEPTH, N_EXPERTS, D_MODEL, D_EXPERT), D_MODEL ** -0.5),
        'w_up': nrm(ks[13], (DEPTH, N_EXPERTS, D_MODEL, D_EXPERT), D_MODEL ** -0.5),
        'w_down': nrm(ks[14], (DEPTH, N_EXPERTS, D_EXPERT, D_MODEL), D_EXPERT ** -0.5),
        'norm_final_g': 1.0 + nrm(ks[15], (D_MODEL,), 0.02),
    }

def first_block(x, norm_mix_g, w_in, rpb, g_out_dil, g_out_na, w_out, norm_ffn_g,
              w_group, b_group, w_router, b_router, w_gate, w_up, w_down, norm_final_g):
    B, S, _ = x.shape
    slopes = alibi_slopes(N_HEADS_DIL)
    h = x
    for layer in range(DEPTH):
        hn = rms_norm(h, norm_mix_g[layer])
        proj = hn @ w_in[layer]
        p_dil = proj[..., :3 * WIDTH_DIL].reshape(B, S, 3, N_HEADS_DIL, HEAD_DIM).transpose(2, 0, 3, 1, 4)
        p_na = proj[..., 3 * WIDTH_DIL:].reshape(B, S, 3, N_HEADS_NA, HEAD_DIM).transpose(2, 0, 3, 1, 4)
        y_dil = dilated_mixture_attention(p_dil[0], p_dil[1], p_dil[2], slopes)
        y_na = neighbourhood_attention(p_na[0], p_na[1], p_na[2], rpb[layer])
        y_dil = rms_norm(y_dil.transpose(0, 2, 1, 3).reshape(B, S, WIDTH_DIL), g_out_dil[layer])
        y_na = rms_norm(y_na.transpose(0, 2, 1, 3).reshape(B, S, WIDTH_NA), g_out_na[layer])
        h = h + jnp.concatenate([y_dil, y_na], axis=-1) @ w_out[layer]
        h = h + hierarchical_moe(rms_norm(h, norm_ffn_g[layer]), w_group[layer], b_group[layer],
                                 w_router[layer], b_router[layer], w_gate[layer], w_up[layer], w_down[layer])
    return rms_norm(h, norm_final_g)


D_MIX = D_MODEL
EPS = 1e-6
GLA_HEADS = 4
GLA_DV_TOTAL = D_MIX // 2
GLA_DK_TOTAL = GLA_DV_TOTAL // 2
GLA_DK = GLA_DK_TOTAL // GLA_HEADS
GLA_DV = GLA_DV_TOTAL // GLA_HEADS
GLA_LOW_RANK = 16
GLA_GATE_NORM = 16.0
GLA_CHUNK = 64
S5_WIDTH = D_MIX // 4
S5_GROUP = 16
S5_GROUPS = S5_WIDTH // S5_GROUP
S5_STATE = 64
S5_DT_MIN = 1e-3
S5_DT_MAX = 1e-1
RG_WIDTH = D_MIX // 4
RG_HEADS = 4
RG_HEAD_DIM = RG_WIDTH // RG_HEADS
RG_CONV = 4
RG_C = 8.0
D_FF = 2816
FFN_CONV = 3
IN_SIZES = (GLA_DK_TOTAL, GLA_DK_TOTAL, GLA_DV_TOTAL, GLA_DV_TOTAL, GLA_LOW_RANK, S5_WIDTH, RG_WIDTH, RG_WIDTH)
D_IN = 2 * GLA_DK_TOTAL + 2 * GLA_DV_TOTAL + GLA_LOW_RANK + S5_WIDTH + 2 * RG_WIDTH


def rmsnorm(x, g):
    xf = x.astype(jnp.float32)
    y = xf * lax.rsqrt(jnp.mean(xf * xf, axis=-1, keepdims=True) + EPS)
    return y.astype(x.dtype) * g

def causal_dwconv(x, w, b):
    k, c = w.shape
    y = lax.conv_general_dilated(x, w[:, None, :].astype(x.dtype), window_strides=(1,),
                                 padding=[(k - 1, 0)], dimension_numbers=('NWC', 'WIO', 'NWC'),
                                 feature_group_count=c)
    return y + b

def linear_rec_combine(e1, e2):
    a1, x1 = e1
    a2, x2 = e2
    return a2 * a1, a2 * x1 + x2

def gla_mixer(q, k, v, g, gk_low, w_gk_up, b_gk, norm_g):
    B, L, _ = q.shape
    H, DK, DV, C = GLA_HEADS, GLA_DK, GLA_DV, GLA_CHUNK
    n = L // C
    f32 = jnp.float32
    gk = jax.nn.log_sigmoid((gk_low @ w_gk_up + b_gk).astype(f32)) / GLA_GATE_NORM

    def chunks(t, d):
        return t.reshape(B, n, C, H, d).transpose(0, 3, 1, 2, 4)

    qc = chunks(q.astype(f32) * (DK ** -0.5), DK)
    kc = chunks(k.astype(f32), DK)
    vc = chunks(v.astype(f32), DV)
    bc = jnp.cumsum(chunks(gk, DK), axis=3)
    b_mid = bc[:, :, :, C // 2 - 1:C // 2]
    scores = jnp.einsum('bhncd,bhnsd->bhncs', qc * jnp.exp(bc - b_mid), kc * jnp.exp(b_mid - bc))
    causal = jnp.tril(jnp.ones((C, C), dtype=bool))
    scores = jnp.where(causal, scores, 0.0)
    o_intra = jnp.einsum('bhncs,bhnsv->bhncv', scores, vc)
    b_last = bc[:, :, :, -1]
    kv = jnp.einsum('bhnsd,bhnsv->bhndv', kc * jnp.exp(b_last[:, :, :, None] - bc), vc)
    decay = jnp.exp(b_last)

    def step(S, inp):
        dec, kv_n = inp
        return dec[..., None] * S + kv_n, S

    S0 = jnp.zeros((B, H, DK, DV), f32)
    _, S_prev = lax.scan(step, S0, (jnp.moveaxis(decay, 2, 0), jnp.moveaxis(kv, 2, 0)))
    S_prev = jnp.moveaxis(S_prev, 0, 2)
    o_inter = jnp.einsum('bhncd,bhndv->bhncv', qc * jnp.exp(bc), S_prev)
    o = (o_intra + o_inter).transpose(0, 2, 3, 1, 4).reshape(B, L, H, DV)
    o = rmsnorm(o, norm_g).reshape(B, L, H * DV).astype(q.dtype)
    return o * jax.nn.silu(g)

def s5_mixer(u, lam_re, lam_im, log_dt, b_re, b_im, c_re, c_im, d, w_glu, b_glu):
    B, L, _ = u.shape
    f32 = jnp.float32
    uf = u.astype(f32)
    ug = uf.reshape(B, L, S5_GROUPS, S5_GROUP).astype(jnp.complex64)
    lam = lax.complex(lam_re.astype(f32), lam_im.astype(f32))
    dt = jnp.exp(log_dt.astype(f32))[:, None]
    lam_bar = jnp.exp(lam * dt)
    b = lax.complex(b_re.astype(f32), b_im.astype(f32))
    b_bar = ((lam_bar - 1.0) / lam)[..., None] * b
    bu = jnp.einsum('gph,blgh->blgp', b_bar, ug)
    a = jnp.broadcast_to(lam_bar, bu.shape)
    _, states = lax.associative_scan(linear_rec_combine, (a, bu), axis=1)
    c = lax.complex(c_re.astype(f32), c_im.astype(f32))
    y = jnp.einsum('ghp,blgp->blgh', c, states).real.reshape(B, L, S5_WIDTH) + d * uf
    y = jax.nn.gelu(y)
    y = y * jax.nn.sigmoid(y @ w_glu + b_glu)
    return y.astype(u.dtype)

def rglru_mixer(xr, gate, conv_w, conv_b, w_a, b_a, w_x, b_x, lam):
    B, L, _ = xr.shape
    f32 = jnp.float32
    xc = causal_dwconv(xr, conv_w, conv_b)
    xh = xc.reshape(B, L, RG_HEADS, RG_HEAD_DIM)
    r = jax.nn.sigmoid(jnp.einsum('blhi,hij->blhj', xh, w_a).reshape(B, L, RG_WIDTH) + b_a)
    i = jax.nn.sigmoid(jnp.einsum('blhi,hij->blhj', xh, w_x).reshape(B, L, RG_WIDTH) + b_x)
    log_a = -RG_C * r.astype(f32) * jax.nn.softplus(-lam.astype(f32))
    a = jnp.exp(log_a)
    xin = jnp.sqrt(-jnp.expm1(2.0 * log_a)) * (i * xc).astype(f32)
    _, h = lax.associative_scan(linear_rec_combine, (a, xin), axis=1)
    return h.astype(xr.dtype) * jax.nn.gelu(gate)

def conv_ffn(h, w_up, conv_w, conv_b, w_down):
    up, gv = jnp.split(h @ w_up, 2, axis=-1)
    up = causal_dwconv(up, conv_w, conv_b)
    return (jax.nn.gelu(up) * gv) @ w_down

def second_inputs(seed: int = 0) -> dict:
    key = jax.random.key(seed)
    ks = jax.random.split(key, 32)
    f32 = jnp.float32
    L = DEPTH
    G, P = S5_GROUPS, S5_STATE

    def nrm(k, shape, scale):
        return scale * jax.random.normal(k, shape, f32)

    def gain(k, shape):
        return 1.0 + 0.02 * jax.random.normal(k, shape, f32)

    a0 = jax.random.uniform(ks[23], (L, RG_WIDTH), f32, 0.9, 0.999)
    return {
        "x": jax.random.normal(ks[0], (BATCH, SEQ, D_MODEL), f32),
        "attn_norm": gain(ks[1], (L, D_MODEL)),
        "w_in": nrm(ks[2], (L, D_MODEL, D_IN), D_MODEL ** -0.5),
        "gla_w_gk_up": nrm(ks[3], (L, GLA_LOW_RANK, GLA_DK_TOTAL), GLA_LOW_RANK ** -0.5),
        "gla_b_gk": nrm(ks[4], (L, GLA_DK_TOTAL), 0.1),
        "gla_norm": gain(ks[5], (L, GLA_DV)),
        "s5_lambda_re": -0.5 + nrm(ks[6], (L, G, P), 0.01),
        "s5_lambda_im": jnp.pi * jnp.arange(P, dtype=f32) + nrm(ks[7], (L, G, P), 0.01),
        "s5_log_dt": jax.random.uniform(ks[8], (L, G), f32, math.log(S5_DT_MIN), math.log(S5_DT_MAX)),
        "s5_b_re": nrm(ks[9], (L, G, P, S5_GROUP), (2 * S5_GROUP) ** -0.5),
        "s5_b_im": nrm(ks[10], (L, G, P, S5_GROUP), (2 * S5_GROUP) ** -0.5),
        "s5_c_re": nrm(ks[11], (L, G, S5_GROUP, P), (2 * P) ** -0.5),
        "s5_c_im": nrm(ks[12], (L, G, S5_GROUP, P), (2 * P) ** -0.5),
        "s5_d": nrm(ks[13], (L, S5_WIDTH), 1.0),
        "s5_w_glu": nrm(ks[14], (L, S5_WIDTH, S5_WIDTH), S5_WIDTH ** -0.5),
        "s5_b_glu": nrm(ks[15], (L, S5_WIDTH), 0.01),
        "s5_norm": gain(ks[16], (L, S5_WIDTH)),
        "rg_conv_w": nrm(ks[17], (L, RG_CONV, RG_WIDTH), RG_CONV ** -0.5),
        "rg_conv_b": nrm(ks[18], (L, RG_WIDTH), 0.01),
        "rg_w_a": nrm(ks[19], (L, RG_HEADS, RG_HEAD_DIM, RG_HEAD_DIM), RG_HEAD_DIM ** -0.5),
        "rg_b_a": nrm(ks[20], (L, RG_WIDTH), 0.01),
        "rg_w_x": nrm(ks[21], (L, RG_HEADS, RG_HEAD_DIM, RG_HEAD_DIM), RG_HEAD_DIM ** -0.5),
        "rg_b_x": nrm(ks[22], (L, RG_WIDTH), 0.01),
        "rg_lambda": jnp.log(a0) - jnp.log1p(-a0),
        "rg_norm": gain(ks[24], (L, RG_WIDTH)),
        "w_out": nrm(ks[25], (L, D_MIX, D_MODEL), D_MIX ** -0.5),
        "mlp_norm": gain(ks[26], (L, D_MODEL)),
        "w_up": nrm(ks[27], (L, D_MODEL, 2 * D_FF), D_MODEL ** -0.5),
        "mlp_conv_w": nrm(ks[28], (L, FFN_CONV, D_FF), FFN_CONV ** -0.5),
        "mlp_conv_b": nrm(ks[29], (L, D_FF), 0.01),
        "w_down": nrm(ks[30], (L, D_FF, D_MODEL), D_FF ** -0.5),
        "final_norm": gain(ks[31], (D_MODEL,)),
    }

def second_block(x, attn_norm, w_in, gla_w_gk_up, gla_b_gk, gla_norm,
              s5_lambda_re, s5_lambda_im, s5_log_dt, s5_b_re, s5_b_im, s5_c_re, s5_c_im,
              s5_d, s5_w_glu, s5_b_glu, s5_norm,
              rg_conv_w, rg_conv_b, rg_w_a, rg_b_a, rg_w_x, rg_b_x, rg_lambda, rg_norm,
              w_out, mlp_norm, w_up, mlp_conv_w, mlp_conv_b, w_down, final_norm):
    splits = np.cumsum(np.array(IN_SIZES))[:-1].tolist()
    for l in range(DEPTH):
        h = rmsnorm(x, attn_norm[l])
        q, k, v, g, gk_low, s5_u, rg_x, rg_gate = jnp.split(h @ w_in[l], splits, axis=-1)
        y_gla = gla_mixer(q, k, v, g, gk_low, gla_w_gk_up[l], gla_b_gk[l], gla_norm[l])
        y_s5 = rmsnorm(s5_mixer(s5_u, s5_lambda_re[l], s5_lambda_im[l], s5_log_dt[l], s5_b_re[l], s5_b_im[l],
                                s5_c_re[l], s5_c_im[l], s5_d[l], s5_w_glu[l], s5_b_glu[l]), s5_norm[l])
        y_rg = rmsnorm(rglru_mixer(rg_x, rg_gate, rg_conv_w[l], rg_conv_b[l], rg_w_a[l], rg_b_a[l],
                                   rg_w_x[l], rg_b_x[l], rg_lambda[l]), rg_norm[l])
        x = x + jnp.concatenate([y_gla, y_s5, y_rg], axis=-1) @ w_out[l]
        h = rmsnorm(x, mlp_norm[l])
        x = x + conv_ffn(h, w_up[l], mlp_conv_w[l], mlp_conv_b[l], w_down[l])
    return rmsnorm(x, final_norm)


_first_inputs = second_inputs


def second_inputs(seed=0):
    import zlib

    import numpy as np

    out = dict(_first_inputs(seed))
    spreads = {}
    factors = {'gla_b_gk': 3.636,
     'gla_norm': 22.388,
     's5_lambda_re': 64.0,
     's5_b_re': 3.53,
     's5_b_im': 3.505,
     's5_c_re': 3.606,
     's5_c_im': 3.637,
     's5_b_glu': 8.0,
     's5_norm': 20.857,
     'rg_conv_b': 3.398,
     'rg_b_a': 26.264,
     'rg_b_x': 21.37,
     'rg_norm': 21.232,
     'mlp_norm': 4.323,
     'mlp_conv_b': 26.219,
     'final_norm': 8.484}
    for name, (base, spread) in spreads.items():
        noise = np.random.default_rng([zlib.crc32(name.encode()), seed]).standard_normal(out[name].shape)
        drawn = base * np.exp(spread * noise) if base else spread * noise
        out[name] = __import__('jax').numpy.asarray(drawn.astype(out[name].dtype))
    for name, factor in factors.items():
        out[name] = (out[name] * factor).astype(out[name].dtype)
    return out


_narrow_inputs = second_inputs


def second_inputs(seed=0):
    out = dict(_narrow_inputs(seed))
    wider = {'gla_norm': 4.37,
     's5_lambda_re': 12.0,
     's5_norm': 4.38,
     'rg_norm': 4.41,
     'mlp_norm': 3.74,
     'final_norm': 3.29}
    for name, times in wider.items():
        mean = out[name].mean()
        out[name] = (mean + times * (out[name] - mean)).astype(out[name].dtype)
    return out


def setup_inputs(seed=0):
    out = dict(first_inputs(seed))
    for name, value in second_inputs(seed + 1).items():
        if name != "x":
            out[name + "_2"] = value
    return out


def reference(
    x, norm_mix_g, w_in, rpb, g_out_dil, g_out_na, w_out, norm_ffn_g, w_group, b_group,
    w_router, b_router, w_gate, w_up, w_down, norm_final_g, attn_norm_2, w_in_2, gla_w_gk_up_2,
    gla_b_gk_2, gla_norm_2, s5_lambda_re_2, s5_lambda_im_2, s5_log_dt_2, s5_b_re_2, s5_b_im_2,
    s5_c_re_2, s5_c_im_2, s5_d_2, s5_w_glu_2, s5_b_glu_2, s5_norm_2, rg_conv_w_2, rg_conv_b_2,
    rg_w_a_2, rg_b_a_2, rg_w_x_2, rg_b_x_2, rg_lambda_2, rg_norm_2, w_out_2, mlp_norm_2, w_up_2,
    mlp_conv_w_2, mlp_conv_b_2, w_down_2, final_norm_2,
):
    x = first_block(
        x, norm_mix_g, w_in, rpb, g_out_dil, g_out_na, w_out, norm_ffn_g, w_group, b_group,
        w_router, b_router, w_gate, w_up, w_down, norm_final_g,
    )
    return second_block(
        x, attn_norm_2, w_in_2, gla_w_gk_up_2, gla_b_gk_2, gla_norm_2, s5_lambda_re_2,
        s5_lambda_im_2, s5_log_dt_2, s5_b_re_2, s5_b_im_2, s5_c_re_2, s5_c_im_2, s5_d_2,
        s5_w_glu_2, s5_b_glu_2, s5_norm_2, rg_conv_w_2, rg_conv_b_2, rg_w_a_2, rg_b_a_2,
        rg_w_x_2, rg_b_x_2, rg_lambda_2, rg_norm_2, w_out_2, mlp_norm_2, w_up_2, mlp_conv_w_2,
        mlp_conv_b_2, w_down_2, final_norm_2,
    )


_drawn_inputs = setup_inputs


def setup_inputs(seed=0):
    import zlib

    import numpy as np

    out = dict(_drawn_inputs(seed))
    spreads = {}
    factors = {'b_group': 5.342,
     'b_router': 3.451,
     's5_lambda_re_2': 200.0,
     's5_lambda_im_2': 34.92,
     's5_log_dt_2': 30.344,
     's5_c_re_2': 21.416,
     's5_b_re_2': 8.0,
     's5_b_im_2': 8.0,
     's5_c_im_2': 8.0}
    for name, (base, spread) in spreads.items():
        noise = np.random.default_rng([zlib.crc32(name.encode()), seed]).standard_normal(out[name].shape)
        drawn = base * np.exp(spread * noise) if base else spread * noise
        out[name] = __import__('jax').numpy.asarray(drawn.astype(out[name].dtype))
    for name, factor in factors.items():
        out[name] = (out[name] * factor).astype(out[name].dtype)
    return out
```

```python
import concourse.bass as bass
from concourse import mybir
from contextlib import ExitStack
import numpy as np

P = 128
S = 1024
D = 1024
NT = D // P
HALF = 512
DH = 64
NH = 16
NEG = -1e30
EPS = 1e-6
SLOTS = 4
RING = 8
STRIP = 1920
NF, NI = 7 * P, 5 * P
N_EXP, N_GRP, EPG, FT = 16, 4, 4, 2
FF = 22
CH = 64
NCH = S // CH

PCOLS = {}
_at = 0
for _name, _n in (("norm_mix", 8), ("g_out", 8), ("norm_ffn", 8), ("norm_final", 8), ("attn_norm", 8),
                  ("gk_bias", 2), ("gla_norm", 1), ("lam_re", 8), ("lam_im", 8), ("log_dt", 8), ("s5_d", 2),
                  ("b_glu", 2), ("s5_norm", 2), ("rg_w", 8), ("rg_cb", 2), ("rg_ba", 2), ("rg_bx", 2),
                  ("rg_lam", 2), ("rg_norm", 2), ("mlp_norm", 8), ("ff_w", 3 * FF), ("ff_cb", FF), ("final_norm", 8)):
    PCOLS[_name] = _at
    _at += _n
MCOLS = {}
for _name, _n in (("ones", P), ("ident", P), ("causal", P), ("route", NT * 20), ("low", NT * 16), ("rg", 4 * P),
                  ("glu", 2 * 256), ("gkup", 256), ("bias20", 20), ("tie", 4)):
    MCOLS[_name] = _at
    _at += _n
NCOL = _at


def key_tiles(h, i):
    if h < 8:
        return 0, 8
    return (max(i - 2, 0), min(i + 3, 8)) if 2 <= i <= 5 else ((0, 4) if i < 2 else (4, 8))


def build(nc, xT, params, w_in, w_out, w_moe, w_in2, w_out2, w_up, w_down, dil_strip, na_strip, s5_mats, out):
    f32, i32 = mybir.dt.float32, mybir.dt.int32
    ALU, ACT, AX = mybir.AluOpType, mybir.ActivationFunctionType, mybir.AxisListType
    comb_dram = nc.dram_tensor("combine_rows", (N_EXP, S), f32, kind="Internal").ap()

    ctx = ExitStack()
    with ctx:
        def sb(name, shape, dt=f32):
            return ctx.enter_context(nc.sbuf_tensor(name, shape, dt))

        def sem(name):
            return ctx.enter_context(nc.semaphore(name))

        hT = sb("hT", [P, NT, S])
        bT = sb("bT", [P, NT, S])
        ring = sb("ring", [P, RING, NT * P])
        W = sb("work", [P, 25, S])
        cst = sb("cst", [P, NCOL])
        small = sb("small", [P, 40, 8])
        s5p = sb("s5p", [P, 26, 8])
        sp4 = sb("sp4", [P, 2])
        epsc = sb("epsc", [P, 1])
        negm = sb("negm", [P, 4])
        den = sb("den", [P, 4])
        rden = sb("rden", [P, 4])
        decay = sb("decay", [P, 2, NCH])
        PS = [ctx.enter_context(nc.psum_tensor(f"ps{i}", [P, S], f32)) for i in range(SLOTS)]

        def par(name, c=0, n=1):
            return cst[:, PCOLS[name] + c:PCOLS[name] + c + n]

        def mat(name, c=0, n=P):
            return cst[:, MCOLS[name] + c:MCOLS[name] + c + n]

        ones, ident = mat("ones"), mat("ident")
        mix_ones = ones

        w_loaded = [sem(f"w_loaded{i}") for i in range(RING)]
        mm_done = sem("mm_done")
        x_loaded = [sem(f"x_loaded{i}") for i in range(4)]
        cst_loaded = sem("cst_loaded")
        strip_loaded = [sem(f"strip_loaded{i}") for i in range(2)]
        x_again = sem("x_again")
        s5_loaded = sem("s5_loaded")
        comb_stored = sem("comb_stored")
        comb_loaded = [sem(f"comb_loaded{i}") for i in range(2)]
        out_stored = sem("out_stored")
        sq_ready, sq_used, std_ready, normed = sem("sq_ready"), sem("sq_used"), sem("std_ready"), sem("normed")
        eps_set = sem("eps_set")
        qkv_ready = sem("qkv_ready")
        scores_ready, exp_done, probs_ready, pT_ready, heads_done = (
            sem("scores_ready"), sem("exp_done"), sem("probs_ready"), sem("pT_ready"), sem("heads_done"))
        h_ready = sem("h_ready")
        gdiff_ready, gexp_done, tdiff_ready, texp_done, comb_ready, combT_ready = (
            sem("gdiff_ready"), sem("gexp_done"), sem("tdiff_ready"), sem("texp_done"), sem("comb_ready"), sem("combT_ready"))
        silu_ready, act_ready = sem("silu_ready"), sem("act_ready")
        in2_ready = sem("in2_ready")
        conv_ready, gates_ready, tanh_ready, root_ready, ggate_ready, rg_ready = (
            sem("conv_ready"), sem("gates_ready"), sem("tanh_ready"), sem("root_ready"), sem("ggate_ready"), sem("rg_ready"))
        s5b_ready, s5bT_ready, s5x_ready, s5y_ready, s5g_ready, s5s_ready, s5_ready = (
            sem("s5b_ready"), sem("s5bT_ready"), sem("s5x_ready"), sem("s5y_ready"), sem("s5g_ready"), sem("s5s_ready"), sem("s5_ready"))
        s5in_ready, gk_biased, gexps_used, decay_ready, gk_abs, gk_exp, gk_ln, bc_ready, gexps, gprods, klT_ready, state_ready, intra_ready, o_ready, gsilu, gla_ready = (
            sem(n) for n in ("s5in_ready", "gk_biased", "gexps_used", "decay_ready", "gk_abs", "gk_exp", "gk_ln", "bc_ready", "gexps", "gprods", "klT_ready", "state_ready",
                             "intra_ready", "o_ready", "gsilu", "gla_ready"))
        conv0_ready, conv1_ready, gelu_ready, ffact_ready = (
            sem("conv0_ready"), sem("conv1_ready"), sem("gelu_ready"), sem("ffact_ready"))
        dve_link, act_link = sem("dve_link"), sem("act_link")
        final_ready = sem("final_ready")

        units = [w_in[n] for n in range(24)] + [w_out[n] for n in range(8)]
        units += [w_moe[n] for n in range(96)] + [w_in2[n] for n in range(18)] + [w_out2[n] for n in range(8)]
        units += [w_up[n] for n in range(2 * FF)] + [w_down[n] for n in range(24)]
        U_IN, U_OUT, U_MOE, U_IN2 = 0, 24, 32, 128
        U_OUT2 = U_IN2 + 18
        U_UP = U_OUT2 + 8
        U_DOWN = U_UP + 2 * FF

        at = [0]

        def take(k):
            at[0] += k
            return at[0] - k

        norms = []
        sq_base = [0]

        emptied = {}

        def done(n):
            return n + 1 - sum(c["use"] < n for c in norms)

        def add_norm(src, gain, dst, scratch, tiles, use):
            norms.append(dict(src=src, gain=gain, dst=dst, scratch=scratch, tiles=tiles, use=use, sq0=sq_base[0],
                              index=len(norms)))
            sq_base[0] += tiles
            emptied[use] = (std_ready, len(norms))
            return norms[-1]

        Hp = [hT[:, t, :] for t in range(NT)]
        Bp = [bT[:, t, :] for t in range(NT)]
        Wp = [W[:, t, :] for t in range(25)]

        n_mix = add_norm(Hp, "norm_mix", Bp, Wp[22:25], 8, take(1))
        U_QKV = take(24)
        LAG_T, LAG_O = 2, 3
        NU = NH * NT
        use_s, use_t, use_o = {}, {}, {}
        for t in range(NU + LAG_O):
            if t < NU:
                use_s[t] = take(1)
            if 0 <= t - LAG_T < NU:
                use_t[t - LAG_T] = take(1)
            if 0 <= t - LAG_O < NU:
                use_o[t - LAG_O] = take(1)
        n_dil = add_norm(Bp[0:4], "g_out", Bp[0:4], Wp[16:19], 4, take(1))
        n_na = add_norm(Bp[4:8], "g_out", Bp[4:8], Wp[19:22], 4, take(1))
        P_OUT = take(8)
        n_ffn = add_norm(Hp, "norm_ffn", Bp, Wp[22:25], 8, take(1))
        P_ROUTE = take(2)
        P_MOE = take(96)
        n_fin1 = add_norm(Hp, "norm_final", Hp, Wp[22:25], 8, take(1))
        n_att2 = add_norm(Hp, "attn_norm", Bp, Wp[22:25], 8, take(1))
        P_IN2 = take(19)
        P_RG = take(4)
        n_rg = add_norm(Wp[2:4], "rg_norm", Bp[6:8], [Wp[4], Wp[5], Wp[19]], 2, take(1))
        P_S5T = take(2)
        P_S5 = take(24)
        P_GLU = take(2)
        n_s5 = add_norm(Wp[0:2], "s5_norm", Bp[4:6], [Wp[19], Wp[20], Wp[21]], 2, take(1))
        P_GK = take(2)
        P_KLT = take(2)
        P_KV = take(8)
        P_SC = take(4)
        P_O = []
        n_gla = []
        for h in range(4):
            P_O.append(take(1))
            n_gla.append(add_norm([Wp[4 + h] if h < 2 else Wp[17 + h]], "gla_norm", [Bp[h]], [Wp[8 + 13 * (h % 2)], None, Wp[9]], 1, take(1)))
        P_OUT2 = take(8)
        n_mlp = add_norm(Hp, "mlp_norm", Bp, Wp[22:25], 8, take(1))
        P_UP = take(2 * FF)
        P_DOWN = take(8)
        n_fin2 = add_norm(Hp, "final_norm", Hp, Wp[22:25], 8, take(1))

        for m in range(24):
            emptied[U_QKV + m] = (qkv_ready, m + 1)
        for u in range(NU):
            emptied[use_s[u]], emptied[use_t[u]], emptied[use_o[u]] = (scores_ready, u + 1), (pT_ready, u + 1), (heads_done, u + 1)
        emptied[P_ROUTE], emptied[P_ROUTE + 1] = (gdiff_ready, 1), (combT_ready, 1)
        for m in range(8):
            emptied[P_OUT + m] = (h_ready, m + 1)
            for g in range(N_GRP):
                j = 8 * g + m
                emptied[P_MOE + 24 * g + 2 * m] = (silu_ready, j + 1)
                emptied[P_MOE + 24 * g + 2 * m + 1] = (act_ready, j + 1)
                emptied[P_MOE + 24 * g + 16 + m] = (h_ready, 8 + j + 1)
            emptied[P_OUT2 + m] = (h_ready, 8 + 8 * N_GRP + m + 1)
            emptied[P_DOWN + m] = (h_ready, 16 + 8 * N_GRP + m + 1)
            emptied[P_KV + m] = (state_ready, m + 1)
            emptied[P_S5 + 3 * m] = emptied[P_S5 + 3 * m + 1] = (s5in_ready, m + 1)
            emptied[P_S5 + 3 * m + 2] = (s5y_ready, m + 1)
        for m in range(19):
            emptied[P_IN2 + m] = (in2_ready, m + 1)
        for m in range(2):
            emptied[P_S5T + m] = (s5bT_ready, m + 1)
            emptied[P_GLU + m] = (s5s_ready, m + 1)
            emptied[P_GK + m] = (gk_biased, m + 1)
            emptied[P_KLT + m] = (klT_ready, m + 1)
        for m in range(4):
            emptied[P_RG + m] = (gates_ready, m + 1)
            emptied[P_SC + m] = (intra_ready, m + 1)
            emptied[P_O[m]] = (o_ready, m + 1)
        for j in range(FF):
            emptied[P_UP + 2 * j] = (conv1_ready, j + 1)
            emptied[P_UP + 2 * j + 1] = (ffact_ready, j + 1)
        unit_use = [U_QKV + m for m in range(16)] + [U_QKV + 19] * 4 + [U_QKV + 23] * 4 + [P_OUT + m for m in range(8)]
        unit_use += [P_MOE + n for n in range(96)] + [P_IN2 + m for m in range(14)] + [P_IN2 + 18] * 4
        unit_use += [P_OUT2 + m for m in range(8)] + [P_UP + j for j in range(2 * FF)] + [P_DOWN + j // 3 for j in range(24)]

        Mp = [Wp[0], Wp[1], Wp[18], Wp[22]]

        PG_U, PG_RX, PG_RG, PG_Q, PG_K, PG_V, PG_G, PG_LOW = 0, 2, 4, 6, 8, 10, 14, 18

        def pair(p0):
            return W[:, p0:p0 + 2, :]

        block = ctx.enter_context(nc.Block())

        RV = {"L": (0, 160), "gd": (160, 32), "oh": (192, 32), "gm": (224, 8), "gw": (232, 8), "v4": (240, 32),
              "o1": (272, 32), "o2": (304, 32), "m1": (336, 8), "m2": (344, 8), "d1": (352, 8), "w1": (360, 8),
              "w2": (368, 8), "t4": (376, 32), "v4b": (408, 32), "c4": (440, 32), "tm": (472, 8), "gs": (480, 8),
              "t5": (488, 32), "comb": (640, 128)}

        def R(name):
            a, n = RV[name]
            return W[:, 20, a:a + n]

        @block.sync
        def _(sp):
            for i in range(4):
                sp.dma_start(hT[:, 2 * i:2 * i + 2, :], xT[:, 2 * i:2 * i + 2, :]).then_inc(x_loaded[i], 16)
                if i == 0:
                    sp.dma_start(cst[:], params).then_inc(cst_loaded, 16)
            for u, src in enumerate(units):
                if u >= RING:
                    sp.wait_ge(mm_done, done(unit_use[u - RING]))
                sp.dma_start(ring[:, u % RING, :], src).then_inc(w_loaded[u % RING], 16)
            for t in range(NT):
                sp.wait_ge(final_ready, t + 1)
                sp.dma_start(out[:, t, :], hT[:, t, :]).then_inc(out_stored, 16)
            sp.wait_ge(out_stored, 16 * NT)

        STRIPS = [hT[:, 0:2, :].rearrange("p a b -> p (a b)")[:, 0:STRIP],
                  hT[:, 2:4, :].rearrange("p a b -> p (a b)")[:, 0:STRIP]]
        SB = [hT[:, 4, :], hT[:, 5, :], W[:, 24, :]]
        PT = [hT[:, 6, :], hT[:, 7, :]]
        combB = [Wp[18], Wp[19]]

        @block.gpsimd
        def _(pool):
            pool.memset(epsc[:], EPS).then_inc(eps_set, 1)
            pool.wait_ge(normed, n_mix["index"] + 1)
            for h in range(NH):
                if h >= 2:
                    pool.wait_ge(scores_ready, NT * (h - 1))
                if h < 8:
                    pool.dma_start(STRIPS[h % 2], dil_strip[h]).then_inc(strip_loaded[h % 2], 16)
                else:
                    pool.dma_start(STRIPS[h % 2][:, 0:NF + NI], na_strip[h - 8]).then_inc(strip_loaded[h % 2], 16)
            pool.wait_ge(heads_done, NU)
            pool.dma_start(hT[:], xT).then_inc(x_again, 16)
            pool.wait_ge(combT_ready, 1)
            pool.dma_start(comb_dram, W[0:N_EXP, 21, :]).then_inc(comb_stored, 16)
            pool.wait_ge(comb_stored, 16)
            for e in range(N_EXP):
                if e >= 2:
                    pool.wait_ge(act_ready, 2 * (e - 1))
                pool.dma_start(combB[e % 2], comb_dram[e:e + 1, :].to_broadcast([P, S])).then_inc(comb_loaded[e % 2], 16)
            pool.wait_ge(rg_ready, 1)
            pool.wait_ge(normed, n_rg["index"] + 1)
            pool.dma_start(bT[:, 0:4, :], s5_mats[:, 0:4, :]).then_inc(s5_loaded, 16)

        @block.tensor
        def _(pe):
            def slot(n):
                if n >= SLOTS:
                    pe.wait_ge(*emptied[n - SLOTS])
                return PS[n % SLOTS]

            def unit(u):
                pe.wait_ge(w_loaded[u % RING], 16 * (u // RING + 1))
                return ring[:, u % RING, :]

            def column_tile(u, n, rhs, kt=NT):
                ps, w = slot(n), unit(u)
                for half in range(2):
                    for k in range(kt):
                        mm = pe.matmul(ps[:, half * HALF:(half + 1) * HALF], w[:, k * P:(k + 1) * P],
                                       rhs[k][:, half * HALF:(half + 1) * HALF], start=(k == 0), stop=(k == kt - 1))
                        if half == 1 and k == kt - 1:
                            mm.then_inc(mm_done, 1)

            def token_major(u0, n0, lhs):
                ws = [unit(u0 + j) for j in range(4)]
                del ws
                s0 = u0 % RING
                for tt in range(NT):
                    if tt % 2 == 0:
                        ps = slot(n0 + tt // 2)
                    for k in range(NT):
                        mm = pe.matmul(ps[:, (tt % 2) * HALF:(tt % 2 + 1) * HALF], lhs[k][:, tt * P:(tt + 1) * P],
                                       ring[:, s0:s0 + 4, k * P:(k + 1) * P], start=(k == 0), stop=(k == NT - 1))
                    if tt % 2 == 1:
                        mm.then_inc(mm_done, 1)

            def norm(c):
                ps = slot(c["use"])
                for t in range(c["tiles"]):
                    pe.wait_ge(sq_ready, c["sq0"] + t + 1)
                    for half in range(2):
                        mm = pe.matmul(ps[:, half * HALF:(half + 1) * HALF], ones,
                                       c["scratch"][t % 2][:, half * HALF:(half + 1) * HALF],
                                       start=(t == 0), stop=(t == c["tiles"] - 1))
                    mm.then_inc(sq_used, 1)

            pe.wait_ge(cst_loaded, 16)
            norm(n_mix)
            pe.wait_ge(normed, n_mix["index"] + 1)
            for m in range(16):
                column_tile(U_IN + m, U_QKV + m, Bp)
            for g in range(2):
                token_major(U_IN + 16 + 4 * g, U_QKV + 16 + 4 * g, Bp)

            def scores(u):
                h, i = u // NT, u % NT
                k0, k1 = key_tiles(h, i)
                r0 = (h % 2) * DH
                ps = slot(use_s[u])
                q, k = Wp[h // 2], Wp[8 + h // 2]
                for c0 in range(k0 * P, k1 * P, HALF):
                    c1 = min(c0 + HALF, k1 * P)
                    mm = pe.matmul(ps[:, c0 - k0 * P:c1 - k0 * P], q[r0:r0 + DH, i * P:(i + 1) * P],
                                   k[r0:r0 + DH, c0:c1], start=True, stop=True)
                mm.then_inc(mm_done, 1)

            def turn(u):
                k0, k1 = key_tiles(u // NT, u % NT)
                pe.wait_ge(probs_ready, u + 1)
                ps = slot(use_t[u])
                for j in range(k1 - k0):
                    mm = pe.transpose(ps[:, j * P:(j + 1) * P], SB[u % 3][:, j * P:(j + 1) * P], ident)
                mm.then_inc(mm_done, 1)

            def mix(u):
                h = u // NT
                k0, k1 = key_tiles(h, u % NT)
                pe.wait_ge(pT_ready, u + 1)
                ps = slot(use_o[u])
                for j in range(k1 - k0):
                    mm = pe.matmul(ps[0:DH, 0:P], Wp[16 + k0 + j][:, h * DH:(h + 1) * DH],
                                   PT[u % 2][:, j * P:(j + 1) * P], start=(j == 0), stop=(j == k1 - k0 - 1))
                mm.then_inc(mm_done, 1)

            pe.wait_ge(qkv_ready, 24)
            for t in range(NU + LAG_O):
                if t < NU:
                    scores(t)
                if 0 <= t - LAG_T < NU:
                    turn(t - LAG_T)
                if 0 <= t - LAG_O < NU:
                    mix(t - LAG_O)
            norm(n_dil)
            norm(n_na)
            pe.wait_ge(normed, n_na["index"] + 1)
            for m in range(8):
                column_tile(U_OUT + m, P_OUT + m, Bp)
            norm(n_ffn)
            pe.wait_ge(normed, n_ffn["index"] + 1)
            ps = slot(P_ROUTE)
            for tt in range(NT):
                for k in range(NT):
                    mm = pe.matmul(ps[:, tt * 20:(tt + 1) * 20], Bp[k][:, tt * P:(tt + 1) * P],
                                   mat("route", k * 20, 20), start=(k == 0), stop=(k == NT - 1))
            mm.then_inc(mm_done, 1)
            pe.wait_ge(comb_ready, 1)
            ps = slot(P_ROUTE + 1)
            for tt in range(NT):
                mm = pe.transpose(ps[0:N_EXP, tt * P:(tt + 1) * P], W[:, 20, 640 + tt * 16:640 + tt * 16 + 16], ident)
            mm.then_inc(mm_done, 1)
            for g in range(N_GRP):
                for j in range(16):
                    column_tile(U_MOE + 24 * g + j, P_MOE + 24 * g + j, Bp)
                pe.wait_ge(act_ready, 8 * (g + 1))
                for m in range(8):
                    column_tile(U_MOE + 24 * g + 16 + m, P_MOE + 24 * g + 16 + m, Wp[0:8])
            norm(n_fin1)
            norm(n_att2)
            pe.wait_ge(normed, n_att2["index"] + 1)
            for m in range(14):
                column_tile(U_IN2 + m, P_IN2 + m, Bp)
            ps = slot(P_IN2 + 14)
            for half in range(2):
                for k in range(NT):
                    mm = pe.matmul(ps[0:16, half * HALF:(half + 1) * HALF], mat("low", k * 16, 16),
                                   Bp[k][:, half * HALF:(half + 1) * HALF], start=(k == 0), stop=(k == NT - 1))
            mm.then_inc(mm_done, 1)
            for j in range(4):
                unit(U_IN2 + 14 + j)
            for tt in range(NT):
                if tt % 2 == 0:
                    ps = slot(P_IN2 + 15 + tt // 2)
                for j in range(4):
                    s0 = (U_IN2 + 14 + j) % RING
                    c0 = (tt % 2) * HALF + j * P
                    for k in range(NT):
                        mm = pe.matmul(ps[:, c0:c0 + P], Bp[k][:, tt * P:(tt + 1) * P], ring[:, s0, k * P:(k + 1) * P],
                                       start=(k == 0), stop=(k == NT - 1))
                if tt % 2 == 1:
                    mm.then_inc(mm_done, 1)

            pe.wait_ge(conv_ready, 2)
            for j in range(4):
                ps = slot(P_RG + j)
                for half in range(2):
                    mm = pe.matmul(ps[:, half * HALF:(half + 1) * HALF], mat("rg", j * P),
                                   Wp[19 + j % 2][:, half * HALF:(half + 1) * HALF], start=True, stop=True)
                mm.then_inc(mm_done, 1)
            norm(n_rg)

            pe.wait_ge(s5b_ready, 1)
            for c in range(2):
                ps = slot(P_S5T + c)
                for j in range(8):
                    mm = pe.transpose(ps[:, j * P:(j + 1) * P], Bp[c][:, j * P:(j + 1) * P], ident)
                mm.then_inc(mm_done, 1)
            pe.wait_ge(s5bT_ready, 2)
            for j in range(8):
                for c in range(2):
                    ps = slot(P_S5 + 3 * j + c)
                    for half in range(2):
                        mm = pe.matmul(ps[:, half * HALF:(half + 1) * HALF], Bp[4 + c][:, j * P:(j + 1) * P],
                                       Wp[PG_U + j // 4][:, half * HALF:(half + 1) * HALF], start=True, stop=True)
                    mm.then_inc(mm_done, 1)
                pe.wait_ge(s5x_ready, j + 1)
                ps = slot(P_S5 + 3 * j + 2)
                for half in range(2):
                    for c in range(2):
                        mm = pe.matmul(ps[:, half * HALF:(half + 1) * HALF], Bp[2 + c][:, j * P:(j + 1) * P],
                                       Wp[4 + c][:, half * HALF:(half + 1) * HALF], start=(c == 0), stop=(c == 1))
                mm.then_inc(mm_done, 1)
            pe.wait_ge(s5g_ready, 2)
            for m in range(2):
                ps = slot(P_GLU + m)
                for half in range(2):
                    for k in range(2):
                        mm = pe.matmul(ps[:, half * HALF:(half + 1) * HALF], mat("glu", k * 256 + m * P),
                                       Wp[k][:, half * HALF:(half + 1) * HALF], start=(k == 0), stop=(k == 1))
                mm.then_inc(mm_done, 1)
            norm(n_s5)

            for m in range(2):
                ps = slot(P_GK + m)
                for half in range(2):
                    mm = pe.matmul(ps[:, half * HALF:(half + 1) * HALF], cst[0:16, MCOLS["gkup"] + m * P:MCOLS["gkup"] + (m + 1) * P],
                                   Wp[PG_LOW][0:16, half * HALF:(half + 1) * HALF], start=True, stop=True)
                mm.then_inc(mm_done, 1)
            pe.wait_ge(gprods, 1)
            for m in range(2):
                ps = slot(P_KLT + m)
                for tt in range(NT):
                    mm = pe.transpose(ps[:, tt * P:(tt + 1) * P], Wp[PG_K + m][:, tt * P:(tt + 1) * P], ident)
                mm.then_inc(mm_done, 1)
            vv = W[:, PG_V:PG_V + 4, :].rearrange("p a (b c) -> p (a b) c", c=HALF)
            for m in range(2):
                pe.wait_ge(klT_ready, m + 1)
                for q4 in range(4):
                    ps = slot(P_KV + 4 * m + q4)
                    for j in range(4):
                        n = 4 * q4 + j
                        r0, tt = (n % 2) * CH, n // 2
                        c0 = (j % 2) * HALF + (j // 2) * 256
                        mm = pe.matmul(ps[:, c0:c0 + 256], Wp[21 + m][r0:r0 + CH, tt * P:(tt + 1) * P],
                                       vv[r0:r0 + CH, tt, m * 256:(m + 1) * 256], start=True, stop=True)
                    mm.then_inc(mm_done, 1)
            for h in range(4):
                m, r0 = h // 2, (h % 2) * DH
                ps = slot(P_SC + h)
                for tt in range(NT):
                    mm = pe.matmul(ps[:, tt * P:(tt + 1) * P], Wp[19 + m][r0:r0 + DH, tt * P:(tt + 1) * P],
                                   Wp[4 + m][r0:r0 + DH, tt * P:(tt + 1) * P], start=True, stop=True)
                mm.then_inc(mm_done, 1)
            states = [pair(23).rearrange("p a (b c) -> p (a b) c", c=P), pair(2).rearrange("p a (b c) -> p (a b) c", c=P)]
            for h in range(4):
                m, r0 = h // 2, (h % 2) * DH
                pe.wait_ge(intra_ready, h + 1)
                pe.wait_ge(state_ready, 8)
                ps = slot(P_O[h])
                for tt in range(NT):
                    o = ps[:, tt * P:(tt + 1) * P]
                    mm = pe.matmul(o, vv[:, tt, h * P:(h + 1) * P], Mp[h][:, tt * P:(tt + 1) * P], start=True, stop=False)
                    for c in range(2):
                        n = 2 * tt + c
                        if n == 0:
                            continue
                        mm = pe.matmul(ps[:, n * CH:(n + 1) * CH], states[m][r0:r0 + DH, n, :],
                                       Wp[PG_Q + m][r0:r0 + DH, n * CH:(n + 1) * CH], start=False, stop=(c == 1))
                mm.then_inc(mm_done, 1)
                norm(n_gla[h])
            pe.wait_ge(gla_ready, 4)
            for m in range(8):
                column_tile(U_OUT2 + m, P_OUT2 + m, Bp)
            norm(n_mlp)
            pe.wait_ge(normed, n_mlp["index"] + 1)
            for j in range(2 * FF):
                column_tile(U_UP + j, P_UP + j, Bp)
            pe.wait_ge(ffact_ready, FF)
            for m in range(8):
                ps = slot(P_DOWN + m)
                for half in range(2):
                    for c in range(3):
                        if half == 0:
                            unit(U_DOWN + 3 * m + c)
                        w = ring[:, (U_DOWN + 3 * m + c) % RING, :]
                        for k in range(8 if c < 2 else 6):
                            kk = 8 * c + k
                            mm = pe.matmul(ps[:, half * HALF:(half + 1) * HALF], w[:, k * P:(k + 1) * P],
                                           Wp[kk][:, half * HALF:(half + 1) * HALF], start=(kk == 0), stop=(kk == FF - 1))
                mm.then_inc(mm_done, 1)
            norm(n_fin2)


        @block.scalar
        def _(act):
            links = [0]

            def link(ins):
                links[0] += 1
                ins.then_inc(act_link, 1)
                act.wait_ge(act_link, links[0])

            def norm(c, gate=None):
                for t in range(c["tiles"]):
                    if gate is not None:
                        gate(t)
                    if c["sq0"] + t >= 2:
                        act.wait_ge(sq_used, c["sq0"] + t - 1)
                    act.activation(c["scratch"][t % 2], c["src"][t], ACT.Square).then_inc(sq_ready, 1)
                act.wait_ge(sq_used, c["sq0"] + c["tiles"])
                if c["index"]:
                    act.wait_ge(normed, c["index"])
                act.activation(c["scratch"][2], PS[c["use"] % SLOTS][:, :], ACT.Sqrt, bias=epsc[:],
                               scale=1.0 / (P * c["tiles"])).then_inc(std_ready, 1)

            act.wait_ge(eps_set, 1)

            def x_gate(t):
                if t % 2 == 0:
                    act.wait_ge(x_loaded[t // 2], 16)
            norm(n_mix, x_gate)
            act.wait_ge(normed, 1)
            for m in range(24):
                n = U_QKV + m
                act.wait_ge(mm_done, done(n))
                ps = PS[n % SLOTS]
                if m < 16:
                    dst, src = Wp[m], ps[:, :]
                else:
                    g, t2 = (m - 16) // 4, (m - 16) % 4
                    dst = W[:, 16 + 2 * t2:18 + 2 * t2, g * HALF:(g + 1) * HALF]
                    src = ps[:, :].rearrange("p (a b) -> p a b", a=2)
                act.activation(dst, src, ACT.Copy, scale=DH ** -0.5 if m < 8 else 1.0).then_inc(qkv_ready, 1)

            def expo(u):
                k0, k1 = key_tiles(u // NT, u % NT)
                act.wait_ge(scores_ready, u + 1)
                s = SB[u % 3][:, 0:(k1 - k0) * P]
                act.activation(s, s, ACT.Exp, bias=negm[:, u % 4:u % 4 + 1], scale=-1.0,
                               accum_out=den[:, u % 4:u % 4 + 1]).then_inc(exp_done, 1)

            def copy_pT(u):
                k0, k1 = key_tiles(u // NT, u % NT)
                n = use_t[u]
                act.wait_ge(mm_done, done(n))
                if u >= 2:
                    act.wait_ge(mm_done, done(use_o[u - 2]))
                act.activation(PT[u % 2][:, 0:(k1 - k0) * P], PS[n % SLOTS][:, 0:(k1 - k0) * P], ACT.Copy).then_inc(pT_ready, 1)

            for t in range(NU + LAG_T):
                if t < NU:
                    expo(t)
                if t >= LAG_T:
                    copy_pT(t - LAG_T)

            def heads_gate(t):
                act.wait_ge(heads_done, NU)
            norm(n_dil, heads_gate)
            norm(n_na, heads_gate)

            def h_gate(t):
                act.wait_ge(h_ready, t + 1)
            norm(n_ffn, h_gate)
            act.wait_ge(gdiff_ready, 1)
            act.activation(R("gd"), R("gd"), ACT.Exp).then_inc(gexp_done, 1)
            act.wait_ge(tdiff_ready, 1)
            act.activation(R("d1"), R("d1"), ACT.Exp).then_inc(texp_done, 1)
            act.wait_ge(mm_done, done(P_ROUTE + 1))
            act.activation(W[0:N_EXP, 21, :], PS[(P_ROUTE + 1) % SLOTS][0:N_EXP, :], ACT.Copy).then_inc(combT_ready, 1)
            for e in range(N_EXP):
                g, el = e // EPG, e % EPG
                for f in range(FT):
                    j = 2 * e + f
                    n = P_MOE + 24 * g + 4 * el + 2 * f
                    act.wait_ge(mm_done, done(n))
                    if j >= 2:
                        act.wait_ge(act_ready, j - 1)
                    act.activation(Wp[16 + j % 2], PS[n % SLOTS][:, :], ACT.Silu).then_inc(silu_ready, 1)

            def moe_gate(t):
                act.wait_ge(h_ready, 8 + 8 * N_GRP)
            norm(n_fin1, moe_gate)

            def fin1_gate(t):
                act.wait_ge(normed, n_fin1["index"] + 1)
            norm(n_att2, fin1_gate)
            act.wait_ge(normed, n_att2["index"] + 1)
            dsts = [Wp[PG_RX], Wp[PG_RX + 1], Wp[PG_RG], Wp[PG_RG + 1], Wp[PG_U], Wp[PG_U + 1], Wp[PG_Q], Wp[PG_Q + 1],
                    Wp[PG_K], Wp[PG_K + 1]] + [Wp[PG_G + j] for j in range(4)]
            for m in range(19):
                n = P_IN2 + m
                act.wait_ge(mm_done, done(n))
                ps = PS[n % SLOTS]
                if m < 14:
                    dst, src = dsts[m], ps[:, :]
                elif m == 14:
                    dst, src = Wp[PG_LOW][0:16, :], ps[0:16, :]
                else:
                    dst, src = Wp[PG_V + m - 15], ps[:, :]
                act.activation(dst, src, ACT.Copy, scale=DH ** -0.5 if m in (6, 7) else 1.0).then_inc(in2_ready, 1)
            for j in range(4):
                n = P_RG + j
                act.wait_ge(mm_done, done(n))
                act.activation(Wp[21 + j], PS[n % SLOTS][:, :], ACT.Sigmoid,
                               bias=par("rg_ba" if j < 2 else "rg_bx", j % 2)).then_inc(gates_ready, 1)
            act.wait_ge(gates_ready, 4)
            for c in range(2):
                act.activation(Wp[21 + c], Wp[21 + c], ACT.Tanh, scale=sp4[:, c:c + 1]).then_inc(tanh_ready, 1)
            act.wait_ge(tanh_ready, 2)
            for c in range(2):
                act.activation(Bp[c], Wp[21 + c], ACT.Sqrt, scale=4.0).then_inc(root_ready, 1)
            for c in range(2):
                act.activation(Wp[PG_RG + c], Wp[PG_RG + c], ACT.Gelu_apprx_tanh).then_inc(ggate_ready, 1)

            def rg_gate(t):
                act.wait_ge(rg_ready, 1)
            norm(n_rg, rg_gate)
            for c in range(2):
                n = P_S5T + c
                act.wait_ge(mm_done, done(n))
                act.activation(Bp[4 + c], PS[n % SLOTS][:, :], ACT.Copy).then_inc(s5bT_ready, 1)
            act.wait_ge(s5y_ready, 8)
            for c in range(2):
                act.activation(Wp[c], Wp[24 - c], ACT.Gelu_apprx_tanh).then_inc(s5g_ready, 1)
            for c in range(2):
                n = P_GLU + c
                act.wait_ge(mm_done, done(n))
                act.activation(Wp[22 - c], PS[n % SLOTS][:, :], ACT.Sigmoid, bias=par("b_glu", c)).then_inc(s5s_ready, 1)

            def s5_gate(t):
                act.wait_ge(s5_ready, 2)
            norm(n_s5, s5_gate)
            act.wait_ge(gk_abs, 2)
            link(act.activation(pair(2), pair(2), ACT.Exp, scale=-1.0))
            act.activation(pair(2), pair(2), ACT.Ln, bias=1.0).then_inc(gk_ln, 1)
            act.wait_ge(bc_ready, 1)
            for k in range(4):
                if k == 3:
                    act.wait_ge(gprods, 1)
                elif k:
                    act.wait_ge(gexps_used, k)
                act.activation(pair(2), pair(2) if k < 3 else pair(0), ACT.Exp).then_inc(gexps, 1)
            for m in range(2):
                last = act.activation(decay[:, m, :], Wp[m].rearrange("p (n c) -> p n c", c=CH)[:, :, CH - 1], ACT.Exp)
            last.then_inc(decay_ready, 1)
            for m in range(2):
                n = P_KLT + m
                act.wait_ge(mm_done, done(n))
                act.activation(Wp[21 + m], PS[n % SLOTS][:, :], ACT.Copy).then_inc(klT_ready, 1)
            for h in range(4):
                act.activation(Wp[PG_G + h], Wp[PG_G + h], ACT.Silu).then_inc(gsilu, 1)
            for h in range(4):
                n = P_O[h]
                act.wait_ge(mm_done, done(n))
                if h >= 2:
                    act.wait_ge(mm_done, done(P_SC + 3))
                act.activation(n_gla[h]["src"][0], PS[n % SLOTS][:, :], ACT.Copy).then_inc(o_ready, 1)
                act.wait_ge(o_ready, h + 1)
                norm(n_gla[h])

            def out2_gate(t):
                act.wait_ge(h_ready, 8 + 8 * N_GRP + t + 1)
            norm(n_mlp, out2_gate)
            for j in range(FF):
                n = P_UP + 2 * j
                act.wait_ge(mm_done, done(n))
                if j >= 3:
                    act.wait_ge(ffact_ready, j - 2)
                act.activation(Wp[22 + j % 3], PS[n % SLOTS][:, :], ACT.Identity, bias=par("ff_cb", j),
                               scale=par("ff_w", 2 * FF + j)).then_inc(conv0_ready, 1)
                act.wait_ge(conv1_ready, j + 1)
                act.activation(Wp[22 + j % 3], Wp[22 + j % 3], ACT.Gelu_apprx_tanh).then_inc(gelu_ready, 1)

            def down_gate(t):
                act.wait_ge(h_ready, 16 + 8 * N_GRP + t + 1)
            norm(n_fin2, down_gate)

        @block.vector
        def _(dve):
            links = [0]

            def link(ins):
                links[0] += 1
                ins.then_inc(dve_link, 1)
                dve.wait_ge(dve_link, links[0])

            def norm(c, last=None):
                r = c["scratch"][2]
                dve.wait_ge(std_ready, c["index"] + 1)
                link(dve.reciprocal(r, r))
                for t in range(c["tiles"]):
                    g = par(c["gain"], t + (4 if c is n_na else 0))
                    ins = dve.scalar_tensor_tensor(out=c["dst"][t], in0=c["src"][t], scalar=g, in1=r,
                                                   op0=ALU.mult, op1=ALU.mult)
                    if last is not None:
                        ins.then_inc(last, 1)
                if last is None:
                    ins.then_inc(normed, 1)
                    dve.wait_ge(normed, c["index"] + 1)

            norm(n_mix)

            dve.wait_ge(cst_loaded, 16)
            free = list(range(40))

            def tmp():
                return small[:, free.pop(0), :]

            def ts(out, a, s1, s2, op0, op1=ALU.bypass):
                if s2 is None:
                    link(dve.tensor_scalar(out, a, s1, None, op0))
                else:
                    link(dve.tensor_scalar(out, a, s1, s2, op0, op1))

            def tt(out, a, b, op):
                link(dve.tensor_tensor(out, a, b, op))

            def stt(out, a, s, b, op0, op1):
                link(dve.scalar_tensor_tensor(out=out, in0=a, scalar=s, in1=b, op0=op0, op1=op1))

            MAGIC = 12582912.0

            def exp_parts(x, w):
                k, r, p, t, ki = (tmp()[:, 0:w] for _ in range(5))
                ts(k, x, 1.4426950408889634, 1000.0, ALU.mult, ALU.min)
                ts(k, k, -1000.0, MAGIC, ALU.max, ALU.add)
                ts(k, k, MAGIC, None, ALU.subtract)
                stt(r, k, -0.693145751953125, x, ALU.mult, ALU.add)
                stt(r, k, -1.42860682030941723e-6, r, ALU.mult, ALU.add)
                ts(r, r, 0.5, -0.5, ALU.min, ALU.max)
                ts(p, r, 1.0 / 40320, 1.0 / 5040, ALU.mult, ALU.add)
                for c in (1.0 / 720, 1.0 / 120, 1.0 / 24, 1.0 / 6, 0.5, 1.0):
                    tt(p, p, r, ALU.mult)
                    ts(p, p, c, None, ALU.add)
                tt(p, p, r, ALU.mult)
                ts(t, k, 127.0, 0.0, ALU.add, ALU.max)
                ts(t, t, 254.0, 8388608.0, ALU.min, ALU.mult)
                link(dve.tensor_copy(ki.bitcast(i32), t))
                tt(p, p, ki, ALU.mult)
                return ki, p

            def keep(n):
                del free[:]
                free.extend(range(n, 40))

            lre, lim = par("lam_re", 0, 8), par("lam_im", 0, 8)
            dt, a, b = tmp(), tmp(), tmp()
            two_k, part = exp_parts(par("log_dt", 0, 8), 8)
            tt(dt, two_k, part, ALU.add)
            tt(a, lre, dt, ALU.mult)
            tt(b, lim, dt, ALU.mult)
            keep(3)
            em1, hs, hc = tmp(), tmp(), tmp()
            two_k, part = exp_parts(a, 8)
            tt(s5p[:, 0, :], two_k, part, ALU.add)
            ts(em1, two_k, -1.0, None, ALU.add)
            tt(em1, em1, part, ALU.add)
            keep(6)
            k, r, x2, s, c = tmp(), tmp(), tmp(), tmp(), tmp()
            ts(k, b, 0.15915494309189535, MAGIC, ALU.mult, ALU.add)
            ts(k, k, MAGIC, None, ALU.subtract)
            stt(r, k, -6.28125, b, ALU.mult, ALU.add)
            stt(r, k, -0.0019350051879882812, r, ALU.mult, ALU.add)
            stt(r, k, -3.019916050561733e-07, r, ALU.mult, ALU.add)
            ts(r, r, 0.5, None, ALU.mult)
            tt(x2, r, r, ALU.mult)

            def series(out, first, coefs):
                ts(out, x2, first, coefs[0], ALU.mult, ALU.add)
                for q in coefs[1:]:
                    tt(out, out, x2, ALU.mult)
                    ts(out, out, q, None, ALU.add)
            series(s, 1.0 / 6227020800, (-1.0 / 39916800, 1.0 / 362880, -1.0 / 5040, 1.0 / 120, -1.0 / 6, 1.0))
            tt(hs, s, r, ALU.mult)
            series(hc, 1.0 / 479001600, (-1.0 / 3628800, 1.0 / 40320, -1.0 / 720, 1.0 / 24, -0.5, 1.0))
            cm1, cosb, sinb, ere, eim, t1, l2, fre, fim = (tmp() for _ in range(9))
            tt(cm1, hs, hs, ALU.mult)
            ts(cm1, cm1, -2.0, None, ALU.mult)
            ts(s5p[:, 1, :], cm1, 1.0, None, ALU.add)
            tt(t1, hs, hc, ALU.mult)
            ts(s5p[:, 2, :], t1, 2.0, None, ALU.mult)
            tt(ere, em1, s5p[:, 1, :], ALU.mult)
            tt(ere, ere, cm1, ALU.add)
            tt(eim, s5p[:, 0, :], s5p[:, 2, :], ALU.mult)
            tt(l2, lre, lre, ALU.mult)
            tt(t1, lim, lim, ALU.mult)
            tt(l2, l2, t1, ALU.add)
            link(dve.reciprocal(l2, l2))
            tt(fre, ere, lre, ALU.mult)
            tt(t1, eim, lim, ALU.mult)
            tt(fre, fre, t1, ALU.add)
            tt(s5p[:, 3, :], fre, l2, ALU.mult)
            tt(fim, eim, lre, ALU.mult)
            tt(t1, ere, lim, ALU.mult)
            tt(fim, fim, t1, ALU.subtract)
            tt(s5p[:, 4, :], fim, l2, ALU.mult)
            ts(s5p[:, 25, :], s5p[:, 4, :], -1.0, None, ALU.mult)
            tt(s5p[:, 5, :], s5p[:, 1, :], s5p[:, 1, :], ALU.bypass) if False else link(dve.tensor_copy(s5p[:, 5, :], s5p[:, 1, :]))
            link(dve.tensor_copy(s5p[:, 6, :], s5p[:, 2, :]))
            for k2 in range(1, 10):
                c0, s0 = s5p[:, 3 + 2 * k2, :], s5p[:, 4 + 2 * k2, :]
                tt(t1, s0, s0, ALU.mult)
                ts(s5p[:, 5 + 2 * k2, :], t1, -2.0, 1.0, ALU.mult, ALU.add)
                tt(t1, c0, s0, ALU.mult)
                ts(s5p[:, 6 + 2 * k2, :], t1, 2.0, None, ALU.mult)
            keep(0)
            lam = par("rg_lam", 0, 2)
            na_, mx_, z, z2 = (tmp()[:, 0:2] for _ in range(4))
            ts(na_, lam, -1.0, None, ALU.mult)
            tt(na_, na_, lam, ALU.min)
            ts(mx_, lam, -1.0, 0.0, ALU.mult, ALU.max)
            two_k, part = exp_parts(na_, 2)
            tt(z, two_k, part, ALU.add)
            ts(z2, z, 2.0, None, ALU.add)
            link(dve.reciprocal(z2, z2))
            tt(z, z, z2, ALU.mult)
            tt(z2, z, z, ALU.mult)
            lg = tmp()[:, 0:2]
            ts(lg, z2, 2.0 / 17, 2.0 / 15, ALU.mult, ALU.add)
            for q in (13, 11, 9, 7, 5, 3, 1):
                tt(lg, lg, z2, ALU.mult)
                ts(lg, lg, 2.0 / q, None, ALU.add)
            tt(lg, lg, z, ALU.mult)
            tt(lg, lg, mx_, ALU.add)
            ts(sp4[:], lg, 4.0, None, ALU.mult)

            def biased(u):
                h, i = u // NT, u % NT
                k0, k1 = key_tiles(h, i)
                nk = (k1 - k0) * P
                n = use_s[u]
                if i == 0:
                    dve.wait_ge(strip_loaded[h % 2], 16 * (h // 2 + 1))
                dve.wait_ge(mm_done, done(n))
                if u >= 3:
                    dve.wait_ge(mm_done, done(use_t[u - 3]))
                st = STRIPS[h % 2]
                if h < 8:
                    bias = st[:, 896 - P * i:896 - P * i + nk]
                elif 2 <= i <= 5:
                    bias = st[:, NF:NF + NI]
                else:
                    bias = st[:, (3 + k0 - i) * P:(3 + k0 - i) * P + nk]
                dve.tensor_tensor_reduce(out=SB[u % 3][:, 0:nk], in0=PS[n % SLOTS][:, 0:nk], in1=bias, scale=-1.0,
                                         scalar=3.0e38, op0=ALU.add, op1=ALU.min,
                                         accum_out=negm[:, u % 4:u % 4 + 1]).then_inc(scores_ready, 1)

            def scaled(u):
                k0, k1 = key_tiles(u // NT, u % NT)
                dve.wait_ge(exp_done, u + 1)
                rd = rden[:, u % 4:u % 4 + 1]
                link(dve.reciprocal(rd, den[:, u % 4:u % 4 + 1]))
                s = SB[u % 3][:, 0:(k1 - k0) * P]
                dve.tensor_scalar(s, s, rd, None, ALU.mult).then_inc(probs_ready, 1)

            def head_out(u):
                h, i = u // NT, u % NT
                n = use_o[u]
                r0 = (h % 2) * DH
                dve.wait_ge(mm_done, done(n))
                dve.tensor_copy(Bp[h // 2][r0:r0 + DH, i * P:(i + 1) * P], PS[n % SLOTS][0:DH, 0:P]).then_inc(heads_done, 1)

            for t in range(NU + LAG_O + 1):
                if t < NU:
                    biased(t)
                if 0 <= t - 1 < NU:
                    scaled(t - 1)
                if 0 <= t - LAG_O - 1 < NU:
                    head_out(t - LAG_O - 1)
            norm(n_dil)
            norm(n_na)

            def add_to_h(n0, base):
                for m in range(8):
                    dve.wait_ge(mm_done, done(n0 + m))
                    dve.tensor_tensor(Hp[m], PS[(n0 + m) % SLOTS][:, :], Hp[m], ALU.add).then_inc(h_ready, 1)

            dve.wait_ge(x_again, 16)
            add_to_h(P_OUT, 0)
            norm(n_ffn)

            def v3(name, n):
                return R(name).rearrange("p (t n) -> p t n", n=n)

            def bc(name, n):
                return R(name).unsqueeze(2).to_broadcast([P, NT, n])

            tie = mat("tie", 0, 4).unsqueeze(1).to_broadcast([P, NT, 4])
            dve.wait_ge(mm_done, done(P_ROUTE))
            link(dve.tensor_tensor(v3("L", 20), PS[P_ROUTE % SLOTS][:, 0:160].rearrange("p (t n) -> p t n", n=20),
                                   mat("bias20", 0, 20).unsqueeze(1).to_broadcast([P, NT, 20]), ALU.add))
            g4 = v3("L", 20)[:, :, 0:4]
            link(dve.tensor_reduce(R("gm"), g4, AX.X, ALU.max))
            dve.tensor_tensor(v3("gd", 4), g4, bc("gm", 4), ALU.subtract).then_inc(gdiff_ready, 1)

            def first_of_max(oh, vals, mx, t4):
                link(dve.tensor_tensor(v3(t4, 4), vals, bc(mx, 4), ALU.is_equal))
                link(dve.tensor_tensor(v3(t4, 4), v3(t4, 4), tie, ALU.mult))
                link(dve.tensor_reduce(R("tm"), v3(t4, 4), AX.X, ALU.max))
                link(dve.tensor_tensor(v3(oh, 4), v3(t4, 4), bc("tm", 4), ALU.is_equal))
            first_of_max("oh", g4, "gm", "t4")
            for g in range(N_GRP):
                sel = v3("oh", 4)[:, :, g:g + 1].to_broadcast([P, NT, 4])
                link(dve.tensor_tensor(v3("t5" if g else "v4", 4), v3("L", 20)[:, :, 4 + 4 * g:8 + 4 * g], sel, ALU.mult))
                if g:
                    link(dve.tensor_tensor(R("v4"), R("v4"), R("t5"), ALU.add))
            link(dve.tensor_reduce(R("m1"), v3("v4", 4), AX.X, ALU.max))
            first_of_max("o1", v3("v4", 4), "m1", "t4")
            link(dve.scalar_tensor_tensor(out=R("v4b"), in0=R("o1"), scalar=-3.0e38, in1=R("v4"), op0=ALU.mult, op1=ALU.add))
            link(dve.tensor_reduce(R("m2"), v3("v4b", 4), AX.X, ALU.max))
            first_of_max("o2", v3("v4b", 4), "m2", "t4")
            dve.tensor_tensor(R("d1"), R("m2"), R("m1"), ALU.subtract).then_inc(tdiff_ready, 1)
            dve.wait_ge(gexp_done, 1)
            link(dve.tensor_reduce(R("gs"), v3("gd", 4), AX.X, ALU.add))
            dve.wait_ge(texp_done, 1)
            link(dve.tensor_scalar(R("w1"), R("d1"), 1.0, None, ALU.add))
            link(dve.tensor_tensor(R("w1"), R("w1"), R("gs"), ALU.mult))
            link(dve.reciprocal(R("w1"), R("w1")))
            link(dve.tensor_tensor(R("w2"), R("w1"), R("d1"), ALU.mult))
            link(dve.tensor_tensor(v3("c4", 4), v3("o1", 4), bc("w1", 4), ALU.mult))
            link(dve.tensor_tensor(v3("t4", 4), v3("o2", 4), bc("w2", 4), ALU.mult))
            link(dve.tensor_tensor(R("c4"), R("c4"), R("t4"), ALU.add))
            for g in range(N_GRP):
                sel = v3("oh", 4)[:, :, g:g + 1].to_broadcast([P, NT, 4])
                last = dve.tensor_tensor(v3("comb", 16)[:, :, 4 * g:4 * g + 4], v3("c4", 4), sel, ALU.mult)
            last.then_inc(comb_ready, 1)

            for g in range(N_GRP):
                for el in range(EPG):
                    e = EPG * g + el
                    for f in range(FT):
                        j = 2 * e + f
                        n = P_MOE + 24 * g + 4 * el + 2 * f + 1
                        pg = Wp[16 + j % 2]
                        dve.wait_ge(mm_done, done(n))
                        dve.wait_ge(silu_ready, j + 1)
                        link(dve.tensor_tensor(pg, PS[n % SLOTS][:, :], pg, ALU.mult))
                        if f == 0:
                            dve.wait_ge(comb_loaded[e % 2], 16 * (e // 2 + 1))
                        dve.tensor_tensor(Wp[2 * el + f], pg, combB[e % 2], ALU.mult).then_inc(act_ready, 1)
                add_to_h(P_MOE + 24 * g + 16, 8 + 8 * g)
            norm(n_fin1)
            norm(n_att2)

            dve.wait_ge(in2_ready, 19)
            for c in range(2):
                x, y = Wp[PG_RX + c], Wp[19 + c]
                link(dve.tensor_scalar(y, x, par("rg_w", 6 + c), par("rg_cb", c), ALU.mult, ALU.add))
                for s_ in range(1, 4):
                    ins = dve.scalar_tensor_tensor(out=y[:, s_:S], in0=x[:, 0:S - s_], scalar=par("rg_w", 2 * (3 - s_) + c),
                                                   in1=y[:, s_:S], op0=ALU.mult, op1=ALU.add)
                    if s_ < 3:
                        link(ins)
                    else:
                        ins.then_inc(conv_ready, 1)
            dve.wait_ge(conv_ready, 2)
            dve.wait_ge(tanh_ready, 2)
            for c in range(2):
                last = dve.tensor_scalar(Bp[2 + c], Wp[21 + c], 1.0, None, ALU.add)
            link(last)
            for c in range(2):
                last = dve.reciprocal(Bp[2 + c], Bp[2 + c])
            link(last)
            for c in range(2):
                dve.tensor_tensor(Wp[23 + c], Wp[23 + c], Wp[19 + c], ALU.mult)
                last = dve.tensor_scalar(Bp[4 + c], Bp[2 + c], 2.0, -1.0, ALU.mult, ALU.add)
            link(last)
            dve.wait_ge(root_ready, 2)
            for c in range(2):
                last = dve.tensor_tensor(Bp[2 + c], Bp[2 + c], Bp[c], ALU.mult)
            link(last)
            for c in range(2):
                last = dve.tensor_tensor(Wp[23 + c], Wp[23 + c], Bp[2 + c], ALU.mult)
            link(last)
            for c in range(2):
                last = dve.tensor_tensor_scan(Wp[PG_RX + c], Bp[4 + c], Wp[23 + c], 0.0, ALU.mult, ALU.add)
            link(last)
            dve.wait_ge(ggate_ready, 2)
            for c in range(2):
                last = dve.tensor_tensor(Wp[PG_RX + c], Wp[PG_RX + c], Wp[PG_RG + c], ALU.mult)
            last.then_inc(rg_ready, 1)
            norm(n_rg)

            dve.wait_ge(s5_loaded, 16)
            for j in range(8):
                cols = slice(j * P, (j + 1) * P)
                fr, fi, nfi = s5p[:, 3, j:j + 1], s5p[:, 4, j:j + 1], s5p[:, 25, j:j + 1]
                dve.tensor_scalar(Wp[19][:, cols], Bp[0][:, cols], fi, None, ALU.mult)
                last = dve.tensor_scalar(Wp[20][:, cols], Bp[1][:, cols], nfi, None, ALU.mult)
            link(last)
            for j in range(8):
                cols = slice(j * P, (j + 1) * P)
                fr = s5p[:, 3, j:j + 1]
                dve.scalar_tensor_tensor(out=Bp[0][:, cols], in0=Bp[0][:, cols], scalar=fr, in1=Wp[20][:, cols],
                                         op0=ALU.mult, op1=ALU.add)
                last = dve.scalar_tensor_tensor(out=Bp[1][:, cols], in0=Bp[1][:, cols], scalar=fr, in1=Wp[19][:, cols],
                                                op0=ALU.mult, op1=ALU.add)
            last.then_inc(s5b_ready, 1)
            ec, es, vr, vi = Wp[2], Wp[3], Wp[19], Wp[20]
            ta, tb, xr, xi = Wp[21], Wp[22], Wp[4], Wp[5]
            dve.memset(ec[:, 0:1], 1.0)
            link(dve.memset(es[:, 0:1], 0.0))
            for c in range(2):
                last = dve.tensor_scalar(Wp[24 - c], Wp[PG_U + c], par("s5_d", c), None, ALU.mult)
            link(last)
            for j in range(8):
                rr = s5p[:, 0, j:j + 1]
                for k2 in range(10):
                    n = 1 << k2
                    wc, ws = s5p[:, 5 + 2 * k2, j:j + 1], s5p[:, 6 + 2 * k2, j:j + 1]
                    dve.tensor_scalar(ta[:, 0:n], es[:, 0:n], ws, None, ALU.mult)
                    link(dve.tensor_scalar(tb[:, 0:n], ec[:, 0:n], ws, None, ALU.mult))
                    dve.scalar_tensor_tensor(out=ec[:, n:2 * n], in0=ec[:, 0:n], scalar=wc, in1=ta[:, 0:n],
                                             op0=ALU.mult, op1=ALU.subtract)
                    link(dve.scalar_tensor_tensor(out=es[:, n:2 * n], in0=es[:, 0:n], scalar=wc, in1=tb[:, 0:n],
                                                  op0=ALU.mult, op1=ALU.add))
                n0 = P_S5 + 3 * j
                dve.wait_ge(mm_done, done(n0 + 1))
                bre, bim = PS[n0 % SLOTS][:, :], PS[(n0 + 1) % SLOTS][:, :]
                dve.tensor_tensor(vr, bre, ec, ALU.mult)
                dve.tensor_tensor(ta, bim, es, ALU.mult)
                dve.tensor_tensor(vi, bim, ec, ALU.mult)
                dve.tensor_tensor(tb, bre, es, ALU.mult).then_inc(s5in_ready, 1)
                dve.wait_ge(s5in_ready, j + 1)
                dve.tensor_tensor(vr, vr, ta, ALU.add)
                link(dve.tensor_tensor(vi, vi, tb, ALU.subtract))
                dve.tensor_tensor_scan(vr, rr.to_broadcast([P, S]), vr, 0.0, ALU.mult, ALU.add)
                link(dve.tensor_tensor_scan(vi, rr.to_broadcast([P, S]), vi, 0.0, ALU.mult, ALU.add))
                if j:
                    dve.wait_ge(mm_done, done(n0 - 1))
                dve.tensor_tensor(xr, vr, ec, ALU.mult)
                dve.tensor_tensor(ta, vi, es, ALU.mult)
                dve.tensor_tensor(xi, vi, ec, ALU.mult)
                link(dve.tensor_tensor(tb, vr, es, ALU.mult))
                dve.tensor_tensor(xr, xr, ta, ALU.subtract)
                dve.scalar_tensor_tensor(out=xi, in0=xi, scalar=-1.0, in1=tb, op0=ALU.mult,
                                         op1=ALU.subtract).then_inc(s5x_ready, 1)
                dve.wait_ge(mm_done, done(n0 + 2))
                acc = Wp[24 - j // 4]
                dve.tensor_tensor(acc, PS[(n0 + 2) % SLOTS][:, :], acc, ALU.add).then_inc(s5y_ready, 1)
            dve.wait_ge(s5s_ready, 2)
            for c in range(2):
                dve.tensor_tensor(Wp[c], Wp[c], Wp[22 - c], ALU.mult).then_inc(s5_ready, 1)
            norm(n_s5)

            bcp, ex = pair(0), pair(2)
            for m in range(2):
                n = P_GK + m
                dve.wait_ge(mm_done, done(n))
                x = PS[n % SLOTS][:, :]
                dve.tensor_scalar(Wp[m], x, par("gk_bias", m), None, ALU.add).then_inc(gk_biased, 1)
                dve.wait_ge(gk_biased, m + 1)
                dve.scalar_tensor_tensor(out=Wp[2 + m], in0=Wp[m], scalar=-1.0, in1=Wp[m], op0=ALU.mult, op1=ALU.max).then_inc(gk_abs, 1)
                link(dve.tensor_scalar(Wp[m], Wp[m], 0.0, 1.0 / 16, ALU.min, ALU.mult))
            link(dve.memset(Wp[4], 1.0))
            link(dve.memset(Wp[4].rearrange("p (n c) -> p n c", c=CH)[:, :, 0:1], 0.0))
            dve.wait_ge(gk_ln, 1)
            link(dve.scalar_tensor_tensor(out=bcp, in0=ex, scalar=-1.0 / 16, in1=bcp, op0=ALU.mult, op1=ALU.add))
            for m in range(2):
                last = dve.tensor_tensor_scan(Wp[m], Wp[4], Wp[m], 0.0, ALU.mult, ALU.add)
            link(last)
            q, k = pair(PG_Q), pair(PG_K)

            def chunks(ap):
                return ap.rearrange("p a (n c) -> p (a n) c", c=CH)
            b3 = chunks(bcp)
            mid = b3[:, :, CH // 2 - 1:CH // 2].to_broadcast([P, 2 * NCH, CH])
            end = b3[:, :, CH - 1:CH].to_broadcast([P, 2 * NCH, CH])
            dve.tensor_tensor(chunks(ex), b3, mid, ALU.subtract).then_inc(bc_ready, 1)
            dve.wait_ge(gexps, 1)
            link(dve.tensor_tensor(pair(4), q, ex, ALU.mult))
            dve.tensor_tensor(chunks(ex), mid, b3, ALU.subtract).then_inc(gexps_used, 1)
            dve.wait_ge(gexps, 2)
            link(dve.tensor_tensor(pair(19), k, ex, ALU.mult))
            dve.tensor_tensor(chunks(ex), end, b3, ALU.subtract).then_inc(gexps_used, 1)
            dve.wait_ge(gexps, 3)
            dve.tensor_tensor(k, k, ex, ALU.mult).then_inc(gprods, 1)
            dve.wait_ge(gexps, 4)
            dve.tensor_tensor(q, q, ex, ALU.mult).then_inc(gprods, 1)
            dve.wait_ge(gprods, 2)
            dve.wait_ge(decay_ready, 1)
            st = [pair(23).rearrange("p a (b c) -> p (a b) c", c=P), pair(2).rearrange("p a (b c) -> p (a b) c", c=P)]
            for m in range(2):
                for q4 in range(4):
                    n_ = P_KV + 4 * m + q4
                    dve.wait_ge(mm_done, done(n_))
                    for j in range(4):
                        n = 4 * q4 + j
                        if n == NCH - 1:
                            continue
                        for hh in range(2):
                            r = slice(hh * DH, (hh + 1) * DH)
                            c0 = (j % 2) * HALF + (j // 2) * 256 + hh * P
                            kv = PS[n_ % SLOTS][r, c0:c0 + P]
                            if n == 0:
                                last = dve.tensor_copy(st[m][r, 1, :], kv)
                            else:
                                last = dve.scalar_tensor_tensor(out=st[m][r, n + 1, :], in0=st[m][r, n, :],
                                                                scalar=decay[r, m, n:n + 1], in1=kv,
                                                                op0=ALU.mult, op1=ALU.add)
                        if j < 3 and n < NCH - 2:
                            link(last)
                    last.then_inc(state_ready, 1)
                    dve.wait_ge(state_ready, 4 * m + q4 + 1)
            causal = mat("causal").bitcast(i32)
            for h in range(4):
                n = P_SC + h
                if h == 3:
                    dve.wait_ge(mm_done, done(P_KV + 7))
                link(dve.memset(Mp[h], 0.0))
                dve.wait_ge(mm_done, done(n))
                for tt_ in range(NT):
                    cols = slice(tt_ * P, (tt_ + 1) * P)
                    last = dve.copy_predicated(Mp[h][:, cols], causal, PS[n % SLOTS][:, cols])
                last.then_inc(intra_ready, 1)
            for h in range(4):
                norm_c = n_gla[h]
                norm(norm_c)
                dve.wait_ge(gsilu, h + 1)
                dve.tensor_tensor(Bp[h], Bp[h], Wp[PG_G + h], ALU.mult).then_inc(gla_ready, 1)
            add_to_h(P_OUT2, 8 + 8 * N_GRP)
            norm(n_mlp)

            for j in range(FF):
                n = P_UP + 2 * j
                y, x = Wp[22 + j % 3], PS[n % SLOTS]
                dve.wait_ge(conv0_ready, j + 1)
                link(dve.scalar_tensor_tensor(out=y[:, 1:S], in0=x[:, 0:S - 1], scalar=par("ff_w", FF + j), in1=y[:, 1:S],
                                              op0=ALU.mult, op1=ALU.add))
                dve.scalar_tensor_tensor(out=y[:, 2:S], in0=x[:, 0:S - 2], scalar=par("ff_w", j), in1=y[:, 2:S],
                                         op0=ALU.mult, op1=ALU.add).then_inc(conv1_ready, 1)
                dve.wait_ge(conv1_ready, j + 1)
                dve.wait_ge(gelu_ready, j + 1)
                dve.wait_ge(mm_done, done(n + 1))
                dve.tensor_tensor(Wp[j], PS[(n + 1) % SLOTS][:, :], y, ALU.mult).then_inc(ffact_ready, 1)
            add_to_h(P_DOWN, 16 + 8 * N_GRP)
            norm(n_fin2, final_ready)


def dilated_strips():
    d = np.arange(STRIP)[None, :] - 896 - np.arange(P)[:, None]
    ad = np.abs(d)
    count = ((ad <= 64).astype(int) + ((d % 4 == 0) & (ad <= 256)) + (d % 16 == 0))
    base = np.where(count > 0, np.log(np.maximum(count, 1)), NEG)
    slopes = 2.0 ** -np.arange(1, 9)
    return np.stack([np.where(count > 0, base - s * ad, NEG) for s in slopes]).astype(np.float32)


def neighbourhood_strips(rpb):
    q, k = np.arange(P), np.arange(NF)
    qr, qc = (q // 64)[:, None], (q % 64)[:, None]
    kr, kc = (k // 64 - 6)[None, :], (k % 64)[None, :]
    dr, dc = kr - qr + 7, kc - qc + 15
    cs = np.clip(qc - 8, 0, 48)
    col_ok = (kc >= cs) & (kc < cs + 16)
    ok = col_ok & (dr >= 0) & (dr <= 14)
    full = np.where(ok, rpb[:, np.clip(dr, 0, 14), np.clip(dc, 0, 30)], np.float32(NEG))
    rows = (kr >= qr - 4) & (kr < qr + 4)
    inner = np.where(rows, full, np.float32(NEG))[:, :, P:P + NI]
    return np.ascontiguousarray(np.concatenate([full, inner], axis=2))


def column_units(w):
    k, m = w.shape
    return np.ascontiguousarray(w.reshape(k // P, P, m // P, P).transpose(2, 1, 0, 3).reshape(m // P, P, (k // P) * P))


def pack(i):
    f = np.float32

    def tiles(v):
        return np.asarray(v, f).reshape(-1, P).T
    x = np.asarray(i["x"])[0]
    cst = np.zeros((P, NCOL), f)

    def put(name, a, cols=PCOLS):
        a = np.asarray(a, f)
        cst[:a.shape[0], cols[name]:cols[name] + a.shape[1]] = a
    put("norm_mix", tiles(i["norm_mix_g"][0]))
    put("g_out", np.concatenate([tiles(i["g_out_dil"][0]), tiles(i["g_out_na"][0])], 1))
    put("norm_ffn", tiles(i["norm_ffn_g"][0]))
    put("norm_final", tiles(i["norm_final_g"]))
    put("attn_norm", tiles(i["attn_norm_2"][0]))
    put("gk_bias", tiles(i["gla_b_gk_2"][0]))
    put("gla_norm", tiles(i["gla_norm_2"][0]))
    put("lam_re", tiles(i["s5_lambda_re_2"][0].reshape(-1)))
    put("lam_im", tiles(i["s5_lambda_im_2"][0].reshape(-1)))
    put("log_dt", tiles(np.repeat(i["s5_log_dt_2"][0], 64)))
    put("s5_d", tiles(i["s5_d_2"][0]))
    put("b_glu", tiles(i["s5_b_glu_2"][0]))
    put("s5_norm", tiles(i["s5_norm_2"][0]))
    put("rg_w", np.concatenate([tiles(i["rg_conv_w_2"][0][t]) for t in range(4)], 1))
    put("rg_cb", tiles(i["rg_conv_b_2"][0]))
    put("rg_ba", tiles(i["rg_b_a_2"][0]))
    put("rg_bx", tiles(i["rg_b_x_2"][0]))
    put("rg_lam", tiles(i["rg_lambda_2"][0]))
    put("rg_norm", tiles(i["rg_norm_2"][0]))
    put("mlp_norm", tiles(i["mlp_norm_2"][0]))
    put("ff_w", np.concatenate([tiles(i["mlp_conv_w_2"][0][t]) for t in range(3)], 1))
    put("ff_cb", tiles(i["mlp_conv_b_2"][0]))
    put("final_norm", tiles(i["final_norm_2"]))
    put("ones", np.ones((P, P)), MCOLS)
    put("ident", np.eye(P), MCOLS)
    s, c = np.arange(P)[:, None], np.arange(P)[None, :]
    put("causal", ((c >= s) & (c // CH == s // CH)).astype(f), MCOLS)
    route = np.concatenate([i["w_group"][0], i["w_router"][0]], 1)
    put("route", route.reshape(NT, P, 20).transpose(1, 0, 2).reshape(P, -1), MCOLS)
    w2 = np.asarray(i["w_in_2"][0])
    put("low", w2[:, 1536:1552].reshape(NT, P, 16).transpose(1, 0, 2).reshape(P, -1), MCOLS)
    rg = np.zeros((P, 4, P), f)
    for j, name in enumerate(("rg_w_a_2", "rg_w_x_2")):
        for h in range(4):
            r = (h % 2) * 64
            rg[r:r + 64, 2 * j + h // 2, r:r + 64] = i[name][0][h]
    put("rg", rg.reshape(P, -1), MCOLS)
    put("glu", np.asarray(i["s5_w_glu_2"][0]).reshape(2, P, 256).transpose(1, 0, 2).reshape(P, -1), MCOLS)
    put("gkup", i["gla_w_gk_up_2"][0], MCOLS)
    put("bias20", np.broadcast_to(np.concatenate([i["b_group"][0], i["b_router"][0]])[None], (P, 20)), MCOLS)
    put("tie", np.broadcast_to(np.array([4.0, 3.0, 2.0, 1.0])[None], (P, 4)), MCOLS)

    w = np.asarray(i["w_in"][0])
    cols = {"dil": [w[:, 512 * n:512 * (n + 1)] for n in range(3)], "na": [w[:, 1536 + 512 * n:1536 + 512 * (n + 1)] for n in range(3)]}
    w_in = column_units(np.concatenate([cols["dil"][0], cols["na"][0], cols["dil"][1], cols["na"][1], cols["dil"][2], cols["na"][2]], 1))
    moe = []
    for g in range(N_GRP):
        for e in range(EPG * g, EPG * g + EPG):
            gate, up = column_units(i["w_gate"][0][e]), column_units(i["w_up"][0][e])
            moe += [gate[0], up[0], gate[1], up[1]]
        moe += list(column_units(np.asarray(i["w_down"][0][EPG * g:EPG * g + EPG]).reshape(EPG * 256, D)))
    w_in2 = column_units(np.concatenate([w2[:, 1808:2064], w2[:, 2064:2320], w2[:, 1552:1808], w2[:, 0:512], w2[:, 1024:1536], w2[:, 512:1024]], 1))
    up_u = column_units(i["w_up_2"][0])
    w_up = np.stack([up_u[j // 2 + (j % 2) * FF] for j in range(2 * FF)])
    down = column_units(np.concatenate([i["w_down_2"][0], np.zeros((2 * P, D), f)], 0))
    w_down = np.ascontiguousarray(down.reshape(8, P, 3, NT * P).transpose(0, 2, 1, 3).reshape(24, P, NT * P))
    mats = np.zeros((P, 4, 8, P), f)
    for g in range(16):
        r, j, c0 = (g % 2) * 64, g // 2, (g % 8) * 16
        mats[r:r + 64, 0, j, c0:c0 + 16] = i["s5_b_re_2"][0][g]
        mats[r:r + 64, 1, j, c0:c0 + 16] = i["s5_b_im_2"][0][g]
        mats[r:r + 64, 2, j, c0:c0 + 16] = i["s5_c_re_2"][0][g].T
        mats[r:r + 64, 3, j, c0:c0 + 16] = i["s5_c_im_2"][0][g].T
    return {
        "xT": np.ascontiguousarray(x.T.reshape(NT, P, S).transpose(1, 0, 2)),
        "params": cst, "w_in_units": w_in, "w_out_units": column_units(i["w_out"][0]), "w_moe_units": np.stack(moe),
        "w_in2_units": w_in2, "w_out2_units": column_units(i["w_out_2"][0]), "w_up_units": w_up, "w_down_units": w_down,
        "dil_strip": dilated_strips(), "na_strip": neighbourhood_strips(np.asarray(i["rpb"][0])),
        "s5_mats": mats.reshape(P, 4, 8 * P),
    }


def kernel(**inputs):
    import concourse.bacc as bacc
    from concourse.bass_utils import run_bass_kernel_spmd

    nc = bacc.Bacc("TRN2", target_bir_lowering=False, num_devices=1)
    arrays = pack({k: np.asarray(v) for k, v in inputs.items()})
    args = [nc.dram_tensor(k, a.shape, mybir.dt.from_np(a.dtype), kind="ExternalInput").ap() for k, a in arrays.items()]
    args.append(nc.dram_tensor("outT", (P, NT, S), mybir.dt.float32, kind="ExternalOutput").ap())
    build(nc, *args)
    r = run_bass_kernel_spmd(nc, [arrays], core_ids=[0])
    got = r.results[0]["outT"]
    return np.ascontiguousarray(got.transpose(1, 0, 2).reshape(D, S).T).reshape(1, S, D)
```

```python
import concourse.bass as bass
from concourse import mybir
from contextlib import ExitStack
import numpy as np

P = 128
S = 1024
D = 1024
NT = D // P
HALF = 512
DH = 64
NH = 16
NEG = -1e30
EPS = 1e-6
SLOTS = 4
RING = 8
STRIP = 1920
NF, NI = 7 * P, 5 * P
N_EXP, N_GRP, EPG = 16, 4, 4
F_EXP = 256
NBLK = 2 * S // P + N_EXP - 1
XPG = 6
XBUF = 3
FF = 22
CH = 64
NCH = S // CH

PCOLS = {}
_at = 0
for _name, _n in (("norm_mix", 8), ("g_out", 8), ("norm_ffn", 8), ("norm_final", 8), ("attn_norm", 8),
                  ("gk_bias", 2), ("gla_norm", 1), ("lam_re", 8), ("lam_im", 8), ("log_dt", 8), ("s5_d", 2),
                  ("b_glu", 2), ("s5_norm", 2), ("rg_w", 8), ("rg_cb", 2), ("rg_ba", 2), ("rg_bx", 2),
                  ("rg_lam", 2), ("rg_norm", 2), ("mlp_norm", 8), ("ff_w", 3 * FF), ("ff_cb", FF), ("final_norm", 8)):
    PCOLS[_name] = _at
    _at += _n
MCOLS = {}
for _name, _n in (("ones", P), ("ident", P), ("causal", P), ("route", NT * 20), ("low", NT * 16), ("rg", 4 * P),
                  ("glu", 2 * 256), ("gkup", 256), ("bias20", 20), ("tie", 4), ("before", P), ("blk", 31)):
    MCOLS[_name] = _at
    _at += _n
NCOL = _at


def key_tiles(h, i):
    if h < 8:
        return 0, 8
    return (max(i - 2, 0), min(i + 3, 8)) if 2 <= i <= 5 else ((0, 4) if i < 2 else (4, 8))


def build(nc, xT, params, w_in, w_out, w_moe, w_in2, w_out2, w_up, w_down, dil_strip, na_strip, s5_mats, out):
    f32, i32, u32 = mybir.dt.float32, mybir.dt.int32, mybir.dt.uint32
    ALU, ACT, AX = mybir.AluOpType, mybir.ActivationFunctionType, mybir.AxisListType
    x_slots = nc.dram_tensor("x_slots", (NBLK * P, D), f32, kind="Internal").ap()
    y_slots = nc.dram_tensor("y_slots", (NBLK * P, D), f32, kind="Internal").ap()

    ctx = ExitStack()
    with ctx:
        def sb(name, shape, dt=f32):
            return ctx.enter_context(nc.sbuf_tensor(name, shape, dt))

        def sem(name):
            return ctx.enter_context(nc.semaphore(name))

        hT = sb("hT", [P, NT, S])
        ring = sb("ring", [P, RING, NT * P])
        W = sb("work", [P, 33, S])
        bT = W[:, 25:33, :]
        cst = sb("cst", [P, NCOL])
        small = sb("small", [P, 40, 8])
        s5p = sb("s5p", [P, 26, 8])
        sp4 = sb("sp4", [P, 2])
        epsc = sb("epsc", [P, 1])
        negm = sb("negm", [P, 4])
        den = sb("den", [P, 4])
        rden = sb("rden", [P, 4])
        decay = sb("decay", [P, 2, NCH])
        PS = [ctx.enter_context(nc.psum_tensor(f"ps{i}", [P, S], f32)) for i in range(SLOTS)]

        def par(name, c=0, n=1):
            return cst[:, PCOLS[name] + c:PCOLS[name] + c + n]

        def mat(name, c=0, n=P):
            return cst[:, MCOLS[name] + c:MCOLS[name] + c + n]

        ones, ident = mat("ones"), mat("ident")
        mix_ones = ones

        w_loaded = [sem(f"w_loaded{i}") for i in range(RING)]
        mm_done = sem("mm_done")
        x_loaded = [sem(f"x_loaded{i}") for i in range(4)]
        cst_loaded = sem("cst_loaded")
        strip_loaded = [sem(f"strip_loaded{i}") for i in range(2)]
        x_again = sem("x_again")
        s5_loaded = sem("s5_loaded")
        zero_set, slots_zeroed, x_scattered = sem("zero_set"), sem("slots_zeroed"), sem("x_scattered")
        expert_dma = [sem(f"expert_dma{i}") for i in range(XBUF)]
        expert_loaded, blocks_done = sem("expert_loaded"), sem("blocks_done")
        block_loaded = [sem(f"block_loaded{i}") for i in range(2)]
        y_stored = [sem(f"y_stored{i}") for i in range(3)]
        y_gathered = [sem(f"y_gathered{i}") for i in range(4)]
        member_ready, rank_read, dispatch_ready, xtm_ready = (
            sem("member_ready"), sem("rank_read"), sem("dispatch_ready"), sem("xtm_ready"))
        xT_ready, up_ready, hT_ready, y_ready, ysum_ready = (
            sem("xT_ready"), sem("up_ready"), sem("hT_ready"), sem("y_ready"), sem("ysum_ready"))
        ysum_added = sem("ysum_added")
        out_stored = sem("out_stored")
        sq_ready, sq_used, std_ready, normed = sem("sq_ready"), sem("sq_used"), sem("std_ready"), sem("normed")
        eps_set = sem("eps_set")
        qkv_ready = sem("qkv_ready")
        scores_ready, exp_done, probs_ready, pT_ready, heads_done = (
            sem("scores_ready"), sem("exp_done"), sem("probs_ready"), sem("pT_ready"), sem("heads_done"))
        h_ready = sem("h_ready")
        gdiff_ready, gexp_done, tdiff_ready, texp_done = (
            sem("gdiff_ready"), sem("gexp_done"), sem("tdiff_ready"), sem("texp_done"))
        silu_ready = sem("silu_ready")
        in2_ready = sem("in2_ready")
        conv_ready, gates_ready, tanh_ready, root_ready, ggate_ready, rg_ready = (
            sem("conv_ready"), sem("gates_ready"), sem("tanh_ready"), sem("root_ready"), sem("ggate_ready"), sem("rg_ready"))
        s5b_ready, s5bT_ready, s5x_ready, s5y_ready, s5g_ready, s5s_ready, s5_ready = (
            sem("s5b_ready"), sem("s5bT_ready"), sem("s5x_ready"), sem("s5y_ready"), sem("s5g_ready"), sem("s5s_ready"), sem("s5_ready"))
        s5in_ready, gk_biased, gexps_used, decay_ready, gk_abs, gk_exp, gk_ln, bc_ready, gexps, gprods, klT_ready, state_ready, intra_ready, o_ready, gsilu, gla_ready = (
            sem(n) for n in ("s5in_ready", "gk_biased", "gexps_used", "decay_ready", "gk_abs", "gk_exp", "gk_ln", "bc_ready", "gexps", "gprods", "klT_ready", "state_ready",
                             "intra_ready", "o_ready", "gsilu", "gla_ready"))
        conv0_ready, conv1_ready, gelu_ready, ffact_ready = (
            sem("conv0_ready"), sem("conv1_ready"), sem("gelu_ready"), sem("ffact_ready"))
        dve_link, act_link = sem("dve_link"), sem("act_link")
        final_ready = sem("final_ready")

        units = [w_in[n] for n in range(24)] + [w_out[n] for n in range(8)]
        units += [w_in2[n] for n in range(18)] + [w_out2[n] for n in range(8)]
        units += [w_up[n] for n in range(2 * FF)] + [w_down[n] for n in range(24)]
        U_IN, U_OUT, U_IN2 = 0, 24, 32
        U_OUT2 = U_IN2 + 18
        U_UP = U_OUT2 + 8
        U_DOWN = U_UP + 2 * FF

        at = [0]

        def take(k):
            at[0] += k
            return at[0] - k

        norms = []
        sq_base = [0]

        emptied = {}

        def done(n):
            return n + 1 - sum(c["use"] < n for c in norms)

        def add_norm(src, gain, dst, scratch, tiles, use):
            norms.append(dict(src=src, gain=gain, dst=dst, scratch=scratch, tiles=tiles, use=use, sq0=sq_base[0],
                              index=len(norms)))
            sq_base[0] += tiles
            emptied[use] = (std_ready, len(norms))
            return norms[-1]

        Hp = [hT[:, t, :] for t in range(NT)]
        Bp = [bT[:, t, :] for t in range(NT)]
        Wp = [W[:, t, :] for t in range(25)]

        n_mix = add_norm(Hp, "norm_mix", Bp, Wp[22:25], 8, take(1))
        U_QKV = take(24)
        LAG_T, LAG_O = 2, 3
        NU = NH * NT
        use_s, use_t, use_o = {}, {}, {}
        for t in range(NU + LAG_O):
            if t < NU:
                use_s[t] = take(1)
            if 0 <= t - LAG_T < NU:
                use_t[t - LAG_T] = take(1)
            if 0 <= t - LAG_O < NU:
                use_o[t - LAG_O] = take(1)
        n_dil = add_norm(Bp[0:4], "g_out", Bp[0:4], Wp[16:19], 4, take(1))
        n_na = add_norm(Bp[4:8], "g_out", Bp[4:8], Wp[19:22], 4, take(1))
        P_OUT = take(8)
        n_ffn = add_norm(Hp, "norm_ffn", Bp, Wp[10:13], 8, take(1))
        P_ROUTE = take(1)
        P_XTM = take(8)
        P_RANK = take(1)
        use_x, use_g, use_y, use_h = {}, {}, {}, {}
        for t in range(NBLK + 2):
            for lag, of in ((0, use_x), (1, use_g), (2, use_y), (1, use_h)):
                if 0 <= t - lag < NBLK:
                    of[t - lag] = take(1)
        P_YSUM = take(8)
        n_fin1 = add_norm(Hp, "norm_final", Hp, Wp[22:25], 8, take(1))
        n_att2 = add_norm(Hp, "attn_norm", Bp, Wp[22:25], 8, take(1))
        P_IN2 = take(19)
        P_RG = take(4)
        n_rg = add_norm(Wp[2:4], "rg_norm", Bp[6:8], [Wp[4], Wp[5], Wp[19]], 2, take(1))
        P_S5T = take(2)
        P_S5 = take(24)
        P_GLU = take(2)
        n_s5 = add_norm(Wp[0:2], "s5_norm", Bp[4:6], [Wp[19], Wp[20], Wp[21]], 2, take(1))
        P_GK = take(2)
        P_KLT = take(2)
        P_KV = take(8)
        P_SC = take(4)
        P_O = []
        n_gla = []
        for h in range(4):
            P_O.append(take(1))
            n_gla.append(add_norm([Wp[4 + h] if h < 2 else Wp[17 + h]], "gla_norm", [Bp[h]], [Wp[8 + 13 * (h % 2)], None, Wp[9]], 1, take(1)))
        P_OUT2 = take(8)
        n_mlp = add_norm(Hp, "mlp_norm", Bp, Wp[22:25], 8, take(1))
        P_UP = take(2 * FF)
        P_DOWN = take(8)
        n_fin2 = add_norm(Hp, "final_norm", Hp, Wp[22:25], 8, take(1))

        for m in range(24):
            emptied[U_QKV + m] = (qkv_ready, m + 1)
        for u in range(NU):
            emptied[use_s[u]], emptied[use_t[u]], emptied[use_o[u]] = (scores_ready, u + 1), (pT_ready, u + 1), (heads_done, u + 1)
        emptied[P_ROUTE], emptied[P_RANK] = (gdiff_ready, 1), (rank_read, 1)
        for b in range(NBLK):
            emptied[use_x[b]], emptied[use_g[b]] = (xT_ready, b + 1), (up_ready, b + 1)
            emptied[use_h[b]], emptied[use_y[b]] = (hT_ready, b + 1), (y_ready, b + 1)
        for m in range(8):
            emptied[P_OUT + m] = (h_ready, m + 1)
            emptied[P_XTM + m] = (xtm_ready, m + 1)
            emptied[P_YSUM + m] = (ysum_ready, m + 1)
            emptied[P_OUT2 + m] = (h_ready, 8 + m + 1)
            emptied[P_DOWN + m] = (h_ready, 16 + m + 1)
            emptied[P_KV + m] = (state_ready, m + 1)
            emptied[P_S5 + 3 * m] = emptied[P_S5 + 3 * m + 1] = (s5in_ready, m + 1)
            emptied[P_S5 + 3 * m + 2] = (s5y_ready, m + 1)
        for m in range(19):
            emptied[P_IN2 + m] = (in2_ready, m + 1)
        for m in range(2):
            emptied[P_S5T + m] = (s5bT_ready, m + 1)
            emptied[P_GLU + m] = (s5s_ready, m + 1)
            emptied[P_GK + m] = (gk_biased, m + 1)
            emptied[P_KLT + m] = (klT_ready, m + 1)
        for m in range(4):
            emptied[P_RG + m] = (gates_ready, m + 1)
            emptied[P_SC + m] = (intra_ready, m + 1)
            emptied[P_O[m]] = (o_ready, m + 1)
        for j in range(FF):
            emptied[P_UP + 2 * j] = (conv1_ready, j + 1)
            emptied[P_UP + 2 * j + 1] = (ffact_ready, j + 1)
        unit_use = [U_QKV + m for m in range(16)] + [U_QKV + 19] * 4 + [U_QKV + 23] * 4 + [P_OUT + m for m in range(8)]
        unit_use += [P_IN2 + m for m in range(14)] + [P_IN2 + 18] * 4
        unit_use += [P_OUT2 + m for m in range(8)] + [P_UP + j for j in range(2 * FF)] + [P_DOWN + j // 3 for j in range(24)]

        Mp = [Wp[0], Wp[1], Wp[18], Wp[22]]

        PG_U, PG_RX, PG_RG, PG_Q, PG_K, PG_V, PG_G, PG_LOW = 0, 2, 4, 6, 8, 10, 14, 18

        def pair(p0):
            return W[:, p0:p0 + 2, :]

        block = ctx.enter_context(nc.Block())

        RV = {"L": (0, 160), "gd": (160, 32), "oh": (192, 32), "gm": (224, 8), "gw": (232, 8), "v4": (240, 32),
              "o1": (272, 32), "o2": (304, 32), "m1": (336, 8), "m2": (344, 8), "d1": (352, 8), "w1": (360, 8),
              "w2": (368, 8), "t4": (376, 32), "v4b": (408, 32), "c4": (440, 32), "tm": (472, 8), "gs": (480, 8),
              "t5": (488, 32), "nblk": (520, 16), "ends": (536, 16), "start": (552, 16), "fe": (568, NBLK), "fq": (600, NBLK),
              "s1": (640, 128), "s2": (768, 128), "member": (896, 128), "p1": (1024, 8), "p2": (1032, 8),
              "p1i": (1040, 8), "p2i": (1048, 8), "wait_i": (1056, NBLK), "page_i": (1088, NBLK), "ends_i": (1120, 16),
              "tot": (1152, 128), "base": (1280, 144), "cmp": (1424, 16 * NBLK), "ntok": (1936, 16)}
        routing = W[:, 8:10, :].rearrange("p a b -> p (a b)")

        def R(name):
            a, n = RV[name]
            return routing[:, a:a + n]

        XB = [Wp[10], Wp[11]]
        XT = [Wp[12], Bp[6]]
        SG = [Wp[0][:, 0:F_EXP], Wp[0][:, F_EXP:2 * F_EXP]]
        HA = [Wp[0][:, 2 * F_EXP:3 * F_EXP], Wp[0][:, 3 * F_EXP:4 * F_EXP]]
        HAT = [Wp[1][:, 0:F_EXP], Wp[1][:, F_EXP:2 * F_EXP]]
        YB = [Wp[2], Wp[3], Wp[4]]
        xw = W[:, 13:13 + XBUF * XPG, :].rearrange("p a b -> p (a b)")
        YG = [Wp[13 + i] for i in range(4)]

        @block.sync
        def _(sp):
            def experts():
                for e in range(N_EXP):
                    if e == 0:
                        sp.wait_ge(mm_done, done(P_RANK - 1))
                        sp.wait_ge(normed, n_ffn["index"] + 1)
                    if e >= XBUF:
                        if e == XBUF:
                            sp.wait_ge(dispatch_ready, 1)
                        sp.wait_ge(blocks_done, sp.value_load(R("ends_i")[0:1, e - XBUF:e - XBUF + 1].bitcast(i32), min_val=1, max_val=NBLK + 1))
                    sp.dma_start(xw[:, (e % XBUF) * XPG * S:(e % XBUF + 1) * XPG * S], w_moe[e]).then_inc(expert_dma[e % XBUF], 16)
                    if e >= 1:
                        sp.wait_ge(expert_dma[(e - 1) % XBUF], 16 * ((e - 1) // XBUF + 1))
                        sp.sem_inc(expert_loaded, 1)
                sp.wait_ge(expert_dma[(N_EXP - 1) % XBUF], 16 * ((N_EXP - 1) // XBUF + 1))
                sp.sem_inc(expert_loaded, 1)

            for i in range(4):
                sp.dma_start(hT[:, 2 * i:2 * i + 2, :], xT[:, 2 * i:2 * i + 2, :]).then_inc(x_loaded[i], 16)
                if i == 0:
                    sp.dma_start(cst[:], params).then_inc(cst_loaded, 16)
            for u, src in enumerate(units):
                if u == U_OUT:
                    sp.wait_ge(zero_set, 1)
                    for b in range(NBLK):
                        sp.dma_start(x_slots[b * P:(b + 1) * P, :], hT[:, 7, :]).then_inc(slots_zeroed, 16)
                if u == U_IN2 + RING:
                    experts()
                if u >= RING:
                    sp.wait_ge(mm_done, done(unit_use[u - RING]))
                sp.dma_start(ring[:, u % RING, :], src).then_inc(w_loaded[u % RING], 16)
            for t in range(NT):
                sp.wait_ge(final_ready, t + 1)
                sp.dma_start(out[:, t, :], hT[:, t, :]).then_inc(out_stored, 16)
            sp.wait_ge(out_stored, 16 * NT)

        STRIPS = [hT[:, 0:2, :].rearrange("p a b -> p (a b)")[:, 0:STRIP],
                  hT[:, 2:4, :].rearrange("p a b -> p (a b)")[:, 0:STRIP]]
        SB = [hT[:, 4, :], hT[:, 5, :], W[:, 24, :]]
        PT = [hT[:, 6, :], hT[:, 7, :]]

        @block.gpsimd
        def _(pool):
            pool.memset(epsc[:], EPS).then_inc(eps_set, 1)
            pool.wait_ge(normed, n_mix["index"] + 1)
            for h in range(NH):
                if h >= 2:
                    pool.wait_ge(scores_ready, NT * (h - 1))
                if h < 8:
                    pool.dma_start(STRIPS[h % 2], dil_strip[h]).then_inc(strip_loaded[h % 2], 16)
                else:
                    pool.dma_start(STRIPS[h % 2][:, 0:NF + NI], na_strip[h - 8]).then_inc(strip_loaded[h % 2], 16)
            pool.wait_ge(heads_done, NU)
            pool.dma_start(hT[:], xT).then_inc(x_again, 16)
            pool.wait_ge(slots_zeroed, 16 * NBLK)
            pool.wait_ge(dispatch_ready, 1)
            for tt in range(NT):
                pool.wait_ge(xtm_ready, tt + 1)
                for name in ("p1i", "p2i"):
                    pool.indirect_dma_start(x_slots, bass.IndirectOffsetOnAxis(ap=R(name)[:, tt:tt + 1].bitcast(u32), axis=0),
                                            Wp[tt], None, bounds_check=NBLK * P - 1, oob_is_err=True).then_inc(x_scattered, 16)
            pool.wait_ge(x_scattered, 16 * 2 * NT)
            for b in range(NBLK):
                if b >= 2:
                    pool.wait_ge(mm_done, done(use_x[b - 2]))
                pool.dma_start(XB[b % 2], x_slots[b * P:(b + 1) * P, :]).then_inc(block_loaded[b % 2], 16)
            for i in range(3):
                pool.wait_ge(y_stored[i], 16 * ((NBLK - i + 2) // 3))
            pool.wait_ge(mm_done, done(use_y[NBLK - 1]))
            for tt in range(NT):
                for r, name in enumerate(("p1i", "p2i")):
                    k = (2 * tt + r) % 4
                    if tt >= 2:
                        pool.wait_ge(ysum_ready, tt - 1)
                    pool.indirect_dma_start(YG[k], None, y_slots, bass.IndirectOffsetOnAxis(ap=R(name)[:, tt:tt + 1].bitcast(u32), axis=0),
                                            bounds_check=NBLK * P - 1, oob_is_err=True).then_inc(y_gathered[k], 16)
            pool.wait_ge(rg_ready, 1)
            pool.wait_ge(normed, n_rg["index"] + 1)
            pool.dma_start(bT[:, 0:4, :], s5_mats[:, 0:4, :]).then_inc(s5_loaded, 16)

        @block.tensor
        def _(pe):
            def slot(n):
                if n >= SLOTS:
                    pe.wait_ge(*emptied[n - SLOTS])
                return PS[n % SLOTS]

            def unit(u):
                pe.wait_ge(w_loaded[u % RING], 16 * (u // RING + 1))
                return ring[:, u % RING, :]

            def column_tile(u, n, rhs, kt=NT):
                ps, w = slot(n), unit(u)
                for half in range(2):
                    for k in range(kt):
                        mm = pe.matmul(ps[:, half * HALF:(half + 1) * HALF], w[:, k * P:(k + 1) * P],
                                       rhs[k][:, half * HALF:(half + 1) * HALF], start=(k == 0), stop=(k == kt - 1))
                        if half == 1 and k == kt - 1:
                            mm.then_inc(mm_done, 1)

            def token_major(u0, n0, lhs):
                ws = [unit(u0 + j) for j in range(4)]
                del ws
                s0 = u0 % RING
                for tt in range(NT):
                    if tt % 2 == 0:
                        ps = slot(n0 + tt // 2)
                    for k in range(NT):
                        mm = pe.matmul(ps[:, (tt % 2) * HALF:(tt % 2 + 1) * HALF], lhs[k][:, tt * P:(tt + 1) * P],
                                       ring[:, s0:s0 + 4, k * P:(k + 1) * P], start=(k == 0), stop=(k == NT - 1))
                    if tt % 2 == 1:
                        mm.then_inc(mm_done, 1)

            def norm(c):
                ps = slot(c["use"])
                for t in range(c["tiles"]):
                    pe.wait_ge(sq_ready, c["sq0"] + t + 1)
                    for half in range(2):
                        mm = pe.matmul(ps[:, half * HALF:(half + 1) * HALF], ones,
                                       c["scratch"][t % 2][:, half * HALF:(half + 1) * HALF],
                                       start=(t == 0), stop=(t == c["tiles"] - 1))
                    mm.then_inc(sq_used, 1)

            pe.wait_ge(cst_loaded, 16)
            norm(n_mix)
            pe.wait_ge(normed, n_mix["index"] + 1)
            for m in range(16):
                column_tile(U_IN + m, U_QKV + m, Bp)
            for g in range(2):
                token_major(U_IN + 16 + 4 * g, U_QKV + 16 + 4 * g, Bp)

            def scores(u):
                h, i = u // NT, u % NT
                k0, k1 = key_tiles(h, i)
                r0 = (h % 2) * DH
                ps = slot(use_s[u])
                q, k = Wp[h // 2], Wp[8 + h // 2]
                for c0 in range(k0 * P, k1 * P, HALF):
                    c1 = min(c0 + HALF, k1 * P)
                    mm = pe.matmul(ps[:, c0 - k0 * P:c1 - k0 * P], q[r0:r0 + DH, i * P:(i + 1) * P],
                                   k[r0:r0 + DH, c0:c1], start=True, stop=True)
                mm.then_inc(mm_done, 1)

            def turn(u):
                k0, k1 = key_tiles(u // NT, u % NT)
                pe.wait_ge(probs_ready, u + 1)
                ps = slot(use_t[u])
                for j in range(k1 - k0):
                    mm = pe.transpose(ps[:, j * P:(j + 1) * P], SB[u % 3][:, j * P:(j + 1) * P], ident)
                mm.then_inc(mm_done, 1)

            def mix(u):
                h = u // NT
                k0, k1 = key_tiles(h, u % NT)
                pe.wait_ge(pT_ready, u + 1)
                ps = slot(use_o[u])
                for j in range(k1 - k0):
                    mm = pe.matmul(ps[0:DH, 0:P], Wp[16 + k0 + j][:, h * DH:(h + 1) * DH],
                                   PT[u % 2][:, j * P:(j + 1) * P], start=(j == 0), stop=(j == k1 - k0 - 1))
                mm.then_inc(mm_done, 1)

            pe.wait_ge(qkv_ready, 24)
            for t in range(NU + LAG_O):
                if t < NU:
                    scores(t)
                if 0 <= t - LAG_T < NU:
                    turn(t - LAG_T)
                if 0 <= t - LAG_O < NU:
                    mix(t - LAG_O)
            norm(n_dil)
            norm(n_na)
            pe.wait_ge(normed, n_na["index"] + 1)
            for m in range(8):
                column_tile(U_OUT + m, P_OUT + m, Bp)
            norm(n_ffn)
            pe.wait_ge(normed, n_ffn["index"] + 1)
            ps = slot(P_ROUTE)
            for tt in range(NT):
                for k in range(NT):
                    mm = pe.matmul(ps[:, tt * 20:(tt + 1) * 20], Bp[k][:, tt * P:(tt + 1) * P],
                                   mat("route", k * 20, 20), start=(k == 0), stop=(k == NT - 1))
            mm.then_inc(mm_done, 1)
            for tt in range(NT):
                ps = slot(P_XTM + tt)
                for k in range(NT):
                    mm = pe.transpose(ps[:, k * P:(k + 1) * P], Bp[k][:, tt * P:(tt + 1) * P], ident)
                mm.then_inc(mm_done, 1)
            pe.wait_ge(member_ready, 1)
            ps = slot(P_RANK)
            pe.matmul(ps[:, 0:P], mat("before"), R("member"), start=True, stop=True)
            pe.matmul(ps[:, HALF:HALF + P], ones, R("member"), start=True, stop=True).then_inc(mm_done, 1)

            pe.wait_ge(dispatch_ready, 1)
            pages = {}

            def block_x(b):
                pe.wait_ge(block_loaded[b % 2], 16 * (b // 2 + 1))
                ps = slot(use_x[b])
                for k in range(NT):
                    mm = pe.transpose(ps[:, k * P:(k + 1) * P], XB[b % 2][:, k * P:(k + 1) * P], ident)
                mm.then_inc(mm_done, 1)

            def block_g(b):
                pages[b] = pe.value_load(R("page_i")[0:1, b:b + 1].bitcast(i32), min_val=0, max_val=2 * XPG * S)
                pe.wait_ge(expert_loaded, pe.value_load(R("wait_i")[0:1, b:b + 1].bitcast(i32), min_val=1, max_val=N_EXP))
                pe.wait_ge(xT_ready, b + 1)
                ps = slot(use_g[b])
                for k in range(NT):
                    mm = pe.matmul(ps[:, 0:HALF], XT[b % 2][:, k * P:(k + 1) * P], xw[:, bass.ds(pages[b] + k * HALF, HALF)],
                                   start=(k == 0), stop=(k == NT - 1))
                mm.then_inc(mm_done, 1)

            def block_h(b):
                pe.wait_ge(up_ready, b + 1)
                ps = slot(use_h[b])
                for f in range(2):
                    mm = pe.transpose(ps[:, f * P:(f + 1) * P], HA[b % 2][:, f * P:(f + 1) * P], ident)
                mm.then_inc(mm_done, 1)

            def block_y(b):
                pe.wait_ge(hT_ready, b + 1)
                ps = slot(use_y[b])
                for half in range(2):
                    for f in range(2):
                        mm = pe.matmul(ps[:, half * HALF:(half + 1) * HALF], HAT[b % 2][:, f * P:(f + 1) * P],
                                       xw[:, bass.ds(pages[b] + 4 * S + f * S + half * HALF, HALF)], start=(f == 0), stop=(f == 1))
                mm.then_inc(mm_done, 1)

            for t in range(NBLK + 2):
                for lag, stage in ((0, block_x), (1, block_g), (2, block_y), (1, block_h)):
                    if 0 <= t - lag < NBLK:
                        stage(t - lag)
            for tt in range(NT):
                pe.wait_ge(ysum_added, tt + 1)
                ps = slot(P_YSUM + tt)
                for k in range(NT):
                    mm = pe.transpose(ps[:, k * P:(k + 1) * P], YG[(2 * tt + 1) % 4][:, k * P:(k + 1) * P], ident)
                mm.then_inc(mm_done, 1)
            norm(n_fin1)
            norm(n_att2)
            pe.wait_ge(normed, n_att2["index"] + 1)
            for m in range(14):
                column_tile(U_IN2 + m, P_IN2 + m, Bp)
            ps = slot(P_IN2 + 14)
            for half in range(2):
                for k in range(NT):
                    mm = pe.matmul(ps[0:16, half * HALF:(half + 1) * HALF], mat("low", k * 16, 16),
                                   Bp[k][:, half * HALF:(half + 1) * HALF], start=(k == 0), stop=(k == NT - 1))
            mm.then_inc(mm_done, 1)
            for j in range(4):
                unit(U_IN2 + 14 + j)
            for tt in range(NT):
                if tt % 2 == 0:
                    ps = slot(P_IN2 + 15 + tt // 2)
                for j in range(4):
                    s0 = (U_IN2 + 14 + j) % RING
                    c0 = (tt % 2) * HALF + j * P
                    for k in range(NT):
                        mm = pe.matmul(ps[:, c0:c0 + P], Bp[k][:, tt * P:(tt + 1) * P], ring[:, s0, k * P:(k + 1) * P],
                                       start=(k == 0), stop=(k == NT - 1))
                if tt % 2 == 1:
                    mm.then_inc(mm_done, 1)

            pe.wait_ge(conv_ready, 2)
            for j in range(4):
                ps = slot(P_RG + j)
                for half in range(2):
                    mm = pe.matmul(ps[:, half * HALF:(half + 1) * HALF], mat("rg", j * P),
                                   Wp[19 + j % 2][:, half * HALF:(half + 1) * HALF], start=True, stop=True)
                mm.then_inc(mm_done, 1)
            norm(n_rg)

            pe.wait_ge(s5b_ready, 1)
            for c in range(2):
                ps = slot(P_S5T + c)
                for j in range(8):
                    mm = pe.transpose(ps[:, j * P:(j + 1) * P], Bp[c][:, j * P:(j + 1) * P], ident)
                mm.then_inc(mm_done, 1)
            pe.wait_ge(s5bT_ready, 2)
            for j in range(8):
                for c in range(2):
                    ps = slot(P_S5 + 3 * j + c)
                    for half in range(2):
                        mm = pe.matmul(ps[:, half * HALF:(half + 1) * HALF], Bp[4 + c][:, j * P:(j + 1) * P],
                                       Wp[PG_U + j // 4][:, half * HALF:(half + 1) * HALF], start=True, stop=True)
                    mm.then_inc(mm_done, 1)
                pe.wait_ge(s5x_ready, j + 1)
                ps = slot(P_S5 + 3 * j + 2)
                for half in range(2):
                    for c in range(2):
                        mm = pe.matmul(ps[:, half * HALF:(half + 1) * HALF], Bp[2 + c][:, j * P:(j + 1) * P],
                                       Wp[4 + c][:, half * HALF:(half + 1) * HALF], start=(c == 0), stop=(c == 1))
                mm.then_inc(mm_done, 1)
            pe.wait_ge(s5g_ready, 2)
            for m in range(2):
                ps = slot(P_GLU + m)
                for half in range(2):
                    for k in range(2):
                        mm = pe.matmul(ps[:, half * HALF:(half + 1) * HALF], mat("glu", k * 256 + m * P),
                                       Wp[k][:, half * HALF:(half + 1) * HALF], start=(k == 0), stop=(k == 1))
                mm.then_inc(mm_done, 1)
            norm(n_s5)

            for m in range(2):
                ps = slot(P_GK + m)
                for half in range(2):
                    mm = pe.matmul(ps[:, half * HALF:(half + 1) * HALF], cst[0:16, MCOLS["gkup"] + m * P:MCOLS["gkup"] + (m + 1) * P],
                                   Wp[PG_LOW][0:16, half * HALF:(half + 1) * HALF], start=True, stop=True)
                mm.then_inc(mm_done, 1)
            pe.wait_ge(gprods, 1)
            for m in range(2):
                ps = slot(P_KLT + m)
                for tt in range(NT):
                    mm = pe.transpose(ps[:, tt * P:(tt + 1) * P], Wp[PG_K + m][:, tt * P:(tt + 1) * P], ident)
                mm.then_inc(mm_done, 1)
            vv = W[:, PG_V:PG_V + 4, :].rearrange("p a (b c) -> p (a b) c", c=HALF)
            for m in range(2):
                pe.wait_ge(klT_ready, m + 1)
                for q4 in range(4):
                    ps = slot(P_KV + 4 * m + q4)
                    for j in range(4):
                        n = 4 * q4 + j
                        r0, tt = (n % 2) * CH, n // 2
                        c0 = (j % 2) * HALF + (j // 2) * 256
                        mm = pe.matmul(ps[:, c0:c0 + 256], Wp[21 + m][r0:r0 + CH, tt * P:(tt + 1) * P],
                                       vv[r0:r0 + CH, tt, m * 256:(m + 1) * 256], start=True, stop=True)
                    mm.then_inc(mm_done, 1)
            for h in range(4):
                m, r0 = h // 2, (h % 2) * DH
                ps = slot(P_SC + h)
                for tt in range(NT):
                    mm = pe.matmul(ps[:, tt * P:(tt + 1) * P], Wp[19 + m][r0:r0 + DH, tt * P:(tt + 1) * P],
                                   Wp[4 + m][r0:r0 + DH, tt * P:(tt + 1) * P], start=True, stop=True)
                mm.then_inc(mm_done, 1)
            states = [pair(23).rearrange("p a (b c) -> p (a b) c", c=P), pair(2).rearrange("p a (b c) -> p (a b) c", c=P)]
            for h in range(4):
                m, r0 = h // 2, (h % 2) * DH
                pe.wait_ge(intra_ready, h + 1)
                pe.wait_ge(state_ready, 8)
                ps = slot(P_O[h])
                for tt in range(NT):
                    o = ps[:, tt * P:(tt + 1) * P]
                    mm = pe.matmul(o, vv[:, tt, h * P:(h + 1) * P], Mp[h][:, tt * P:(tt + 1) * P], start=True, stop=False)
                    for c in range(2):
                        n = 2 * tt + c
                        if n == 0:
                            continue
                        mm = pe.matmul(ps[:, n * CH:(n + 1) * CH], states[m][r0:r0 + DH, n, :],
                                       Wp[PG_Q + m][r0:r0 + DH, n * CH:(n + 1) * CH], start=False, stop=(c == 1))
                mm.then_inc(mm_done, 1)
                norm(n_gla[h])
            pe.wait_ge(gla_ready, 4)
            for m in range(8):
                column_tile(U_OUT2 + m, P_OUT2 + m, Bp)
            norm(n_mlp)
            pe.wait_ge(normed, n_mlp["index"] + 1)
            for j in range(2 * FF):
                column_tile(U_UP + j, P_UP + j, Bp)
            pe.wait_ge(ffact_ready, FF)
            for m in range(8):
                ps = slot(P_DOWN + m)
                for half in range(2):
                    for c in range(3):
                        if half == 0:
                            unit(U_DOWN + 3 * m + c)
                        w = ring[:, (U_DOWN + 3 * m + c) % RING, :]
                        for k in range(8 if c < 2 else 6):
                            kk = 8 * c + k
                            mm = pe.matmul(ps[:, half * HALF:(half + 1) * HALF], w[:, k * P:(k + 1) * P],
                                           Wp[kk][:, half * HALF:(half + 1) * HALF], start=(kk == 0), stop=(kk == FF - 1))
                mm.then_inc(mm_done, 1)
            norm(n_fin2)


        @block.scalar
        def _(act):
            links = [0]

            def link(ins):
                links[0] += 1
                ins.then_inc(act_link, 1)
                act.wait_ge(act_link, links[0])

            def norm(c, gate=None):
                for t in range(c["tiles"]):
                    if gate is not None:
                        gate(t)
                    if c["sq0"] + t >= 2:
                        act.wait_ge(sq_used, c["sq0"] + t - 1)
                    act.activation(c["scratch"][t % 2], c["src"][t], ACT.Square).then_inc(sq_ready, 1)
                act.wait_ge(sq_used, c["sq0"] + c["tiles"])
                if c["index"]:
                    act.wait_ge(normed, c["index"])
                act.activation(c["scratch"][2], PS[c["use"] % SLOTS][:, :], ACT.Sqrt, bias=epsc[:],
                               scale=1.0 / (P * c["tiles"])).then_inc(std_ready, 1)

            act.wait_ge(eps_set, 1)

            def x_gate(t):
                if t % 2 == 0:
                    act.wait_ge(x_loaded[t // 2], 16)
            norm(n_mix, x_gate)
            act.wait_ge(normed, 1)
            for m in range(24):
                n = U_QKV + m
                act.wait_ge(mm_done, done(n))
                ps = PS[n % SLOTS]
                if m < 16:
                    dst, src = Wp[m], ps[:, :]
                else:
                    g, t2 = (m - 16) // 4, (m - 16) % 4
                    dst = W[:, 16 + 2 * t2:18 + 2 * t2, g * HALF:(g + 1) * HALF]
                    src = ps[:, :].rearrange("p (a b) -> p a b", a=2)
                act.activation(dst, src, ACT.Copy, scale=DH ** -0.5 if m < 8 else 1.0).then_inc(qkv_ready, 1)

            def expo(u):
                k0, k1 = key_tiles(u // NT, u % NT)
                act.wait_ge(scores_ready, u + 1)
                s = SB[u % 3][:, 0:(k1 - k0) * P]
                act.activation(s, s, ACT.Exp, bias=negm[:, u % 4:u % 4 + 1], scale=-1.0,
                               accum_out=den[:, u % 4:u % 4 + 1]).then_inc(exp_done, 1)

            def copy_pT(u):
                k0, k1 = key_tiles(u // NT, u % NT)
                n = use_t[u]
                act.wait_ge(mm_done, done(n))
                if u == 1:
                    act.wait_ge(slots_zeroed, 16 * NBLK)
                if u >= 2:
                    act.wait_ge(mm_done, done(use_o[u - 2]))
                act.activation(PT[u % 2][:, 0:(k1 - k0) * P], PS[n % SLOTS][:, 0:(k1 - k0) * P], ACT.Copy).then_inc(pT_ready, 1)

            for t in range(NU + LAG_T):
                if t < NU:
                    expo(t)
                if t >= LAG_T:
                    copy_pT(t - LAG_T)

            def heads_gate(t):
                act.wait_ge(heads_done, NU)
            norm(n_dil, heads_gate)
            norm(n_na, heads_gate)

            def h_gate(t):
                act.wait_ge(h_ready, t + 1)
            norm(n_ffn, h_gate)
            act.wait_ge(gdiff_ready, 1)
            act.activation(R("gd"), R("gd"), ACT.Exp).then_inc(gexp_done, 1)
            act.wait_ge(tdiff_ready, 1)
            act.activation(R("d1"), R("d1"), ACT.Exp).then_inc(texp_done, 1)
            for tt in range(NT):
                act.wait_ge(mm_done, done(P_XTM + tt))
                act.activation(Wp[tt], PS[(P_XTM + tt) % SLOTS][:, :], ACT.Copy).then_inc(xtm_ready, 1)
            act.wait_ge(x_scattered, 16 * 2 * NT)

            def block_xT(b):
                act.wait_ge(mm_done, done(use_x[b]))
                if b >= 2:
                    act.wait_ge(mm_done, done(use_g[b - 2]))
                act.activation(XT[b % 2], PS[use_x[b] % SLOTS][:, :], ACT.Copy).then_inc(xT_ready, 1)

            def block_silu(b):
                act.wait_ge(mm_done, done(use_g[b]))
                if b >= 2:
                    act.wait_ge(up_ready, b - 1)
                act.activation(SG[b % 2], PS[use_g[b] % SLOTS][:, 0:F_EXP], ACT.Silu).then_inc(silu_ready, 1)

            def block_store(b):
                act.wait_ge(y_ready, b + 1)
                act.dma_start(y_slots[b * P:(b + 1) * P, :], YB[b % 3]).then_inc(y_stored[b % 3], 16)

            for t in range(NBLK + 3):
                for lag, stage in ((0, block_xT), (1, block_silu), (3, block_store)):
                    if 0 <= t - lag < NBLK:
                        stage(t - lag)

            def moe_gate(t):
                act.wait_ge(ysum_ready, NT)
            norm(n_fin1, moe_gate)

            def fin1_gate(t):
                act.wait_ge(normed, n_fin1["index"] + 1)
            norm(n_att2, fin1_gate)
            act.wait_ge(normed, n_att2["index"] + 1)
            dsts = [Wp[PG_RX], Wp[PG_RX + 1], Wp[PG_RG], Wp[PG_RG + 1], Wp[PG_U], Wp[PG_U + 1], Wp[PG_Q], Wp[PG_Q + 1],
                    Wp[PG_K], Wp[PG_K + 1]] + [Wp[PG_G + j] for j in range(4)]
            for m in range(19):
                n = P_IN2 + m
                act.wait_ge(mm_done, done(n))
                ps = PS[n % SLOTS]
                if m < 14:
                    dst, src = dsts[m], ps[:, :]
                elif m == 14:
                    dst, src = Wp[PG_LOW][0:16, :], ps[0:16, :]
                else:
                    dst, src = Wp[PG_V + m - 15], ps[:, :]
                act.activation(dst, src, ACT.Copy, scale=DH ** -0.5 if m in (6, 7) else 1.0).then_inc(in2_ready, 1)
            for j in range(4):
                n = P_RG + j
                act.wait_ge(mm_done, done(n))
                act.activation(Wp[21 + j], PS[n % SLOTS][:, :], ACT.Sigmoid,
                               bias=par("rg_ba" if j < 2 else "rg_bx", j % 2)).then_inc(gates_ready, 1)
            act.wait_ge(gates_ready, 4)
            for c in range(2):
                act.activation(Wp[21 + c], Wp[21 + c], ACT.Tanh, scale=sp4[:, c:c + 1]).then_inc(tanh_ready, 1)
            act.wait_ge(tanh_ready, 2)
            for c in range(2):
                act.activation(Bp[c], Wp[21 + c], ACT.Sqrt, scale=4.0).then_inc(root_ready, 1)
            for c in range(2):
                act.activation(Wp[PG_RG + c], Wp[PG_RG + c], ACT.Gelu_apprx_tanh).then_inc(ggate_ready, 1)

            def rg_gate(t):
                act.wait_ge(rg_ready, 1)
            norm(n_rg, rg_gate)
            for c in range(2):
                n = P_S5T + c
                act.wait_ge(mm_done, done(n))
                act.activation(Bp[4 + c], PS[n % SLOTS][:, :], ACT.Copy).then_inc(s5bT_ready, 1)
            act.wait_ge(s5y_ready, 8)
            for c in range(2):
                act.activation(Wp[c], Wp[24 - c], ACT.Gelu_apprx_tanh).then_inc(s5g_ready, 1)
            for c in range(2):
                n = P_GLU + c
                act.wait_ge(mm_done, done(n))
                act.activation(Wp[22 - c], PS[n % SLOTS][:, :], ACT.Sigmoid, bias=par("b_glu", c)).then_inc(s5s_ready, 1)

            def s5_gate(t):
                act.wait_ge(s5_ready, 2)
            norm(n_s5, s5_gate)
            act.wait_ge(gk_abs, 2)
            link(act.activation(pair(2), pair(2), ACT.Exp, scale=-1.0))
            act.activation(pair(2), pair(2), ACT.Ln, bias=1.0).then_inc(gk_ln, 1)
            act.wait_ge(bc_ready, 1)
            for k in range(4):
                if k == 3:
                    act.wait_ge(gprods, 1)
                elif k:
                    act.wait_ge(gexps_used, k)
                act.activation(pair(2), pair(2) if k < 3 else pair(0), ACT.Exp).then_inc(gexps, 1)
            for m in range(2):
                last = act.activation(decay[:, m, :], Wp[m].rearrange("p (n c) -> p n c", c=CH)[:, :, CH - 1], ACT.Exp)
            last.then_inc(decay_ready, 1)
            for m in range(2):
                n = P_KLT + m
                act.wait_ge(mm_done, done(n))
                act.activation(Wp[21 + m], PS[n % SLOTS][:, :], ACT.Copy).then_inc(klT_ready, 1)
            for h in range(4):
                act.activation(Wp[PG_G + h], Wp[PG_G + h], ACT.Silu).then_inc(gsilu, 1)
            for h in range(4):
                n = P_O[h]
                act.wait_ge(mm_done, done(n))
                if h >= 2:
                    act.wait_ge(mm_done, done(P_SC + 3))
                act.activation(n_gla[h]["src"][0], PS[n % SLOTS][:, :], ACT.Copy).then_inc(o_ready, 1)
                act.wait_ge(o_ready, h + 1)
                norm(n_gla[h])

            def out2_gate(t):
                act.wait_ge(h_ready, 8 + t + 1)
            norm(n_mlp, out2_gate)
            for j in range(FF):
                n = P_UP + 2 * j
                act.wait_ge(mm_done, done(n))
                if j >= 3:
                    act.wait_ge(ffact_ready, j - 2)
                act.activation(Wp[22 + j % 3], PS[n % SLOTS][:, :], ACT.Identity, bias=par("ff_cb", j),
                               scale=par("ff_w", 2 * FF + j)).then_inc(conv0_ready, 1)
                act.wait_ge(conv1_ready, j + 1)
                act.activation(Wp[22 + j % 3], Wp[22 + j % 3], ACT.Gelu_apprx_tanh).then_inc(gelu_ready, 1)

            def down_gate(t):
                act.wait_ge(h_ready, 16 + t + 1)
            norm(n_fin2, down_gate)

        @block.vector
        def _(dve):
            links = [0]

            def link(ins):
                links[0] += 1
                ins.then_inc(dve_link, 1)
                dve.wait_ge(dve_link, links[0])

            def norm(c, last=None):
                r = c["scratch"][2]
                dve.wait_ge(std_ready, c["index"] + 1)
                link(dve.reciprocal(r, r))
                for t in range(c["tiles"]):
                    g = par(c["gain"], t + (4 if c is n_na else 0))
                    ins = dve.scalar_tensor_tensor(out=c["dst"][t], in0=c["src"][t], scalar=g, in1=r,
                                                   op0=ALU.mult, op1=ALU.mult)
                    if last is not None:
                        ins.then_inc(last, 1)
                if last is None:
                    ins.then_inc(normed, 1)
                    dve.wait_ge(normed, c["index"] + 1)

            norm(n_mix)

            dve.memset(hT[:, 7, :], 0.0).then_inc(zero_set, 1)
            dve.wait_ge(cst_loaded, 16)
            free = list(range(40))

            def tmp():
                return small[:, free.pop(0), :]

            def ts(out, a, s1, s2, op0, op1=ALU.bypass):
                if s2 is None:
                    link(dve.tensor_scalar(out, a, s1, None, op0))
                else:
                    link(dve.tensor_scalar(out, a, s1, s2, op0, op1))

            def tt(out, a, b, op):
                link(dve.tensor_tensor(out, a, b, op))

            def tt_(out, a, b, op, signal=None):
                ins = dve.tensor_tensor(out, a, b, op)
                if signal is None:
                    link(ins)
                else:
                    ins.then_inc(signal, 1)
                    dve.wait_ge(signal, 1)

            def stt(out, a, s, b, op0, op1):
                link(dve.scalar_tensor_tensor(out=out, in0=a, scalar=s, in1=b, op0=op0, op1=op1))

            MAGIC = 12582912.0

            def exp_parts(x, w):
                k, r, p, t, ki = (tmp()[:, 0:w] for _ in range(5))
                ts(k, x, 1.4426950408889634, 1000.0, ALU.mult, ALU.min)
                ts(k, k, -1000.0, MAGIC, ALU.max, ALU.add)
                ts(k, k, MAGIC, None, ALU.subtract)
                stt(r, k, -0.693145751953125, x, ALU.mult, ALU.add)
                stt(r, k, -1.42860682030941723e-6, r, ALU.mult, ALU.add)
                ts(r, r, 0.5, -0.5, ALU.min, ALU.max)
                ts(p, r, 1.0 / 40320, 1.0 / 5040, ALU.mult, ALU.add)
                for c in (1.0 / 720, 1.0 / 120, 1.0 / 24, 1.0 / 6, 0.5, 1.0):
                    tt(p, p, r, ALU.mult)
                    ts(p, p, c, None, ALU.add)
                tt(p, p, r, ALU.mult)
                ts(t, k, 127.0, 0.0, ALU.add, ALU.max)
                ts(t, t, 254.0, 8388608.0, ALU.min, ALU.mult)
                link(dve.tensor_copy(ki.bitcast(i32), t))
                tt(p, p, ki, ALU.mult)
                return ki, p

            def keep(n):
                del free[:]
                free.extend(range(n, 40))

            lre, lim = par("lam_re", 0, 8), par("lam_im", 0, 8)
            dt, a, b = tmp(), tmp(), tmp()
            two_k, part = exp_parts(par("log_dt", 0, 8), 8)
            tt(dt, two_k, part, ALU.add)
            tt(a, lre, dt, ALU.mult)
            tt(b, lim, dt, ALU.mult)
            keep(3)
            em1, hs, hc = tmp(), tmp(), tmp()
            two_k, part = exp_parts(a, 8)
            tt(s5p[:, 0, :], two_k, part, ALU.add)
            ts(em1, two_k, -1.0, None, ALU.add)
            tt(em1, em1, part, ALU.add)
            keep(6)
            k, r, x2, s, c = tmp(), tmp(), tmp(), tmp(), tmp()
            ts(k, b, 0.15915494309189535, MAGIC, ALU.mult, ALU.add)
            ts(k, k, MAGIC, None, ALU.subtract)
            stt(r, k, -6.28125, b, ALU.mult, ALU.add)
            stt(r, k, -0.0019350051879882812, r, ALU.mult, ALU.add)
            stt(r, k, -3.019916050561733e-07, r, ALU.mult, ALU.add)
            ts(r, r, 0.5, None, ALU.mult)
            tt(x2, r, r, ALU.mult)

            def series(out, first, coefs):
                ts(out, x2, first, coefs[0], ALU.mult, ALU.add)
                for q in coefs[1:]:
                    tt(out, out, x2, ALU.mult)
                    ts(out, out, q, None, ALU.add)
            series(s, 1.0 / 6227020800, (-1.0 / 39916800, 1.0 / 362880, -1.0 / 5040, 1.0 / 120, -1.0 / 6, 1.0))
            tt(hs, s, r, ALU.mult)
            series(hc, 1.0 / 479001600, (-1.0 / 3628800, 1.0 / 40320, -1.0 / 720, 1.0 / 24, -0.5, 1.0))
            cm1, cosb, sinb, ere, eim, t1, l2, fre, fim = (tmp() for _ in range(9))
            tt(cm1, hs, hs, ALU.mult)
            ts(cm1, cm1, -2.0, None, ALU.mult)
            ts(s5p[:, 1, :], cm1, 1.0, None, ALU.add)
            tt(t1, hs, hc, ALU.mult)
            ts(s5p[:, 2, :], t1, 2.0, None, ALU.mult)
            tt(ere, em1, s5p[:, 1, :], ALU.mult)
            tt(ere, ere, cm1, ALU.add)
            tt(eim, s5p[:, 0, :], s5p[:, 2, :], ALU.mult)
            tt(l2, lre, lre, ALU.mult)
            tt(t1, lim, lim, ALU.mult)
            tt(l2, l2, t1, ALU.add)
            link(dve.reciprocal(l2, l2))
            tt(fre, ere, lre, ALU.mult)
            tt(t1, eim, lim, ALU.mult)
            tt(fre, fre, t1, ALU.add)
            tt(s5p[:, 3, :], fre, l2, ALU.mult)
            tt(fim, eim, lre, ALU.mult)
            tt(t1, ere, lim, ALU.mult)
            tt(fim, fim, t1, ALU.subtract)
            tt(s5p[:, 4, :], fim, l2, ALU.mult)
            ts(s5p[:, 25, :], s5p[:, 4, :], -1.0, None, ALU.mult)
            tt(s5p[:, 5, :], s5p[:, 1, :], s5p[:, 1, :], ALU.bypass) if False else link(dve.tensor_copy(s5p[:, 5, :], s5p[:, 1, :]))
            link(dve.tensor_copy(s5p[:, 6, :], s5p[:, 2, :]))
            for k2 in range(1, 10):
                c0, s0 = s5p[:, 3 + 2 * k2, :], s5p[:, 4 + 2 * k2, :]
                tt(t1, s0, s0, ALU.mult)
                ts(s5p[:, 5 + 2 * k2, :], t1, -2.0, 1.0, ALU.mult, ALU.add)
                tt(t1, c0, s0, ALU.mult)
                ts(s5p[:, 6 + 2 * k2, :], t1, 2.0, None, ALU.mult)
            keep(0)
            lam = par("rg_lam", 0, 2)
            na_, mx_, z, z2 = (tmp()[:, 0:2] for _ in range(4))
            ts(na_, lam, -1.0, None, ALU.mult)
            tt(na_, na_, lam, ALU.min)
            ts(mx_, lam, -1.0, 0.0, ALU.mult, ALU.max)
            two_k, part = exp_parts(na_, 2)
            tt(z, two_k, part, ALU.add)
            ts(z2, z, 2.0, None, ALU.add)
            link(dve.reciprocal(z2, z2))
            tt(z, z, z2, ALU.mult)
            tt(z2, z, z, ALU.mult)
            lg = tmp()[:, 0:2]
            ts(lg, z2, 2.0 / 17, 2.0 / 15, ALU.mult, ALU.add)
            for q in (13, 11, 9, 7, 5, 3, 1):
                tt(lg, lg, z2, ALU.mult)
                ts(lg, lg, 2.0 / q, None, ALU.add)
            tt(lg, lg, z, ALU.mult)
            tt(lg, lg, mx_, ALU.add)
            ts(sp4[:], lg, 4.0, None, ALU.mult)

            def biased(u):
                h, i = u // NT, u % NT
                k0, k1 = key_tiles(h, i)
                nk = (k1 - k0) * P
                n = use_s[u]
                if i == 0:
                    dve.wait_ge(strip_loaded[h % 2], 16 * (h // 2 + 1))
                dve.wait_ge(mm_done, done(n))
                if u >= 3:
                    dve.wait_ge(mm_done, done(use_t[u - 3]))
                st = STRIPS[h % 2]
                if h < 8:
                    bias = st[:, 896 - P * i:896 - P * i + nk]
                elif 2 <= i <= 5:
                    bias = st[:, NF:NF + NI]
                else:
                    bias = st[:, (3 + k0 - i) * P:(3 + k0 - i) * P + nk]
                dve.tensor_tensor_reduce(out=SB[u % 3][:, 0:nk], in0=PS[n % SLOTS][:, 0:nk], in1=bias, scale=-1.0,
                                         scalar=3.0e38, op0=ALU.add, op1=ALU.min,
                                         accum_out=negm[:, u % 4:u % 4 + 1]).then_inc(scores_ready, 1)

            def scaled(u):
                k0, k1 = key_tiles(u // NT, u % NT)
                dve.wait_ge(exp_done, u + 1)
                rd = rden[:, u % 4:u % 4 + 1]
                link(dve.reciprocal(rd, den[:, u % 4:u % 4 + 1]))
                s = SB[u % 3][:, 0:(k1 - k0) * P]
                dve.tensor_scalar(s, s, rd, None, ALU.mult).then_inc(probs_ready, 1)

            def head_out(u):
                h, i = u // NT, u % NT
                n = use_o[u]
                r0 = (h % 2) * DH
                dve.wait_ge(mm_done, done(n))
                dve.tensor_copy(Bp[h // 2][r0:r0 + DH, i * P:(i + 1) * P], PS[n % SLOTS][0:DH, 0:P]).then_inc(heads_done, 1)

            for t in range(NU + LAG_O + 1):
                if t < NU:
                    biased(t)
                if 0 <= t - 1 < NU:
                    scaled(t - 1)
                if 0 <= t - LAG_O - 1 < NU:
                    head_out(t - LAG_O - 1)
            norm(n_dil)
            norm(n_na)

            def add_to_h(n0, base):
                for m in range(8):
                    dve.wait_ge(mm_done, done(n0 + m))
                    dve.tensor_tensor(Hp[m], PS[(n0 + m) % SLOTS][:, :], Hp[m], ALU.add).then_inc(h_ready, 1)

            dve.wait_ge(x_again, 16)
            add_to_h(P_OUT, 0)
            norm(n_ffn)

            def v3(name, n):
                return R(name).rearrange("p (t n) -> p t n", n=n)

            def bc(name, n):
                return R(name).unsqueeze(2).to_broadcast([P, NT, n])

            tie = mat("tie", 0, 4).unsqueeze(1).to_broadcast([P, NT, 4])
            dve.wait_ge(mm_done, done(P_ROUTE))
            link(dve.tensor_tensor(v3("L", 20), PS[P_ROUTE % SLOTS][:, 0:160].rearrange("p (t n) -> p t n", n=20),
                                   mat("bias20", 0, 20).unsqueeze(1).to_broadcast([P, NT, 20]), ALU.add))
            g4 = v3("L", 20)[:, :, 0:4]
            link(dve.tensor_reduce(R("gm"), g4, AX.X, ALU.max))
            dve.tensor_tensor(v3("gd", 4), g4, bc("gm", 4), ALU.subtract).then_inc(gdiff_ready, 1)

            def first_of_max(oh, vals, mx, t4):
                link(dve.tensor_tensor(v3(t4, 4), vals, bc(mx, 4), ALU.is_equal))
                link(dve.tensor_tensor(v3(t4, 4), v3(t4, 4), tie, ALU.mult))
                link(dve.tensor_reduce(R("tm"), v3(t4, 4), AX.X, ALU.max))
                link(dve.tensor_tensor(v3(oh, 4), v3(t4, 4), bc("tm", 4), ALU.is_equal))
            first_of_max("oh", g4, "gm", "t4")
            for g in range(N_GRP):
                sel = v3("oh", 4)[:, :, g:g + 1].to_broadcast([P, NT, 4])
                link(dve.tensor_tensor(v3("t5" if g else "v4", 4), v3("L", 20)[:, :, 4 + 4 * g:8 + 4 * g], sel, ALU.mult))
                if g:
                    link(dve.tensor_tensor(R("v4"), R("v4"), R("t5"), ALU.add))
            link(dve.tensor_reduce(R("m1"), v3("v4", 4), AX.X, ALU.max))
            first_of_max("o1", v3("v4", 4), "m1", "t4")
            link(dve.scalar_tensor_tensor(out=R("v4b"), in0=R("o1"), scalar=-3.0e38, in1=R("v4"), op0=ALU.mult, op1=ALU.add))
            link(dve.tensor_reduce(R("m2"), v3("v4b", 4), AX.X, ALU.max))
            first_of_max("o2", v3("v4b", 4), "m2", "t4")
            dve.tensor_tensor(R("d1"), R("m2"), R("m1"), ALU.subtract).then_inc(tdiff_ready, 1)
            for g in range(N_GRP):
                sel = v3("oh", 4)[:, :, g:g + 1].to_broadcast([P, NT, 4])
                dve.tensor_tensor(v3("s1", 16)[:, :, 4 * g:4 * g + 4], v3("o1", 4), sel, ALU.mult)
                last = dve.tensor_tensor(v3("s2", 16)[:, :, 4 * g:4 * g + 4], v3("o2", 4), sel, ALU.mult)
            link(last)
            dve.tensor_tensor(R("member"), R("s1"), R("s2"), ALU.add).then_inc(member_ready, 1)
            dve.wait_ge(gexp_done, 1)
            link(dve.tensor_reduce(R("gs"), v3("gd", 4), AX.X, ALU.add))
            dve.wait_ge(texp_done, 1)
            link(dve.tensor_scalar(R("w1"), R("d1"), 1.0, None, ALU.add))
            link(dve.tensor_tensor(R("w1"), R("w1"), R("gs"), ALU.mult))
            link(dve.reciprocal(R("w1"), R("w1")))
            link(dve.tensor_tensor(R("w2"), R("w1"), R("d1"), ALU.mult))

            def by_tile(name):
                return v3(name, 16)
            dve.wait_ge(mm_done, done(P_RANK))
            rank = PS[P_RANK % SLOTS][:, 0:P].rearrange("p (t e) -> p t e", e=16)
            link(dve.tensor_copy(R("tot"), PS[P_RANK % SLOTS][:, HALF:HALF + P]))
            base = R("base")
            link(dve.memset(base[:, 0:16], 0.0))
            for tt in range(NT):
                link(dve.tensor_tensor(base[:, 16 * tt + 16:16 * tt + 32], base[:, 16 * tt:16 * tt + 16],
                                       R("tot")[:, 16 * tt:16 * tt + 16], ALU.add))
            ts(R("nblk"), base[:, 128:144], 1.0 / P, 127.0 / 256, ALU.mult, ALU.add)
            ts(R("nblk"), R("nblk"), MAGIC, None, ALU.add)
            ts(R("nblk"), R("nblk"), MAGIC, None, ALU.subtract)
            link(dve.tensor_tensor_scan(R("ends"), ones[:, 0:16], R("nblk"), 0.0, ALU.mult, ALU.add))
            tt_(R("start"), R("ends"), R("nblk"), ALU.subtract)
            ts(R("start"), R("start"), float(P), None, ALU.mult)
            tt_(by_tile("tot"), rank, base[:, 0:128].rearrange("p (t e) -> p t e", e=16), ALU.add, rank_read)
            tt_(by_tile("tot"), by_tile("tot"), R("start").unsqueeze(1).to_broadcast([P, NT, 16]), ALU.add)
            for sel, p, pi in (("s1", "p1", "p1i"), ("s2", "p2", "p2i")):
                tt_(R(sel), R(sel), R("tot"), ALU.mult)
                link(dve.tensor_reduce(R(p), by_tile(sel), AX.X, ALU.add))
                link(dve.tensor_copy(R(pi).bitcast(i32), R(p)))
            cmp3 = R("cmp").rearrange("p (b e) -> p b e", e=16)
            tt_(cmp3, R("ends").unsqueeze(1).to_broadcast([P, NBLK, 16]),
                mat("blk", 0, NBLK).unsqueeze(2).to_broadcast([P, NBLK, 16]), ALU.is_le)
            link(dve.tensor_reduce(R("fe"), cmp3, AX.X, ALU.add))
            ts(R("fe"), R("fe"), float(N_EXP - 1), None, ALU.min)
            ts(R("fq"), R("fe"), 1.0, None, ALU.add)
            link(dve.tensor_copy(R("wait_i").bitcast(i32), R("fq")))
            ts(R("fq"), R("fe"), 1.0 / XBUF, -1.0 / XBUF, ALU.mult, ALU.add)
            ts(R("fq"), R("fq"), MAGIC, None, ALU.add)
            ts(R("fq"), R("fq"), MAGIC, None, ALU.subtract)
            stt(R("fq"), R("fq"), -float(XBUF), R("fe"), ALU.mult, ALU.add)
            ts(R("fq"), R("fq"), float(XPG * S), None, ALU.mult)
            link(dve.tensor_copy(R("page_i").bitcast(i32), R("fq")))
            ts(R("nblk"), R("ends"), 1.0, None, ALU.add)
            dve.tensor_copy(R("ends_i").bitcast(i32), R("nblk")).then_inc(dispatch_ready, 1)
            dve.sem_inc(blocks_done, 1)

            dve.wait_ge(x_scattered, 16 * 2 * NT)

            def block_up(b):
                dve.wait_ge(silu_ready, b + 1)
                if b >= 2:
                    dve.wait_ge(mm_done, done(use_h[b - 2]))
                dve.tensor_tensor(HA[b % 2], PS[use_g[b] % SLOTS][:, F_EXP:2 * F_EXP], SG[b % 2], ALU.mult).then_inc(up_ready, 1)

            def block_hT(b):
                dve.wait_ge(mm_done, done(use_h[b]))
                if b >= 2:
                    dve.wait_ge(mm_done, done(use_y[b - 2]))
                dve.tensor_copy(HAT[b % 2], PS[use_h[b] % SLOTS][:, 0:F_EXP]).then_inc(hT_ready, 1)

            def block_y(b):
                dve.wait_ge(mm_done, done(use_y[b]))
                dve.sem_inc(blocks_done, 1)
                if b >= 3:
                    dve.wait_ge(y_stored[b % 3], 16 * (b // 3))
                dve.tensor_copy(YB[b % 3], PS[use_y[b] % SLOTS][:, :]).then_inc(y_ready, 1)

            for t in range(1, NBLK + 2):
                for lag, stage in ((1, block_up), (2, block_y), (1, block_hT)):
                    if 0 <= t - lag < NBLK:
                        stage(t - lag)
            for tt in range(NT):
                k = (2 * tt) % 4
                a, b = YG[k], YG[k + 1]
                dve.wait_ge(y_gathered[k], 16 * (tt // 2 + 1))
                link(dve.tensor_scalar(a, a, R("w1")[:, tt:tt + 1], None, ALU.mult))
                dve.wait_ge(y_gathered[k + 1], 16 * (tt // 2 + 1))
                dve.scalar_tensor_tensor(out=b, in0=b, scalar=R("w2")[:, tt:tt + 1], in1=a, op0=ALU.mult,
                                         op1=ALU.add).then_inc(ysum_added, 1)
                dve.wait_ge(mm_done, done(P_YSUM + tt))
                cols = hT[:, :, tt * P:(tt + 1) * P]
                dve.tensor_tensor(cols, PS[(P_YSUM + tt) % SLOTS][:, :].rearrange("p (k n) -> p k n", n=P), cols,
                                  ALU.add).then_inc(ysum_ready, 1)
            norm(n_fin1)
            norm(n_att2)

            dve.wait_ge(in2_ready, 19)
            for c in range(2):
                x, y = Wp[PG_RX + c], Wp[19 + c]
                link(dve.tensor_scalar(y, x, par("rg_w", 6 + c), par("rg_cb", c), ALU.mult, ALU.add))
                for s_ in range(1, 4):
                    ins = dve.scalar_tensor_tensor(out=y[:, s_:S], in0=x[:, 0:S - s_], scalar=par("rg_w", 2 * (3 - s_) + c),
                                                   in1=y[:, s_:S], op0=ALU.mult, op1=ALU.add)
                    if s_ < 3:
                        link(ins)
                    else:
                        ins.then_inc(conv_ready, 1)
            dve.wait_ge(conv_ready, 2)
            dve.wait_ge(tanh_ready, 2)
            for c in range(2):
                last = dve.tensor_scalar(Bp[2 + c], Wp[21 + c], 1.0, None, ALU.add)
            link(last)
            for c in range(2):
                last = dve.reciprocal(Bp[2 + c], Bp[2 + c])
            link(last)
            for c in range(2):
                dve.tensor_tensor(Wp[23 + c], Wp[23 + c], Wp[19 + c], ALU.mult)
                last = dve.tensor_scalar(Bp[4 + c], Bp[2 + c], 2.0, -1.0, ALU.mult, ALU.add)
            link(last)
            dve.wait_ge(root_ready, 2)
            for c in range(2):
                last = dve.tensor_tensor(Bp[2 + c], Bp[2 + c], Bp[c], ALU.mult)
            link(last)
            for c in range(2):
                last = dve.tensor_tensor(Wp[23 + c], Wp[23 + c], Bp[2 + c], ALU.mult)
            link(last)
            for c in range(2):
                last = dve.tensor_tensor_scan(Wp[PG_RX + c], Bp[4 + c], Wp[23 + c], 0.0, ALU.mult, ALU.add)
            link(last)
            dve.wait_ge(ggate_ready, 2)
            for c in range(2):
                last = dve.tensor_tensor(Wp[PG_RX + c], Wp[PG_RX + c], Wp[PG_RG + c], ALU.mult)
            last.then_inc(rg_ready, 1)
            norm(n_rg)

            dve.wait_ge(s5_loaded, 16)
            for j in range(8):
                cols = slice(j * P, (j + 1) * P)
                fr, fi, nfi = s5p[:, 3, j:j + 1], s5p[:, 4, j:j + 1], s5p[:, 25, j:j + 1]
                dve.tensor_scalar(Wp[19][:, cols], Bp[0][:, cols], fi, None, ALU.mult)
                last = dve.tensor_scalar(Wp[20][:, cols], Bp[1][:, cols], nfi, None, ALU.mult)
            link(last)
            for j in range(8):
                cols = slice(j * P, (j + 1) * P)
                fr = s5p[:, 3, j:j + 1]
                dve.scalar_tensor_tensor(out=Bp[0][:, cols], in0=Bp[0][:, cols], scalar=fr, in1=Wp[20][:, cols],
                                         op0=ALU.mult, op1=ALU.add)
                last = dve.scalar_tensor_tensor(out=Bp[1][:, cols], in0=Bp[1][:, cols], scalar=fr, in1=Wp[19][:, cols],
                                                op0=ALU.mult, op1=ALU.add)
            last.then_inc(s5b_ready, 1)
            ec, es, vr, vi = Wp[2], Wp[3], Wp[19], Wp[20]
            ta, tb, xr, xi = Wp[21], Wp[22], Wp[4], Wp[5]
            dve.memset(ec[:, 0:1], 1.0)
            link(dve.memset(es[:, 0:1], 0.0))
            for c in range(2):
                last = dve.tensor_scalar(Wp[24 - c], Wp[PG_U + c], par("s5_d", c), None, ALU.mult)
            link(last)
            for j in range(8):
                rr = s5p[:, 0, j:j + 1]
                for k2 in range(10):
                    n = 1 << k2
                    wc, ws = s5p[:, 5 + 2 * k2, j:j + 1], s5p[:, 6 + 2 * k2, j:j + 1]
                    dve.tensor_scalar(ta[:, 0:n], es[:, 0:n], ws, None, ALU.mult)
                    link(dve.tensor_scalar(tb[:, 0:n], ec[:, 0:n], ws, None, ALU.mult))
                    dve.scalar_tensor_tensor(out=ec[:, n:2 * n], in0=ec[:, 0:n], scalar=wc, in1=ta[:, 0:n],
                                             op0=ALU.mult, op1=ALU.subtract)
                    link(dve.scalar_tensor_tensor(out=es[:, n:2 * n], in0=es[:, 0:n], scalar=wc, in1=tb[:, 0:n],
                                                  op0=ALU.mult, op1=ALU.add))
                n0 = P_S5 + 3 * j
                dve.wait_ge(mm_done, done(n0 + 1))
                bre, bim = PS[n0 % SLOTS][:, :], PS[(n0 + 1) % SLOTS][:, :]
                dve.tensor_tensor(vr, bre, ec, ALU.mult)
                dve.tensor_tensor(ta, bim, es, ALU.mult)
                dve.tensor_tensor(vi, bim, ec, ALU.mult)
                dve.tensor_tensor(tb, bre, es, ALU.mult).then_inc(s5in_ready, 1)
                dve.wait_ge(s5in_ready, j + 1)
                dve.tensor_tensor(vr, vr, ta, ALU.add)
                link(dve.tensor_tensor(vi, vi, tb, ALU.subtract))
                dve.tensor_tensor_scan(vr, rr.to_broadcast([P, S]), vr, 0.0, ALU.mult, ALU.add)
                link(dve.tensor_tensor_scan(vi, rr.to_broadcast([P, S]), vi, 0.0, ALU.mult, ALU.add))
                if j:
                    dve.wait_ge(mm_done, done(n0 - 1))
                dve.tensor_tensor(xr, vr, ec, ALU.mult)
                dve.tensor_tensor(ta, vi, es, ALU.mult)
                dve.tensor_tensor(xi, vi, ec, ALU.mult)
                link(dve.tensor_tensor(tb, vr, es, ALU.mult))
                dve.tensor_tensor(xr, xr, ta, ALU.subtract)
                dve.scalar_tensor_tensor(out=xi, in0=xi, scalar=-1.0, in1=tb, op0=ALU.mult,
                                         op1=ALU.subtract).then_inc(s5x_ready, 1)
                dve.wait_ge(mm_done, done(n0 + 2))
                acc = Wp[24 - j // 4]
                dve.tensor_tensor(acc, PS[(n0 + 2) % SLOTS][:, :], acc, ALU.add).then_inc(s5y_ready, 1)
            dve.wait_ge(s5s_ready, 2)
            for c in range(2):
                dve.tensor_tensor(Wp[c], Wp[c], Wp[22 - c], ALU.mult).then_inc(s5_ready, 1)
            norm(n_s5)

            bcp, ex = pair(0), pair(2)
            for m in range(2):
                n = P_GK + m
                dve.wait_ge(mm_done, done(n))
                x = PS[n % SLOTS][:, :]
                dve.tensor_scalar(Wp[m], x, par("gk_bias", m), None, ALU.add).then_inc(gk_biased, 1)
                dve.wait_ge(gk_biased, m + 1)
                dve.scalar_tensor_tensor(out=Wp[2 + m], in0=Wp[m], scalar=-1.0, in1=Wp[m], op0=ALU.mult, op1=ALU.max).then_inc(gk_abs, 1)
                link(dve.tensor_scalar(Wp[m], Wp[m], 0.0, 1.0 / 16, ALU.min, ALU.mult))
            link(dve.memset(Wp[4], 1.0))
            link(dve.memset(Wp[4].rearrange("p (n c) -> p n c", c=CH)[:, :, 0:1], 0.0))
            dve.wait_ge(gk_ln, 1)
            link(dve.scalar_tensor_tensor(out=bcp, in0=ex, scalar=-1.0 / 16, in1=bcp, op0=ALU.mult, op1=ALU.add))
            for m in range(2):
                last = dve.tensor_tensor_scan(Wp[m], Wp[4], Wp[m], 0.0, ALU.mult, ALU.add)
            link(last)
            q, k = pair(PG_Q), pair(PG_K)

            def chunks(ap):
                return ap.rearrange("p a (n c) -> p (a n) c", c=CH)
            b3 = chunks(bcp)
            mid = b3[:, :, CH // 2 - 1:CH // 2].to_broadcast([P, 2 * NCH, CH])
            end = b3[:, :, CH - 1:CH].to_broadcast([P, 2 * NCH, CH])
            dve.tensor_tensor(chunks(ex), b3, mid, ALU.subtract).then_inc(bc_ready, 1)
            dve.wait_ge(gexps, 1)
            link(dve.tensor_tensor(pair(4), q, ex, ALU.mult))
            dve.tensor_tensor(chunks(ex), mid, b3, ALU.subtract).then_inc(gexps_used, 1)
            dve.wait_ge(gexps, 2)
            link(dve.tensor_tensor(pair(19), k, ex, ALU.mult))
            dve.tensor_tensor(chunks(ex), end, b3, ALU.subtract).then_inc(gexps_used, 1)
            dve.wait_ge(gexps, 3)
            dve.tensor_tensor(k, k, ex, ALU.mult).then_inc(gprods, 1)
            dve.wait_ge(gexps, 4)
            dve.tensor_tensor(q, q, ex, ALU.mult).then_inc(gprods, 1)
            dve.wait_ge(gprods, 2)
            dve.wait_ge(decay_ready, 1)
            st = [pair(23).rearrange("p a (b c) -> p (a b) c", c=P), pair(2).rearrange("p a (b c) -> p (a b) c", c=P)]
            for m in range(2):
                for q4 in range(4):
                    n_ = P_KV + 4 * m + q4
                    dve.wait_ge(mm_done, done(n_))
                    for j in range(4):
                        n = 4 * q4 + j
                        if n == NCH - 1:
                            continue
                        for hh in range(2):
                            r = slice(hh * DH, (hh + 1) * DH)
                            c0 = (j % 2) * HALF + (j // 2) * 256 + hh * P
                            kv = PS[n_ % SLOTS][r, c0:c0 + P]
                            if n == 0:
                                last = dve.tensor_copy(st[m][r, 1, :], kv)
                            else:
                                last = dve.scalar_tensor_tensor(out=st[m][r, n + 1, :], in0=st[m][r, n, :],
                                                                scalar=decay[r, m, n:n + 1], in1=kv,
                                                                op0=ALU.mult, op1=ALU.add)
                        if j < 3 and n < NCH - 2:
                            link(last)
                    last.then_inc(state_ready, 1)
                    dve.wait_ge(state_ready, 4 * m + q4 + 1)
            causal = mat("causal").bitcast(i32)
            for h in range(4):
                n = P_SC + h
                if h == 3:
                    dve.wait_ge(mm_done, done(P_KV + 7))
                link(dve.memset(Mp[h], 0.0))
                dve.wait_ge(mm_done, done(n))
                for tt_ in range(NT):
                    cols = slice(tt_ * P, (tt_ + 1) * P)
                    last = dve.copy_predicated(Mp[h][:, cols], causal, PS[n % SLOTS][:, cols])
                last.then_inc(intra_ready, 1)
            for h in range(4):
                norm_c = n_gla[h]
                norm(norm_c)
                dve.wait_ge(gsilu, h + 1)
                dve.tensor_tensor(Bp[h], Bp[h], Wp[PG_G + h], ALU.mult).then_inc(gla_ready, 1)
            add_to_h(P_OUT2, 8)
            norm(n_mlp)

            for j in range(FF):
                n = P_UP + 2 * j
                y, x = Wp[22 + j % 3], PS[n % SLOTS]
                dve.wait_ge(conv0_ready, j + 1)
                link(dve.scalar_tensor_tensor(out=y[:, 1:S], in0=x[:, 0:S - 1], scalar=par("ff_w", FF + j), in1=y[:, 1:S],
                                              op0=ALU.mult, op1=ALU.add))
                dve.scalar_tensor_tensor(out=y[:, 2:S], in0=x[:, 0:S - 2], scalar=par("ff_w", j), in1=y[:, 2:S],
                                         op0=ALU.mult, op1=ALU.add).then_inc(conv1_ready, 1)
                dve.wait_ge(conv1_ready, j + 1)
                dve.wait_ge(gelu_ready, j + 1)
                dve.wait_ge(mm_done, done(n + 1))
                dve.tensor_tensor(Wp[j], PS[(n + 1) % SLOTS][:, :], y, ALU.mult).then_inc(ffact_ready, 1)
            add_to_h(P_DOWN, 16)
            norm(n_fin2, final_ready)


def dilated_strips():
    d = np.arange(STRIP)[None, :] - 896 - np.arange(P)[:, None]
    ad = np.abs(d)
    count = ((ad <= 64).astype(int) + ((d % 4 == 0) & (ad <= 256)) + (d % 16 == 0))
    base = np.where(count > 0, np.log(np.maximum(count, 1)), NEG)
    slopes = 2.0 ** -np.arange(1, 9)
    return np.stack([np.where(count > 0, base - s * ad, NEG) for s in slopes]).astype(np.float32)


def neighbourhood_strips(rpb):
    q, k = np.arange(P), np.arange(NF)
    qr, qc = (q // 64)[:, None], (q % 64)[:, None]
    kr, kc = (k // 64 - 6)[None, :], (k % 64)[None, :]
    dr, dc = kr - qr + 7, kc - qc + 15
    cs = np.clip(qc - 8, 0, 48)
    col_ok = (kc >= cs) & (kc < cs + 16)
    ok = col_ok & (dr >= 0) & (dr <= 14)
    full = np.where(ok, rpb[:, np.clip(dr, 0, 14), np.clip(dc, 0, 30)], np.float32(NEG))
    rows = (kr >= qr - 4) & (kr < qr + 4)
    inner = np.where(rows, full, np.float32(NEG))[:, :, P:P + NI]
    return np.ascontiguousarray(np.concatenate([full, inner], axis=2))


def column_units(w):
    k, m = w.shape
    return np.ascontiguousarray(w.reshape(k // P, P, m // P, P).transpose(2, 1, 0, 3).reshape(m // P, P, (k // P) * P))


def pack(i):
    f = np.float32

    def tiles(v):
        return np.asarray(v, f).reshape(-1, P).T
    x = np.asarray(i["x"])[0]
    cst = np.zeros((P, NCOL), f)

    def put(name, a, cols=PCOLS):
        a = np.asarray(a, f)
        cst[:a.shape[0], cols[name]:cols[name] + a.shape[1]] = a
    put("norm_mix", tiles(i["norm_mix_g"][0]))
    put("g_out", np.concatenate([tiles(i["g_out_dil"][0]), tiles(i["g_out_na"][0])], 1))
    put("norm_ffn", tiles(i["norm_ffn_g"][0]))
    put("norm_final", tiles(i["norm_final_g"]))
    put("attn_norm", tiles(i["attn_norm_2"][0]))
    put("gk_bias", tiles(i["gla_b_gk_2"][0]))
    put("gla_norm", tiles(i["gla_norm_2"][0]))
    put("lam_re", tiles(i["s5_lambda_re_2"][0].reshape(-1)))
    put("lam_im", tiles(i["s5_lambda_im_2"][0].reshape(-1)))
    put("log_dt", tiles(np.repeat(i["s5_log_dt_2"][0], 64)))
    put("s5_d", tiles(i["s5_d_2"][0]))
    put("b_glu", tiles(i["s5_b_glu_2"][0]))
    put("s5_norm", tiles(i["s5_norm_2"][0]))
    put("rg_w", np.concatenate([tiles(i["rg_conv_w_2"][0][t]) for t in range(4)], 1))
    put("rg_cb", tiles(i["rg_conv_b_2"][0]))
    put("rg_ba", tiles(i["rg_b_a_2"][0]))
    put("rg_bx", tiles(i["rg_b_x_2"][0]))
    put("rg_lam", tiles(i["rg_lambda_2"][0]))
    put("rg_norm", tiles(i["rg_norm_2"][0]))
    put("mlp_norm", tiles(i["mlp_norm_2"][0]))
    put("ff_w", np.concatenate([tiles(i["mlp_conv_w_2"][0][t]) for t in range(3)], 1))
    put("ff_cb", tiles(i["mlp_conv_b_2"][0]))
    put("final_norm", tiles(i["final_norm_2"]))
    put("ones", np.ones((P, P)), MCOLS)
    put("ident", np.eye(P), MCOLS)
    s, c = np.arange(P)[:, None], np.arange(P)[None, :]
    put("causal", ((c >= s) & (c // CH == s // CH)).astype(f), MCOLS)
    route = np.concatenate([i["w_group"][0], i["w_router"][0]], 1)
    put("route", route.reshape(NT, P, 20).transpose(1, 0, 2).reshape(P, -1), MCOLS)
    w2 = np.asarray(i["w_in_2"][0])
    put("low", w2[:, 1536:1552].reshape(NT, P, 16).transpose(1, 0, 2).reshape(P, -1), MCOLS)
    rg = np.zeros((P, 4, P), f)
    for j, name in enumerate(("rg_w_a_2", "rg_w_x_2")):
        for h in range(4):
            r = (h % 2) * 64
            rg[r:r + 64, 2 * j + h // 2, r:r + 64] = i[name][0][h]
    put("rg", rg.reshape(P, -1), MCOLS)
    put("glu", np.asarray(i["s5_w_glu_2"][0]).reshape(2, P, 256).transpose(1, 0, 2).reshape(P, -1), MCOLS)
    put("gkup", i["gla_w_gk_up_2"][0], MCOLS)
    put("bias20", np.broadcast_to(np.concatenate([i["b_group"][0], i["b_router"][0]])[None], (P, 20)), MCOLS)
    put("before", (s < c).astype(f), MCOLS)
    put("blk", np.broadcast_to(np.arange(NBLK)[None], (P, NBLK)), MCOLS)
    put("tie", np.broadcast_to(np.array([4.0, 3.0, 2.0, 1.0])[None], (P, 4)), MCOLS)

    w = np.asarray(i["w_in"][0])
    cols = {"dil": [w[:, 512 * n:512 * (n + 1)] for n in range(3)], "na": [w[:, 1536 + 512 * n:1536 + 512 * (n + 1)] for n in range(3)]}
    w_in = column_units(np.concatenate([cols["dil"][0], cols["na"][0], cols["dil"][1], cols["na"][1], cols["dil"][2], cols["na"][2]], 1))
    gate, up = (np.asarray(i[n][0]).reshape(N_EXP, NT, P, F_EXP) for n in ("w_gate", "w_up"))
    gu = np.concatenate([gate, up], 3).transpose(0, 2, 1, 3).reshape(N_EXP, P, 4 * S)
    dn = np.asarray(i["w_down"][0]).reshape(N_EXP, 2, P, D).transpose(0, 2, 1, 3).reshape(N_EXP, P, 2 * S)
    moe = np.concatenate([gu, dn], 2)
    w_in2 = column_units(np.concatenate([w2[:, 1808:2064], w2[:, 2064:2320], w2[:, 1552:1808], w2[:, 0:512], w2[:, 1024:1536], w2[:, 512:1024]], 1))
    up_u = column_units(i["w_up_2"][0])
    w_up = np.stack([up_u[j // 2 + (j % 2) * FF] for j in range(2 * FF)])
    down = column_units(np.concatenate([i["w_down_2"][0], np.zeros((2 * P, D), f)], 0))
    w_down = np.ascontiguousarray(down.reshape(8, P, 3, NT * P).transpose(0, 2, 1, 3).reshape(24, P, NT * P))
    mats = np.zeros((P, 4, 8, P), f)
    for g in range(16):
        r, j, c0 = (g % 2) * 64, g // 2, (g % 8) * 16
        mats[r:r + 64, 0, j, c0:c0 + 16] = i["s5_b_re_2"][0][g]
        mats[r:r + 64, 1, j, c0:c0 + 16] = i["s5_b_im_2"][0][g]
        mats[r:r + 64, 2, j, c0:c0 + 16] = i["s5_c_re_2"][0][g].T
        mats[r:r + 64, 3, j, c0:c0 + 16] = i["s5_c_im_2"][0][g].T
    return {
        "xT": np.ascontiguousarray(x.T.reshape(NT, P, S).transpose(1, 0, 2)),
        "params": cst, "w_in_units": w_in, "w_out_units": column_units(i["w_out"][0]), "w_moe": moe,
        "w_in2_units": w_in2, "w_out2_units": column_units(i["w_out_2"][0]), "w_up_units": w_up, "w_down_units": w_down,
        "dil_strip": dilated_strips(), "na_strip": neighbourhood_strips(np.asarray(i["rpb"][0])),
        "s5_mats": mats.reshape(P, 4, 8 * P),
    }


def kernel(**inputs):
    import concourse.bacc as bacc
    from concourse.bass_utils import run_bass_kernel_spmd

    nc = bacc.Bacc("TRN2", target_bir_lowering=False, num_devices=1)
    arrays = pack({k: np.asarray(v) for k, v in inputs.items()})
    args = [nc.dram_tensor(k, a.shape, mybir.dt.from_np(a.dtype), kind="ExternalInput").ap() for k, a in arrays.items()]
    args.append(nc.dram_tensor("outT", (P, NT, S), mybir.dt.float32, kind="ExternalOutput").ap())
    build(nc, *args)
    r = run_bass_kernel_spmd(nc, [arrays], core_ids=[0])
    got = r.results[0]["outT"]
    return np.ascontiguousarray(got.transpose(1, 0, 2).reshape(D, S).T).reshape(1, S, D)
```

```python
import concourse.bass as bass
from concourse import mybir
from contextlib import ExitStack
import numpy as np

P = 128
S = 1024
D = 1024
NT = D // P
HALF = 512
DH = 64
NH = 16
NEG = -1e30
EPS = 1e-6
SLOTS = 4
RING = 4
STRIP = 1920
NF, NI = 7 * P, 5 * P
N_EXP, N_GRP, EPG = 16, 4, 4
F_EXP = 256
NBLK = 2 * S // P + N_EXP - 1
XPG = 6
XBUF = 3
FF = 22
FF_GROUPS = [range(0, 6), range(6, 12), range(12, 18), range(18, FF)]
FF_KEEP = 7
FFN_STEPS = [("up", j) for j in FF_GROUPS[0]]
for _g in range(4):
    _next = list(FF_GROUPS[_g + 1]) if _g < 3 else []
    FFN_STEPS += [("up", j) for j in _next[:1]] + [("down", _g)] + [("up", j) for j in _next[1:]]
CH = 64
GLA_STEPS = [("o", 0), ("o", 1), ("sum", 0), ("o", 2), ("root", 0), ("sum", 1), ("o", 3), ("root", 1), ("sum", 2),
             ("root", 2), ("sum", 3), ("root", 3)]
NCH = S // CH

PCOLS = {}
_at = 0
for _name, _n in (("norm_mix", 8), ("g_out", 8), ("norm_ffn", 8), ("norm_final", 8), ("attn_norm", 8),
                  ("gk_bias", 2), ("gla_norm", 1), ("lam_re", 8), ("lam_im", 8), ("log_dt", 8), ("s5_d", 2),
                  ("b_glu", 2), ("s5_norm", 2), ("rg_w", 8), ("rg_cb", 2), ("rg_ba", 2), ("rg_bx", 2),
                  ("rg_lam", 2), ("rg_norm", 2), ("mlp_norm", 8), ("ff_w", 3 * FF), ("ff_cb", FF), ("final_norm", 8)):
    PCOLS[_name] = _at
    _at += _n
MCOLS = {}
for _name, _n in (("ones", P), ("ident", P), ("causal", P), ("route", NT * 20), ("low", NT * 16), ("rg", 4 * P),
                  ("glu", 2 * 256), ("gkup", 256), ("bias20", 20), ("tie", 4), ("before", P), ("blk", 31)):
    MCOLS[_name] = _at
    _at += _n
NCOL = _at


def key_tiles(h, i):
    if h < 8:
        return 0, 8
    return (max(i - 2, 0), min(i + 3, 8)) if 2 <= i <= 5 else ((0, 4) if i < 2 else (4, 8))


def build(nc, xT, params, w_in, w_out, w_moe, w_in2, w_out2, w_up, w_down, dil_strip, na_strip, s5_b, s5_c, out):
    f32, i32, u32 = mybir.dt.float32, mybir.dt.int32, mybir.dt.uint32
    ALU, ACT, AX = mybir.AluOpType, mybir.ActivationFunctionType, mybir.AxisListType
    x_slots = nc.dram_tensor("x_slots", (NBLK * P, D), f32, kind="Internal").ap()
    y_slots = nc.dram_tensor("y_slots", (NBLK * P, D), f32, kind="Internal").ap()

    ctx = ExitStack()
    with ctx:
        def sb(name, shape, dt=f32):
            return ctx.enter_context(nc.sbuf_tensor(name, shape, dt))

        def sem(name):
            return ctx.enter_context(nc.semaphore(name))

        f32r = mybir.dt.float32r
        with ExitStack() as second:
            hTr = [second.enter_context(nc.sbuf_tensor(f"hT_part{t}", [P, S], f32r)) for t in range(NT)]
            Wr = [second.enter_context(nc.sbuf_tensor(f"work_part{t}", [P, S], f32r)) for t in range(37 + RING)]
        hT = sb("hT", [P, NT, S])
        W = sb("work", [P, 37, S])
        ring = sb("ring", [P, RING, NT * P])
        bT = W[:, 29:37, :]
        cst = sb("cst", [P, NCOL])
        small = sb("small", [P, 40, 8])
        s5p = sb("s5p", [P, 26, 8])
        sp4 = sb("sp4", [P, 2])
        epsc = sb("epsc", [P, 1])
        negm = sb("negm", [P, 4])
        den = sb("den", [P, 8])
        rden = sb("rden", [P, 8])
        zeros = sb("zeros", [P, NT])
        std = sb("std", [P, 4, NT])
        decay = sb("decay", [P, 2, NCH])
        PS = [ctx.enter_context(nc.psum_tensor(f"ps{i}", [P, S], f32)) for i in range(SLOTS)]

        BHI = [Wr[29 + t][:, :] for t in range(NT)]
        WHI, WLO = [Wr[25][:, :], Wr[27][:, :]], [Wr[26][:, :], Wr[28][:, :]]
        QS, KH = [Wr[25][:, :], Wr[27][:, :]], [Wr[26][:, :], Wr[28][:, :]]
        KL = [Wr[37 + 2][:, :], Wr[37 + 3][:, :]]
        WHI_F = [a.bitcast(f32) for a in WHI]

        def par(name, c=0, n=1):
            return cst[:, PCOLS[name] + c:PCOLS[name] + c + n]

        def mat(name, c=0, n=P):
            return cst[:, MCOLS[name] + c:MCOLS[name] + c + n]

        ones, ident = mat("ones"), mat("ident")

        w_loaded = [sem(f"w_loaded{i}") for i in range(RING)]
        mm_done = sem("mm_done")
        x_loaded = [sem(f"x_loaded{i}") for i in range(4)]
        cst_loaded = sem("cst_loaded")
        strip_loaded = [sem(f"strip_loaded{i}") for i in range(2)]
        x_again = sem("x_again")
        s5_loaded = sem("s5_loaded")
        zero_set, slots_zeroed, x_scattered = sem("zero_set"), sem("slots_zeroed"), sem("x_scattered")
        expert_dma = [sem(f"expert_dma{i}") for i in range(XBUF)]
        expert_loaded, blocks_done = sem("expert_loaded"), sem("blocks_done")
        block_loaded = [sem(f"block_loaded{i}") for i in range(2)]
        y_stored = [sem(f"y_stored{i}") for i in range(3)]
        y_gathered = [sem(f"y_gathered{i}") for i in range(4)]
        member_ready, rank_read, dispatch_ready, xtm_ready = (
            sem("member_ready"), sem("rank_read"), sem("dispatch_ready"), sem("xtm_ready"))
        xT_ready, up_ready, hT_ready, y_ready, ysum_ready = (
            sem("xT_ready"), sem("up_ready"), sem("hT_ready"), sem("y_ready"), sem("ysum_ready"))
        ysum_added = sem("ysum_added")
        out_stored = sem("out_stored")
        sq_ready, sq_used, std_ready, normed = sem("sq_ready"), sem("sq_used"), sem("std_ready"), sem("normed")
        eps_set = sem("eps_set")
        qk_parts = sem("qk_parts")
        whi_ready, wlo_ready = sem("whi_ready"), sem("wlo_ready")
        xn_ready, xhi_ready, xlo_ready = sem("xn_ready"), sem("xhi_ready"), sem("xlo_ready")
        prod_ready, ffhi_ready = sem("prod_ready"), sem("ffhi_ready")
        qkv_ready, vT_ready = sem("qkv_ready"), sem("vT_ready")
        inverse_ready, root_spread = sem("inverse_ready"), sem("root_spread")
        scores_ready, exp_done, pT_ready, heads_done, f_ready = (
            sem("scores_ready"), sem("exp_done"), sem("pT_ready"), sem("heads_done"), sem("f_ready"))
        h_ready = sem("h_ready")
        gdiff_ready, gexp_done, tdiff_ready, texp_done = (
            sem("gdiff_ready"), sem("gexp_done"), sem("tdiff_ready"), sem("texp_done"))
        silu_ready = sem("silu_ready")
        in2_ready = sem("in2_ready")
        onep_ready, s5v_ready, pool_link, s5c_ready = (sem(n) for n in ("onep_ready", "s5v_ready", "pool_link", "s5c_ready"))
        conv_ready, gates_ready, tanh_ready, root_ready, ggate_ready, rg_ready = (
            sem("conv_ready"), sem("gates_ready"), sem("tanh_ready"), sem("root_ready"), sem("ggate_ready"), sem("rg_ready"))
        s5b_ready, s5bT_ready, s5x_ready, s5y_ready, s5g_ready, s5s_ready, s5_ready = (
            sem("s5b_ready"), sem("s5bT_ready"), sem("s5x_ready"), sem("s5y_ready"), sem("s5g_ready"), sem("s5s_ready"), sem("s5_ready"))
        s5in_ready, gk_biased, gexps_used, decay_ready, gk_abs, gk_exp, gk_ln, bc_ready, gexps, gprods, klT_ready, state_ready, intra_ready, o_ready, gsilu, gla_ready = (
            sem(n) for n in ("s5in_ready", "gk_biased", "gexps_used", "decay_ready", "gk_abs", "gk_exp", "gk_ln", "bc_ready", "gexps", "gprods", "klT_ready", "state_ready",
                             "intra_ready", "o_ready", "gsilu", "gla_ready"))
        conv0_ready, conv1_ready, gelu_ready, ffact_ready = (
            sem("conv0_ready"), sem("conv1_ready"), sem("gelu_ready"), sem("ffact_ready"))
        dve_link, act_link = sem("dve_link"), sem("act_link")

        units = [w_in[n] for n in range(24)] + [w_out[n] for n in range(8)]
        units += [w_in2[n] for n in range(18)] + [w_out2[n] for n in range(8)]
        for what, i in FFN_STEPS:
            if what == "up":
                units += [w_up[2 * i], w_up[2 * i + 1]]
            else:
                units += [w_down[8 * i + m, :, 0:len(FF_GROUPS[i]) * P] for m in range(8)]
        U_IN, U_OUT, U_IN2 = 0, 24, 32
        U_OUT2 = U_IN2 + 18
        U_UP = U_OUT2 + 8
        split_units = list(range(0, U_IN2)) + list(range(U_UP, len(units)))
        split_of = {u: n for n, u in enumerate(split_units)}

        at = [0]

        def take(k):
            at[0] += k
            return at[0] - k

        norms = []
        sq_base = [0]

        emptied = {}

        def done(n):
            return n + 1 - sum((c["use"] < n) + (c["root_use"] < n) for c in norms)

        split_base = [0]

        xn_base = [0]

        def add_norm(src, gain, dst, scratch, tiles, use, root_use=None, parts=None):
            root_use = use + 1 if root_use is None else root_use
            norms.append(dict(src=src, gain=gain, dst=dst, scratch=scratch, tiles=tiles, use=use, sq0=sq_base[0],
                              index=len(norms), parts=parts, lo0=split_base[0], xn0=xn_base[0], root_use=root_use))
            xn_base[0] += tiles
            if parts:
                split_base[0] += tiles
            sq_base[0] += tiles
            emptied[use] = (std_ready, len(norms))
            emptied[root_use] = (xn_ready, xn_base[0])
            return norms[-1]

        Hp = [hT[:, t, :] for t in range(NT)]
        Bp = [bT[:, t, :] for t in range(NT)]
        Wp = [W[:, t, :] for t in range(29)]

        n_mix = add_norm(Hp, "norm_mix", (Wp[19:22] * 3)[0:8], Wp[22:25], 8, take(2),
                         parts=(BHI, [hTr[t][:, :] for t in range(NT)]))
        U_QKV = [take(1) for m in range(16)]
        U_VT, U_V = [], []
        for m in range(9):
            if m < 8:
                U_VT.append(take(1))
            if m >= 1:
                U_V.append(take(1))
        LAG_T, LAG_O = 2, 3
        NU = NH * NT
        LAG_F = 5
        use_s, use_t, use_o, use_f = {}, {}, {}, {}
        for t in range(NU + LAG_F):
            if t < NU:
                use_s[t] = take(1)
            if 0 <= t - LAG_T < NU:
                use_t[t - LAG_T] = take(1)
            if 0 <= t - LAG_O < NU:
                use_o[t - LAG_O] = take(1)
            if NU - NT <= t - LAG_F:
                use_f[t - LAG_F - (NU - NT)] = take(1)
        YHI, YLO = [Wr[t][:, :] for t in range(8)], [Wr[t][:, :] for t in (15, 8, 9, 10, 11, 12, 13, 14)]
        n_dil = add_norm(Wp[0:4], "g_out", Bp[0:4], Wp[16:19], 4, take(1), at[0] + 1, parts=(YHI[0:4], YLO[0:4]))
        n_na = add_norm(Wp[4:7] + [Wp[14]], "g_out", Bp[4:8], Wp[19:22], 4, take(1), at[0] + 1, parts=(YHI[4:8], YLO[4:8]))
        take(2)
        P_OUT = take(8)
        n_ffn = add_norm(Hp, "norm_ffn", Bp, Wp[19:22], 8, take(2))
        P_ROUTE = take(1)
        P_XTM = take(8)
        P_RANK = take(1)
        use_x, use_g, use_y, use_h = {}, {}, {}, {}
        for t in range(NBLK + 2):
            for lag, of in ((0, use_x), (1, use_g), (2, use_y), (1, use_h)):
                if 0 <= t - lag < NBLK:
                    of[t - lag] = take(1)
        P_YSUM = take(8)
        n_fin1 = add_norm(Hp, "norm_final", Hp, Wp[22:25], 8, take(2))
        n_att2 = add_norm(Hp, "attn_norm", Bp, Wp[22:25], 8, take(2))
        MAIN = [take(1) for _ in range(3)]
        P_RG = [take(1) for _ in range(4)]
        MAIN.append(take(1))
        P_S5T = take(2)
        MAIN += [take(1), take(1)]
        P_BU, P_CX = [], []
        for j in range(9):
            if j < 8:
                P_BU.append(take(2))
                MAIN.append(take(1))
            if j >= 1:
                P_CX.append(take(1))
        MAIN += [take(1), take(1)]
        P_GLU = take(2)
        MAIN.append(take(1))
        n_rg = add_norm(Wp[2:4], "rg_norm", Wp[2:4], [Wp[19], Wp[20], Wp[23]], 2, take(1), at[0] + 3)
        n_s5 = add_norm(Wp[0:2], "s5_norm", Wp[0:2], [Wp[19], Wp[20], Wp[21]], 2, take(1), at[0] + 3)
        P_GK = take(2)
        take(2)
        MAIN += [take(1), take(1)]
        P_KLT = take(2)
        P_KV = take(8)
        P_SC = take(4)
        P_O, gla_sum, gla_root = {}, {}, {}
        for what, h in GLA_STEPS:
            {"o": P_O, "sum": gla_sum, "root": gla_root}[what][h] = take(1)
        n_gla = [add_norm([Wp[4 + h] if h < 2 else Wp[17 + h]], "gla_norm", [Bp[h]],
                          [Bp[4], None, Bp[5]] if h % 2 == 0 else [Wp[21], None, Wp[22]], 1, gla_sum[h], gla_root[h]) for h in range(4)]
        P_OUT2 = take(8)
        XLO = [Wr[t][:, :] for t in range(8)]
        n_mlp = add_norm(Hp, "mlp_norm", (Wp[19:22] * 3)[0:8], Wp[22:25], 8, take(2), parts=(BHI, XLO))
        P_UP, P_DOWN = {}, {}
        for what, i in FFN_STEPS:
            if what == "up":
                P_UP[i] = take(2)
            else:
                P_DOWN[i] = take(8)
        group_of = {j: g for g, group in enumerate(FF_GROUPS) for j in group}
        FHI = [Wr[8 + i][:, :] for i in range(FF_KEEP)]
        FHI_F = [a.bitcast(f32) for a in FHI]
        FLO = [Wr[8 + FF_KEEP + i][:, :] for i in range(FF_KEEP)]
        n_fin2 = add_norm(Hp, "final_norm", Hp, Wp[22:25], 8, take(2))

        for m in range(16):
            emptied[U_QKV[m]] = (qkv_ready, m + 1)
        for m in range(8):
            emptied[U_VT[m]], emptied[U_V[m]] = (vT_ready, m + 1), (qkv_ready, 16 + m + 1)
        for u in range(NU):
            emptied[use_s[u]], emptied[use_t[u]], emptied[use_o[u]] = (scores_ready, u + 1), (pT_ready, u + 1), (heads_done, u + 1)
        for i in range(NT):
            emptied[use_f[i]] = (f_ready, i + 1)
        emptied[P_ROUTE], emptied[P_RANK] = (gdiff_ready, 1), (rank_read, 1)
        for b in range(NBLK):
            emptied[use_x[b]], emptied[use_g[b]] = (xT_ready, b + 1), (up_ready, b + 1)
            emptied[use_h[b]], emptied[use_y[b]] = (hT_ready, b + 1), (y_ready, b + 1)
        for m in range(8):
            emptied[P_OUT + m] = (h_ready, m + 1)
            emptied[P_XTM + m] = (xtm_ready, m + 1)
            emptied[P_YSUM + m] = (ysum_ready, m + 1)
            emptied[P_OUT2 + m] = (h_ready, 8 + m + 1)
            for g in range(4):
                emptied[P_DOWN[g] + m] = (h_ready, 16 + 8 * g + m + 1)
            emptied[P_KV + m] = (state_ready, m + 1)
            emptied[P_BU[m]] = emptied[P_BU[m] + 1] = (s5in_ready, m + 1)
            emptied[P_CX[m]] = (s5y_ready, m + 1)
        for m in range(19):
            emptied[MAIN[m]] = (in2_ready, m + 1)
        for m in range(2):
            emptied[P_S5T + m] = (s5bT_ready, m + 1)
            emptied[P_GLU + m] = (s5s_ready, m + 1)
            emptied[P_GK + m] = (gk_biased, m + 1)
            emptied[P_KLT + m] = (klT_ready, m + 1)
        for m in range(4):
            emptied[P_RG[m]] = (gates_ready, m + 1)
            emptied[P_SC + m] = (intra_ready, m + 1)
            emptied[P_O[m]] = (o_ready, m + 1)
        for j in range(FF):
            emptied[P_UP[j]] = (conv1_ready, j + 1)
            emptied[P_UP[j] + 1] = (prod_ready, j + 1)
        unit_use = U_QKV + U_VT + [P_OUT + m for m in range(8)]
        unit_use += MAIN[0:16] + MAIN[17:19]
        unit_use += [P_OUT2 + m for m in range(8)]
        for what, i in FFN_STEPS:
            unit_use += [P_UP[i], P_UP[i] + 1] if what == "up" else [P_DOWN[i] + m for m in range(8)]

        Mp = Wp[25:29]

        PG_U, PG_RX, PG_RG, PG_Q, PG_K, PG_V, PG_G = 0, 2, 4, 6, 8, 10, 14

        def pair(p0):
            return W[:, p0:p0 + 2, :]

        EC, ES, TA, TB = [Wp[19], Wp[21]], [Wp[20], Wp[22]], Wp[23], Wp[24]
        VR, VI, QA, QB = [Wp[25], Wp[10]], [Wp[26], Wp[11]], Wp[12], Wp[13]
        BT, YS = [Wp[27], Wp[28]], [Wp[4], Wp[5]]
        cmat = Wp[18][:, 0:512].rearrange("p (c j n) -> p c j n", c=2, j=8)
        block = ctx.enter_context(nc.Block())

        ZERO = hT[:, 1, S - P:S]
        RV = {"L": (0, 160), "gd": (160, 32), "oh": (192, 32), "gm": (224, 8), "gw": (232, 8), "v4": (240, 32),
              "o1": (272, 32), "o2": (304, 32), "m1": (336, 8), "m2": (344, 8), "d1": (352, 8), "w1": (360, 8),
              "w2": (368, 8), "t4": (376, 32), "v4b": (408, 32), "c4": (440, 32), "tm": (472, 8), "gs": (480, 8),
              "t5": (488, 32), "nblk": (520, 16), "ends": (536, 16), "start": (552, 16), "fe": (568, NBLK), "fq": (600, NBLK),
              "s1": (640, 128), "s2": (768, 128), "member": (896, 128), "p1": (1024, 8), "p2": (1032, 8),
              "p1i": (1040, 8), "p2i": (1048, 8), "wait_i": (1056, NBLK), "page_i": (1088, NBLK), "ends_i": (1120, 16),
              "tot": (1152, 128), "base": (1280, 144), "cmp": (1424, 16 * NBLK), "ntok": (1936, 16)}
        routing = W[:, 8:10, :].rearrange("p a b -> p (a b)")

        def R(name):
            a, n = RV[name]
            return routing[:, a:a + n]

        XB = [Wp[10], Wp[11]]
        XT = [Wp[12], Bp[6]]
        SG = [Wp[0][:, 0:F_EXP], Wp[0][:, F_EXP:2 * F_EXP]]
        HA = [Wp[0][:, 2 * F_EXP:3 * F_EXP], Wp[0][:, 3 * F_EXP:4 * F_EXP]]
        HAT = [Wp[1][:, 0:F_EXP], Wp[1][:, F_EXP:2 * F_EXP]]
        YB = [Wp[2], Wp[3], Wp[4]]
        xw = W[:, 13:13 + XBUF * XPG, :].rearrange("p a b -> p (a b)")
        YG = [Wp[13 + i] for i in range(4)]

        @block.sync
        def _(sp):
            def experts():
                for e in range(N_EXP):
                    if e == 0:
                        sp.wait_ge(mm_done, done(P_OUT + 7))
                        sp.wait_ge(heads_done, NU)
                    if e == 1:
                        sp.wait_ge(normed, n_ffn["index"] + 1)
                    if e == 2:
                        sp.wait_ge(mm_done, done(P_RANK - 1))
                    if e >= XBUF:
                        if e == XBUF:
                            sp.wait_ge(dispatch_ready, 1)
                        sp.wait_ge(blocks_done, sp.value_load(R("ends_i")[0:1, e - XBUF:e - XBUF + 1].bitcast(i32), min_val=1, max_val=NBLK + 1))
                    sp.dma_start(xw[:, (e % XBUF) * XPG * S:(e % XBUF + 1) * XPG * S], w_moe[e]).then_inc(expert_dma[e % XBUF], 16)
                    if e >= 1:
                        sp.wait_ge(expert_dma[(e - 1) % XBUF], 16 * ((e - 1) // XBUF + 1))
                        sp.sem_inc(expert_loaded, 1)
                sp.wait_ge(expert_dma[(N_EXP - 1) % XBUF], 16 * ((N_EXP - 1) // XBUF + 1))
                sp.sem_inc(expert_loaded, 1)

            for i in range(4):
                sp.dma_start(hT[:, 2 * i:2 * i + 2, :], xT[:, 2 * i:2 * i + 2, :]).then_inc(x_loaded[i], 16)
                if i == 0:
                    sp.dma_start(cst[:], params).then_inc(cst_loaded, 16)
            for u, src in enumerate(units):
                if u == U_IN2 + RING:
                    experts()
                if u == U_OUT + 2:
                    sp.wait_ge(zero_set, 1)
                    for b in range(NBLK):
                        sp.wait_ge(scores_ready, NU // (NBLK + 1) * (b + 1))
                        sp.dma_start(x_slots[b * P:(b + 1) * P, :].rearrange("p (k n) -> p k n", n=P), ZERO.unsqueeze(1).to_broadcast([P, NT, P])).then_inc(slots_zeroed, 16)
                if u == U_OUT + 2:
                    sp.wait_ge(mm_done, done(use_s[NU - 1]))
                if u >= RING and u - RING in split_of:
                    sp.wait_ge(wlo_ready, split_of[u - RING] + 1)
                elif u >= RING:
                    sp.wait_ge(mm_done, done(unit_use[u - RING]))
                sp.dma_start(ring[:, u % RING, 0:src.shape[-1]], src).then_inc(w_loaded[u % RING], 16)
            for t in range(NT):
                sp.wait_ge(xn_ready, n_fin2["xn0"] + t + 1)
                sp.dma_start(out[:, t, :], hT[:, t, :]).then_inc(out_stored, 16)
            sp.wait_ge(out_stored, 16 * NT)

        STRIPS = [hT[:, 0:2, :].rearrange("p a b -> p (a b)")[:, 0:STRIP],
                  hT[:, 2:4, :].rearrange("p a b -> p (a b)")[:, 0:STRIP]]
        SB = [hT[:, 4, :], hT[:, 5, :], W[:, 24, :]]
        PT = [hT[:, 6, :], hT[:, 7, :]]

        @block.gpsimd
        def _(pool):
            pool.memset(epsc[:], EPS).then_inc(eps_set, 1)
            pool.memset(zeros[:], 0.0).then_inc(eps_set, 1)

            def split(n):
                u = split_units[n]
                cols = units[u].shape[-1]
                pool.wait_ge(w_loaded[u % RING], 16 * (u // RING + 1))
                if n >= 2:
                    pool.wait_ge(mm_done, done(unit_use[split_units[n - 2]]))
                w = ring[:, u % RING, 0:cols]
                pool.tensor_copy(WHI[n % 2][:, 0:cols], w).then_inc(whi_ready, 1)
                pool.wait_ge(whi_ready, n + 1)
                pool.tensor_tensor(WLO[n % 2][:, 0:cols], w, WHI_F[n % 2][:, 0:cols], ALU.subtract).then_inc(wlo_ready, 1)

            for n in range(24):
                split(n)
            for h in range(NH):
                own, other = (slice(0, DH), slice(DH, P)) if h % 2 == 0 else (slice(DH, P), slice(0, DH))
                q, k = Wp[h // 2], Wp[8 + h // 2]
                if h == 0:
                    pool.wait_ge(qkv_ready, 16)
                    pool.wait_ge(mm_done, done(U_VT[6]))
                if h >= 1:
                    pool.wait_ge(qk_parts, 6 * h)
                if h >= 2:
                    pool.wait_ge(mm_done, done(use_s[NT * (h - 1) - 1]))
                pool.tensor_copy(QS[h % 2][own, :], q[own, :]).then_inc(qk_parts, 1)
                pool.tensor_copy(KH[h % 2][own, :], k[own, :]).then_inc(qk_parts, 1)
                pool.wait_ge(qk_parts, 6 * h + 2)
                pool.tensor_tensor(QS[h % 2][other, :], q[own, :], QS[h % 2][own, :].bitcast(f32), ALU.subtract).then_inc(qk_parts, 1)
                pool.tensor_tensor(KL[h % 2][own, :], k[own, :], KH[h % 2][own, :].bitcast(f32), ALU.subtract).then_inc(qk_parts, 1)
                pool.tensor_tensor(KL[h % 2][other, :], k[own, :], KH[h % 2][own, :].bitcast(f32), ALU.subtract).then_inc(qk_parts, 1)
                pool.tensor_copy(KH[h % 2][other, :], k[own, :]).then_inc(qk_parts, 1)
                if h == 0:
                    pool.wait_ge(mm_done, done(U_VT[7]))
                    pool.wait_ge(qk_parts, 6)
                    pool.memset(ZERO, 0.0).then_inc(zero_set, 1)
                    pool.wait_ge(zero_set, 1)
                if h >= 2:
                    pool.wait_ge(scores_ready, NT * (h - 1))
                if h < 8:
                    pool.dma_start(STRIPS[h % 2], dil_strip[h]).then_inc(strip_loaded[h % 2], 16)
                else:
                    pool.dma_start(STRIPS[h % 2][:, 0:NF + NI], na_strip[h - 8]).then_inc(strip_loaded[h % 2], 16)
            pool.wait_ge(slots_zeroed, 16 * NBLK)
            pool.wait_ge(mm_done, done(use_s[NU - 1]))
            pool.wait_ge(qk_parts, 6 * NH)
            split(24)
            split(25)
            pool.wait_ge(heads_done, NU)
            pool.dma_start(hT[:], xT).then_inc(x_again, 16)
            for n in range(26, 32):
                split(n)
            pool.wait_ge(dispatch_ready, 1)
            for tt in range(NT):
                pool.wait_ge(xtm_ready, tt + 1)
                for name in ("p1i", "p2i"):
                    pool.indirect_dma_start(x_slots, bass.IndirectOffsetOnAxis(ap=R(name)[:, tt:tt + 1].bitcast(u32), axis=0),
                                            Wp[tt], None, bounds_check=NBLK * P - 1, oob_is_err=True).then_inc(x_scattered, 16)
            pool.wait_ge(x_scattered, 16 * 2 * NT)
            for b in range(NBLK):
                if b >= 2:
                    pool.wait_ge(mm_done, done(use_x[b - 2]))
                pool.dma_start(XB[b % 2], x_slots[b * P:(b + 1) * P, :]).then_inc(block_loaded[b % 2], 16)
            for i in range(3):
                pool.wait_ge(y_stored[i], 16 * ((NBLK - i + 2) // 3))
            pool.wait_ge(mm_done, done(use_y[NBLK - 1]))
            for tt in range(NT):
                for r, name in enumerate(("p1i", "p2i")):
                    k = (2 * tt + r) % 4
                    if tt >= 2:
                        pool.wait_ge(ysum_ready, tt - 1)
                    pool.indirect_dma_start(YG[k], None, y_slots, bass.IndirectOffsetOnAxis(ap=R(name)[:, tt:tt + 1].bitcast(u32), axis=0),
                                            bounds_check=NBLK * P - 1, oob_is_err=True).then_inc(y_gathered[k], 16)
            pool.wait_ge(ysum_ready, NT)
            pool.dma_start(W[:, 10:12, :], s5_b).then_inc(s5_loaded, 16)
            pool.dma_start(Wp[18][:, 0:512], s5_c).then_inc(s5_loaded, 16)
            links = [0]

            def link(ins):
                links[0] += 1
                ins.then_inc(pool_link, 1)
                pool.wait_ge(pool_link, links[0])
            for j in range(8):
                vr, vi, ec, es = VR[j % 2], VI[j % 2], EC[j % 2], ES[j % 2]
                pool.wait_ge(s5v_ready, j + 1)
                if j >= 1:
                    pool.wait_ge(s5x_ready, j)
                pool.tensor_tensor(QA, vi, es, ALU.mult)
                link(pool.tensor_tensor(QB, vr, es, ALU.mult))
                pool.tensor_tensor(vr, vr, ec, ALU.mult)
                link(pool.tensor_tensor(vi, vi, ec, ALU.mult))
                pool.tensor_tensor(vr, vr, QA, ALU.subtract)
                pool.tensor_tensor(vi, vi, QB, ALU.add).then_inc(s5x_ready, 1)
            pool.wait_ge(mm_done, done(P_O[3]))
            for n in range(32, len(split_units)):
                split(n)

        @block.tensor
        def _(pe):
            def slot(n):
                if n >= SLOTS:
                    pe.wait_ge(*emptied[n - SLOTS])
                return PS[n % SLOTS]

            def unit(u):
                pe.wait_ge(w_loaded[u % RING], 16 * (u // RING + 1))
                return ring[:, u % RING, :]

            def column_tile(u, n, rhs, kt=NT):
                ps, w = slot(n), unit(u)
                for half in range(2):
                    for k in range(kt):
                        mm = pe.matmul(ps[:, half * HALF:(half + 1) * HALF], w[:, k * P:(k + 1) * P],
                                       rhs[k][:, half * HALF:(half + 1) * HALF], start=(k == 0), stop=(k == kt - 1))
                        if half == 1 and k == kt - 1:
                            mm.then_inc(mm_done, 1)

            def first_pair(u, n0, n1, hi, ready, base, lo=None):
                pss = [slot(n0), slot(n1)]
                if lo is None:
                    ws = [(unit(u + i), None) for i in range(2)]
                else:
                    pe.wait_ge(wlo_ready, split_of[u + 1] + 1)
                    ws = [(WHI[split_of[u + i] % 2], WLO[split_of[u + i] % 2]) for i in range(2)]
                last = len(hi) - 1
                for k in range(len(hi)):
                    pe.wait_ge(ready, base + k + 1)
                    w = slice(k * P, (k + 1) * P)
                    for i in range(2):
                        for half in range(2):
                            c = slice(half * HALF, (half + 1) * HALF)
                            mm = pe.matmul(pss[i][:, c], ws[i][0][:, w], hi[k][:, c], start=(k == 0), stop=(lo is None and k == last))
                            if lo is not None:
                                pe.matmul(pss[i][:, c], ws[i][0][:, w], lo[k][:, c], start=False, stop=False)
                                mm = pe.matmul(pss[i][:, c], ws[i][1][:, w], hi[k][:, c], start=False, stop=(k == last))
                        if k == last:
                            mm.then_inc(mm_done, 1)

            def parts_tile(u, n, hi, lo, ready=None, base=0):
                ps, s = slot(n), split_of[u]
                pe.wait_ge(wlo_ready, s + 1)
                whi, wlo = WHI[s % 2], WLO[s % 2]
                for half in range(2):
                    c = slice(half * HALF, (half + 1) * HALF)
                    for k in range(len(hi)):
                        if ready is not None and half == 0:
                            pe.wait_ge(ready, base + k + 1)
                        w = slice(k * P, (k + 1) * P)
                        pe.matmul(ps[:, c], whi[:, w], hi[k][:, c], start=(k == 0), stop=False)
                        pe.matmul(ps[:, c], whi[:, w], lo[k][:, c], start=False, stop=False)
                        mm = pe.matmul(ps[:, c], wlo[:, w], hi[k][:, c], start=False, stop=(k == len(hi) - 1))
                mm.then_inc(mm_done, 1)

            def token_tile(u, n, lhs):
                ps, w = slot(n), unit(u)
                for tt in range(NT):
                    for k in range(NT):
                        mm = pe.matmul(ps[:, tt * P:(tt + 1) * P], lhs[k][:, tt * P:(tt + 1) * P],
                                       w[:, k * P:(k + 1) * P], start=(k == 0), stop=(k == NT - 1))
                mm.then_inc(mm_done, 1)

            def norm_sum(c):
                ps = slot(c["use"])
                pe.matmul(ps[:, 0:NT], ones, zeros[:], start=True, stop=False)
                for t in range(c["tiles"]):
                    pe.wait_ge(sq_ready, c["sq0"] + t + 1)
                    for tt in range(NT):
                        mm = pe.matmul(ps[:, tt:tt + 1], c["scratch"][t % 2][:, tt * P:(tt + 1) * P], ones[:, 0:1],
                                       start=False, stop=(t == c["tiles"] - 1 and tt == NT - 1))
                    mm.then_inc(sq_used, 1)

            def norm_root(c):
                pe.wait_ge(inverse_ready, c["index"] + 1)
                ps = slot(c["root_use"])
                for half in range(2):
                    mm = pe.matmul(ps[:, half * HALF:(half + 1) * HALF], ones, c["scratch"][2][:, half * HALF:(half + 1) * HALF],
                                   start=True, stop=True)
                mm.then_inc(root_spread, 1)

            def norm(c):
                norm_sum(c)
                norm_root(c)

            pe.wait_ge(cst_loaded, 16)
            pe.wait_ge(eps_set, 2)
            norm(n_mix)
            first_pair(U_IN, U_QKV[0], U_QKV[1], BHI, xlo_ready, n_mix["lo0"], n_mix["parts"][1])
            for m in range(2, 16):
                parts_tile(U_IN + m, U_QKV[m], *n_mix["parts"])
            for m in range(9):
                if m < 8:
                    parts_tile(U_IN + 16 + m, U_VT[m], *n_mix["parts"])
                if m >= 1:
                    pe.wait_ge(vT_ready, m)
                    ps = slot(U_V[m - 1])
                    for tt in range(NT):
                        mm = pe.transpose(ps[:, tt * P:(tt + 1) * P], Wp[24][:, tt * P:(tt + 1) * P], ident)
                    mm.then_inc(mm_done, 1)

            def scores(u):
                h, i = u // NT, u % NT
                k0, k1 = key_tiles(h, i)
                ps = slot(use_s[u])
                pe.wait_ge(qk_parts, 6 * (h + 1))
                n = (k1 - k0) * P
                w = n if n <= HALF else n // 2
                for b in range(n // w):
                    c0 = k0 * P + b * w
                    for part in (KH, KL):
                        mm = pe.matmul(ps[:, b * HALF:b * HALF + w], QS[h % 2][:, i * P:(i + 1) * P],
                                       part[h % 2][:, c0:c0 + w], start=(part is KH), stop=(part is KL))
                mm.then_inc(mm_done, 1)

            def turn(u):
                k0, k1 = key_tiles(u // NT, u % NT)
                pe.wait_ge(exp_done, u + 1)
                ps = slot(use_t[u])
                for j in range(k1 - k0):
                    mm = pe.transpose(ps[:, j * P:(j + 1) * P], SB[u % 3][:, j * P:(j + 1) * P], ident)
                mm.then_inc(mm_done, 1)

            def mix(u):
                h = u // NT
                k0, k1 = key_tiles(h, u % NT)
                pe.wait_ge(pT_ready, u + 1)
                ps = slot(use_o[u])
                for j in range(k1 - k0):
                    mm = pe.matmul(ps[:, 0:DH], PT[u % 2][:, j * P:(j + 1) * P], Wp[16 + k0 + j][:, h * DH:(h + 1) * DH],
                                   start=(j == 0), stop=(j == k1 - k0 - 1))
                mm.then_inc(mm_done, 1)

            def turn_out(i):
                pe.wait_ge(heads_done, NU - NT + i + 1)
                ps = slot(use_f[i])
                for k in range(NT):
                    mm = pe.transpose(ps[:, k * P:(k + 1) * P], Bp[i][:, k * P:(k + 1) * P], ident)
                mm.then_inc(mm_done, 1)

            pe.wait_ge(qkv_ready, 24)
            for t in range(NU + LAG_F):
                if t < NU:
                    scores(t)
                if 0 <= t - LAG_T < NU:
                    turn(t - LAG_T)
                if 0 <= t - LAG_O < NU:
                    mix(t - LAG_O)
                if NU - NT <= t - LAG_F:
                    turn_out(t - LAG_F - (NU - NT))
            norm_sum(n_dil)
            norm_sum(n_na)
            norm_root(n_dil)
            norm_root(n_na)
            first_pair(U_OUT, P_OUT, P_OUT + 1, YHI, xlo_ready, n_dil["lo0"], YLO)
            for m in range(2, 8):
                parts_tile(U_OUT + m, P_OUT + m, YHI, YLO)
            norm(n_ffn)
            pe.wait_ge(normed, n_ffn["index"] + 1)
            ps = slot(P_ROUTE)
            for tt in range(NT):
                for k in range(NT):
                    mm = pe.matmul(ps[:, tt * 20:(tt + 1) * 20], Bp[k][:, tt * P:(tt + 1) * P],
                                   mat("route", k * 20, 20), start=(k == 0), stop=(k == NT - 1))
            mm.then_inc(mm_done, 1)
            for tt in range(NT):
                ps = slot(P_XTM + tt)
                for k in range(NT):
                    mm = pe.transpose(ps[:, k * P:(k + 1) * P], Bp[k][:, tt * P:(tt + 1) * P], ident)
                mm.then_inc(mm_done, 1)
            pe.wait_ge(member_ready, 1)
            ps = slot(P_RANK)
            pe.matmul(ps[:, 0:P], mat("before"), R("member"), start=True, stop=True)
            pe.matmul(ps[:, HALF:HALF + P], ones, R("member"), start=True, stop=True).then_inc(mm_done, 1)

            pe.wait_ge(dispatch_ready, 1)
            pages = {}

            def block_x(b):
                pe.wait_ge(block_loaded[b % 2], 16 * (b // 2 + 1))
                ps = slot(use_x[b])
                for k in range(NT):
                    mm = pe.transpose(ps[:, k * P:(k + 1) * P], XB[b % 2][:, k * P:(k + 1) * P], ident)
                mm.then_inc(mm_done, 1)

            def block_g(b):
                pages[b] = pe.value_load(R("page_i")[0:1, b:b + 1].bitcast(i32), min_val=0, max_val=2 * XPG * S)
                pe.wait_ge(expert_loaded, pe.value_load(R("wait_i")[0:1, b:b + 1].bitcast(i32), min_val=1, max_val=N_EXP))
                pe.wait_ge(xT_ready, b + 1)
                ps = slot(use_g[b])
                for k in range(NT):
                    mm = pe.matmul(ps[:, 0:HALF], XT[b % 2][:, k * P:(k + 1) * P], xw[:, bass.ds(pages[b] + k * HALF, HALF)],
                                   start=(k == 0), stop=(k == NT - 1))
                mm.then_inc(mm_done, 1)

            def block_h(b):
                pe.wait_ge(up_ready, b + 1)
                ps = slot(use_h[b])
                for f in range(2):
                    mm = pe.transpose(ps[:, f * P:(f + 1) * P], HA[b % 2][:, f * P:(f + 1) * P], ident)
                mm.then_inc(mm_done, 1)

            def block_y(b):
                pe.wait_ge(hT_ready, b + 1)
                ps = slot(use_y[b])
                for half in range(2):
                    for f in range(2):
                        mm = pe.matmul(ps[:, half * HALF:(half + 1) * HALF], HAT[b % 2][:, f * P:(f + 1) * P],
                                       xw[:, bass.ds(pages[b] + 4 * S + f * S + half * HALF, HALF)], start=(f == 0), stop=(f == 1))
                mm.then_inc(mm_done, 1)

            for t in range(NBLK + 2):
                for lag, stage in ((0, block_x), (1, block_g), (2, block_y), (1, block_h)):
                    if 0 <= t - lag < NBLK:
                        stage(t - lag)
            for tt in range(NT):
                pe.wait_ge(ysum_added, tt + 1)
                ps = slot(P_YSUM + tt)
                for k in range(NT):
                    mm = pe.transpose(ps[:, k * P:(k + 1) * P], YG[(2 * tt + 1) % 4][:, k * P:(k + 1) * P], ident)
                mm.then_inc(mm_done, 1)
            norm(n_fin1)
            norm(n_att2)
            main = [0]

            def project(count=1):
                for _ in range(count):
                    m = main[0]
                    main[0] += 1
                    if m < 14:
                        column_tile(U_IN2 + m, MAIN[m], Bp)
                    elif m != 16:
                        token_tile(U_IN2 + m - (m > 16), MAIN[m], Bp)
                    else:
                        ps = slot(MAIN[m])
                        for half in range(2):
                            for k in range(NT):
                                mm = pe.matmul(ps[0:16, half * HALF:(half + 1) * HALF], mat("low", k * 16, 16),
                                               Bp[k][:, half * HALF:(half + 1) * HALF], start=(k == 0), stop=(k == NT - 1))
                        mm.then_inc(mm_done, 1)

            first_pair(U_IN2, MAIN[0], MAIN[1], Bp, xn_ready, n_att2["xn0"])
            main[0] = 2
            project(1)
            for c in range(2):
                pe.wait_ge(conv_ready, c + 1)
                for gate in range(2):
                    ps = slot(P_RG[2 * c + gate])
                    for half in range(2):
                        mm = pe.matmul(ps[:, half * HALF:(half + 1) * HALF], mat("rg", (2 * gate + c) * P),
                                       Wp[19 + c][:, half * HALF:(half + 1) * HALF], start=True, stop=True)
                    mm.then_inc(mm_done, 1)
            project(1)
            pe.wait_ge(s5b_ready, 1)
            for c in range(2):
                ps = slot(P_S5T + c)
                for j in range(8):
                    mm = pe.transpose(ps[:, j * P:(j + 1) * P], Wp[10 + c][:, j * P:(j + 1) * P], ident)
                mm.then_inc(mm_done, 1)
            project(2)
            pe.wait_ge(s5bT_ready, 2)
            for j in range(9):
                if j < 8:
                    pe.wait_ge(in2_ready, 4)
                    for c in range(2):
                        ps = slot(P_BU[j] + c)
                        for half in range(2):
                            mm = pe.matmul(ps[:, half * HALF:(half + 1) * HALF], BT[c][:, j * P:(j + 1) * P],
                                           Wp[PG_U + j // 4][:, half * HALF:(half + 1) * HALF], start=True, stop=True)
                        mm.then_inc(mm_done, 1)
                if j < 8:
                    project()
                if j >= 1:
                    i = j - 1
                    pe.wait_ge(s5x_ready, i + 1)
                    pe.wait_ge(s5c_ready, 1)
                    r = 32 * (i % 4)
                    ps = slot(P_CX[i])
                    for half in range(2):
                        for c, x in enumerate((VR[i % 2], VI[i % 2])):
                            mm = pe.matmul(ps[r:r + 32, half * HALF:(half + 1) * HALF], cmat[:, c, i, :],
                                           x[:, half * HALF:(half + 1) * HALF], start=(c == 0), stop=(c == 1))
                    mm.then_inc(mm_done, 1)
            project(2)
            pe.wait_ge(s5g_ready, 2)
            for m in range(2):
                ps = slot(P_GLU + m)
                for half in range(2):
                    for k in range(2):
                        mm = pe.matmul(ps[:, half * HALF:(half + 1) * HALF], mat("glu", k * 256 + m * P),
                                       Wp[k][:, half * HALF:(half + 1) * HALF], start=(k == 0), stop=(k == 1))
                mm.then_inc(mm_done, 1)
            project(1)
            norm_sum(n_rg)
            norm_sum(n_s5)

            pe.wait_ge(in2_ready, 17)
            for m in range(2):
                ps = slot(P_GK + m)
                for half in range(2):
                    mm = pe.matmul(ps[:, half * HALF:(half + 1) * HALF], cst[0:16, MCOLS["gkup"] + m * P:MCOLS["gkup"] + (m + 1) * P],
                                   Wp[5][0:16, half * HALF:(half + 1) * HALF], start=True, stop=True)
                mm.then_inc(mm_done, 1)
            norm_root(n_rg)
            norm_root(n_s5)
            project(2)
            pe.wait_ge(gprods, 1)
            for m in range(2):
                ps = slot(P_KLT + m)
                for tt in range(NT):
                    mm = pe.transpose(ps[:, tt * P:(tt + 1) * P], Wp[PG_K + m][:, tt * P:(tt + 1) * P], ident)
                mm.then_inc(mm_done, 1)
            vv = W[:, PG_V:PG_V + 4, :].rearrange("p a (b c) -> p (a b) c", c=HALF)
            for m in range(2):
                pe.wait_ge(klT_ready, m + 1)
                for q4 in range(4):
                    ps = slot(P_KV + 4 * m + q4)
                    for j in range(4):
                        n = 4 * q4 + j
                        r0, tt = (n % 2) * CH, n // 2
                        c0 = (j % 2) * HALF + (j // 2) * 256
                        mm = pe.matmul(ps[:, c0:c0 + 256], Wp[21 + m][r0:r0 + CH, tt * P:(tt + 1) * P],
                                       vv[r0:r0 + CH, tt, m * 256:(m + 1) * 256], start=True, stop=True)
                    mm.then_inc(mm_done, 1)
            for h in range(4):
                m, r0 = h // 2, (h % 2) * DH
                ps = slot(P_SC + h)
                for tt in range(NT):
                    mm = pe.matmul(ps[:, tt * P:(tt + 1) * P], Wp[19 + m][r0:r0 + DH, tt * P:(tt + 1) * P],
                                   Wp[4 + m][r0:r0 + DH, tt * P:(tt + 1) * P], start=True, stop=True)
                mm.then_inc(mm_done, 1)
            states = [pair(23).rearrange("p a (b c) -> p (a b) c", c=P), pair(8).rearrange("p a (b c) -> p (a b) c", c=P)]
            pe.wait_ge(in2_ready, 19)
            pe.wait_ge(state_ready, 8)
            for what, h in GLA_STEPS:
                if what == "sum":
                    norm_sum(n_gla[h])
                    continue
                if what == "root":
                    norm_root(n_gla[h])
                    continue
                m, r0 = h // 2, (h % 2) * DH
                pe.wait_ge(intra_ready, h + 1)
                ps = slot(P_O[h])
                for tt in range(NT):
                    o = ps[:, tt * P:(tt + 1) * P]
                    mm = pe.matmul(o, vv[:, tt, h * P:(h + 1) * P], Mp[h][:, tt * P:(tt + 1) * P], start=True, stop=False)
                    for c in range(2):
                        n = 2 * tt + c
                        if n == 0:
                            continue
                        mm = pe.matmul(ps[:, n * CH:(n + 1) * CH], states[m][r0:r0 + DH, n, :],
                                       Wp[PG_Q + m][r0:r0 + DH, n * CH:(n + 1) * CH], start=False, stop=(c == 1))
                mm.then_inc(mm_done, 1)
            pe.wait_ge(gla_ready, 4)
            for m in range(8):
                column_tile(U_OUT2 + m, P_OUT2 + m, Bp[0:4] + Wp[0:4])
            norm(n_mlp)
            u = U_UP
            for what, i in FFN_STEPS:
                if what == "up":
                    if i == 0:
                        first_pair(u, P_UP[i], P_UP[i] + 1, BHI, xlo_ready, n_mlp["lo0"], XLO)
                    else:
                        for n in range(2):
                            parts_tile(u + n, P_UP[i] + n, BHI, XLO)
                    u += 2
                else:
                    group = FF_GROUPS[i]
                    hi, lo = [FHI[j % FF_KEEP] for j in group], [FLO[j % FF_KEEP] for j in group]
                    for m in range(8):
                        parts_tile(u + m, P_DOWN[i] + m, hi, lo, ffact_ready if m == 0 else None, group[0])
                    u += 8
            norm(n_fin2)


        @block.scalar
        def _(act):
            links = [0]

            def link(ins):
                links[0] += 1
                ins.then_inc(act_link, 1)
                act.wait_ge(act_link, links[0])

            def norm_squares(c, gate=None):
                for t in range(c["tiles"]):
                    if gate is not None:
                        gate(t)
                    if c["sq0"] + t >= 2:
                        act.wait_ge(sq_used, c["sq0"] + t - 1)
                    act.activation(c["scratch"][t % 2], c["src"][t], ACT.Square).then_inc(sq_ready, 1)

            def norm_std(c):
                act.wait_ge(sq_used, c["sq0"] + c["tiles"])
                if c["index"] >= 4:
                    act.wait_ge(inverse_ready, c["index"] - 3)
                act.activation(std[:, c["index"] % 4, :], PS[c["use"] % SLOTS][:, 0:NT], ACT.Sqrt, bias=epsc[:],
                               scale=1.0 / (P * c["tiles"])).then_inc(std_ready, 1)

            def norm(c, gate=None):
                norm_squares(c, gate)
                norm_std(c)

            def norm_parts(c):
                for t in range(c["tiles"]):
                    act.wait_ge(xn_ready, c["xn0"] + t + 1)
                    act.activation(c["parts"][0][t], c["dst"][t], ACT.Copy).then_inc(xhi_ready, 1)

            act.wait_ge(eps_set, 1)

            def x_gate(t):
                if t % 2 == 0:
                    act.wait_ge(x_loaded[t // 2], 16)
            norm(n_mix, x_gate)
            norm_parts(n_mix)
            act.wait_ge(normed, 1)
            for m in range(24):
                if m >= 16:
                    if m > 16:
                        act.wait_ge(mm_done, done(U_V[m - 17]))
                    act.wait_ge(mm_done, done(U_VT[m - 16]))
                    act.activation(Wp[24], PS[U_VT[m - 16] % SLOTS][:, :], ACT.Copy).then_inc(vT_ready, 1)
                n = U_QKV[m] if m < 16 else U_V[m - 16]
                act.wait_ge(mm_done, done(n))
                ps = PS[n % SLOTS]
                if m < 16:
                    dst, src = Wp[m], ps[:, :]
                else:
                    dst = W[:, 16:24, (m - 16) * P:(m - 15) * P]
                    src = ps[:, :].rearrange("p (a b) -> p a b", a=NT)
                act.activation(dst, src, ACT.Copy, scale=DH ** -0.5 if m < 8 else 1.0).then_inc(qkv_ready, 1)

            def expo(u):
                k0, k1 = key_tiles(u // NT, u % NT)
                act.wait_ge(scores_ready, u + 1)
                s = SB[u % 3][:, 0:(k1 - k0) * P]
                act.activation(s, s, ACT.Exp, bias=negm[:, u % 4:u % 4 + 1], scale=-1.0,
                               accum_out=den[:, u % 8:u % 8 + 1]).then_inc(exp_done, 1)

            def copy_pT(u):
                k0, k1 = key_tiles(u // NT, u % NT)
                n = use_t[u]
                act.wait_ge(mm_done, done(n))
                if u >= 2:
                    act.wait_ge(mm_done, done(use_o[u - 2]))
                act.activation(PT[u % 2][:, 0:(k1 - k0) * P], PS[n % SLOTS][:, 0:(k1 - k0) * P], ACT.Copy).then_inc(pT_ready, 1)

            def copy_f(i):
                act.wait_ge(mm_done, done(use_f[i]))
                ps = PS[use_f[i] % SLOTS]
                act.activation(W[:, 0:7, i * P:(i + 1) * P], ps[:, 0:7 * P].rearrange("p (k n) -> p k n", n=P), ACT.Copy)
                act.activation(Wp[14][:, i * P:(i + 1) * P], ps[:, 7 * P:8 * P], ACT.Copy).then_inc(f_ready, 1)

            for t in range(NU + LAG_F):
                if t < NU:
                    expo(t)
                if 0 <= t - LAG_T < NU:
                    copy_pT(t - LAG_T)
                if NU - NT <= t - LAG_F:
                    copy_f(t - LAG_F - (NU - NT))

            def heads_gate(t):
                act.wait_ge(f_ready, NT)
            norm(n_dil, heads_gate)
            norm(n_na, heads_gate)
            norm_parts(n_dil)
            norm_parts(n_na)

            def h_gate(t):
                act.wait_ge(h_ready, t + 1)
            norm(n_ffn, h_gate)
            act.wait_ge(gdiff_ready, 1)
            act.activation(R("gd"), R("gd"), ACT.Exp).then_inc(gexp_done, 1)
            act.wait_ge(tdiff_ready, 1)
            act.activation(R("d1"), R("d1"), ACT.Exp).then_inc(texp_done, 1)
            for tt in range(NT):
                act.wait_ge(mm_done, done(P_XTM + tt))
                act.activation(Wp[tt], PS[(P_XTM + tt) % SLOTS][:, :], ACT.Copy).then_inc(xtm_ready, 1)
            act.wait_ge(x_scattered, 16 * 2 * NT)

            def block_xT(b):
                act.wait_ge(mm_done, done(use_x[b]))
                if b >= 2:
                    act.wait_ge(mm_done, done(use_g[b - 2]))
                act.activation(XT[b % 2], PS[use_x[b] % SLOTS][:, :], ACT.Copy).then_inc(xT_ready, 1)

            def block_silu(b):
                act.wait_ge(mm_done, done(use_g[b]))
                if b >= 2:
                    act.wait_ge(up_ready, b - 1)
                act.activation(SG[b % 2], PS[use_g[b] % SLOTS][:, 0:F_EXP], ACT.Silu).then_inc(silu_ready, 1)

            def block_store(b):
                act.wait_ge(y_ready, b + 1)
                act.dma_start(y_slots[b * P:(b + 1) * P, :], YB[b % 3]).then_inc(y_stored[b % 3], 16)

            for t in range(NBLK + 3):
                for lag, stage in ((0, block_xT), (1, block_silu), (3, block_store)):
                    if 0 <= t - lag < NBLK:
                        stage(t - lag)

            def moe_gate(t):
                act.wait_ge(ysum_ready, NT)
            norm(n_fin1, moe_gate)

            def fin1_gate(t):
                act.wait_ge(xn_ready, n_fin1["xn0"] + t + 1)
            norm(n_att2, fin1_gate)
            act.wait_ge(normed, n_att2["index"] + 1)
            dsts = [Wp[PG_RX], Wp[PG_RX + 1], Wp[PG_U], Wp[PG_U + 1], Wp[PG_RG], Wp[PG_RG + 1], Wp[PG_Q], Wp[PG_Q + 1],
                    Wp[PG_K], Wp[PG_K + 1]] + [Wp[PG_G + j] for j in range(4)]
            vdst = W[:, PG_V:PG_V + 4, :].rearrange("p a (b c) -> p (a b) c", c=HALF)
            main = [0]

            def take_out(count=1):
                for _ in range(count):
                    m = main[0]
                    main[0] += 1
                    act.wait_ge(mm_done, done(MAIN[m]))
                    ps = PS[MAIN[m] % SLOTS]
                    if m < 14:
                        dst, src = dsts[m], ps[:, :]
                    elif m != 16:
                        v = m - 14 - (m > 16)
                        dst, src = vdst[:, :, v * P:(v + 1) * P], ps[:, :].rearrange("p (a b) -> p a b", a=NT)
                    else:
                        act.wait_ge(s5g_ready, 2)
                        dst, src = Wp[5][0:16, :], ps[0:16, :]
                    act.activation(dst, src, ACT.Copy, scale=DH ** -0.5 if m in (6, 7) else 1.0).then_inc(in2_ready, 1)

            take_out(3)
            for c in range(2):
                for gate in range(2):
                    n = P_RG[2 * c + gate]
                    act.wait_ge(mm_done, done(n))
                    act.activation(Wp[(23 if gate else 21) + c], PS[n % SLOTS][:, :], ACT.Sigmoid,
                                   bias=par("rg_bx" if gate else "rg_ba", c)).then_inc(gates_ready, 1)
                act.wait_ge(gates_ready, 2 * c + 2)
                act.activation(Wp[21 + c], Wp[21 + c], ACT.Tanh, scale=sp4[:, c:c + 1]).then_inc(tanh_ready, 1)

            def rg_root(c):
                act.wait_ge(onep_ready, c + 1)
                act.activation(Wp[21 + c], Wp[21 + c], ACT.Sqrt, scale=4.0).then_inc(root_ready, 1)

            rg_root(0)
            take_out(1)
            for c in range(2):
                act.wait_ge(mm_done, done(P_S5T + c))
                act.activation(BT[c], PS[(P_S5T + c) % SLOTS][:, :], ACT.Copy).then_inc(s5bT_ready, 1)
            take_out(1)
            rg_root(1)
            take_out(1)
            act.wait_ge(in2_ready, 6)
            for c in range(2):
                act.activation(Wp[PG_RG + c], Wp[PG_RG + c], ACT.Gelu_apprx_tanh).then_inc(ggate_ready, 1)
            take_out(8)
            act.wait_ge(s5y_ready, 8)
            for c in range(2):
                act.activation(Wp[c], YS[c], ACT.Gelu_apprx_tanh).then_inc(s5g_ready, 1)
            act.wait_ge(s5x_ready, 8)
            act.wait_ge(mm_done, done(P_CX[7]))
            take_out(2)
            for c in range(2):
                n = P_GLU + c
                act.wait_ge(mm_done, done(n))
                act.activation(Wp[22 - c], PS[n % SLOTS][:, :], ACT.Sigmoid, bias=par("b_glu", c)).then_inc(s5s_ready, 1)
            def rg_gate(t):
                act.wait_ge(rg_ready, 2)
            norm_squares(n_rg, rg_gate)
            take_out(1)

            def s5_gate(t):
                act.wait_ge(s5_ready, 2)
            norm_squares(n_s5, s5_gate)
            norm_std(n_rg)
            norm_std(n_s5)
            act.wait_ge(gk_abs, 2)
            link(act.activation(pair(27), pair(27), ACT.Exp, scale=-1.0))
            act.activation(pair(27), pair(27), ACT.Ln, bias=1.0).then_inc(gk_ln, 1)
            act.wait_ge(bc_ready, 1)
            for k in range(4):
                if k == 3:
                    act.wait_ge(gprods, 1)
                elif k:
                    act.wait_ge(gexps_used, k)
                act.activation(pair(27), pair(27) if k < 3 else pair(25), ACT.Exp).then_inc(gexps, 1)
                if k in (0, 2):
                    take_out(1)
            for m in range(2):
                last = act.activation(decay[:, m, :], Wp[25 + m].rearrange("p (n c) -> p n c", c=CH)[:, :, CH - 1], ACT.Exp)
            last.then_inc(decay_ready, 1)
            for m in range(2):
                n = P_KLT + m
                act.wait_ge(mm_done, done(n))
                act.activation(Wp[21 + m], PS[n % SLOTS][:, :], ACT.Copy).then_inc(klT_ready, 1)
            for h in range(4):
                act.activation(Wp[PG_G + h], Wp[PG_G + h], ACT.Silu).then_inc(gsilu, 1)
            for h in range(5):
                if h < 4:
                    act.wait_ge(mm_done, done(P_O[h]))
                    if h >= 2:
                        act.wait_ge(mm_done, done(P_SC + 3))
                    act.activation(n_gla[h]["src"][0], PS[P_O[h] % SLOTS][:, :], ACT.Copy).then_inc(o_ready, 1)
                    act.wait_ge(o_ready, h + 1)
                    norm_squares(n_gla[h])
                if h >= 1:
                    norm_std(n_gla[h - 1])

            def out2_gate(t):
                act.wait_ge(h_ready, 8 + t + 1)
            norm(n_mlp, out2_gate)
            norm_parts(n_mlp)
            for j in range(FF):
                n = P_UP[j]
                act.wait_ge(mm_done, done(n))
                if j >= 3:
                    act.wait_ge(ffact_ready, j - 2)
                act.activation(Wp[22 + j % 3], PS[n % SLOTS][:, :], ACT.Identity, bias=par("ff_cb", j),
                               scale=par("ff_w", 2 * FF + j)).then_inc(conv0_ready, 1)
                act.wait_ge(conv1_ready, j + 1)
                act.activation(Wp[22 + j % 3], Wp[22 + j % 3], ACT.Gelu_apprx_tanh).then_inc(gelu_ready, 1)
                act.wait_ge(prod_ready, j + 1)
                if j >= FF_KEEP:
                    act.wait_ge(mm_done, done(P_DOWN[group_of[j - FF_KEEP]] + 7))
                act.activation(FHI[j % FF_KEEP], Wp[22 + j % 3], ACT.Copy).then_inc(ffhi_ready, 1)

            def down_gate(t):
                act.wait_ge(h_ready, 16 + 8 * 3 + t + 1)
            norm(n_fin2, down_gate)

        @block.vector
        def _(dve):
            links = [0]

            def link(ins):
                links[0] += 1
                ins.then_inc(dve_link, 1)
                dve.wait_ge(dve_link, links[0])

            def norm_inverse(c):
                r = std[:, c["index"] % 4, :]
                dve.wait_ge(std_ready, c["index"] + 1)
                link(dve.reciprocal(r, r))
                dve.tensor_tensor(c["scratch"][2].rearrange("p (t n) -> p t n", n=P), r.unsqueeze(2).to_broadcast([P, NT, P]),
                                  ident.unsqueeze(1).to_broadcast([P, NT, P]), ALU.mult).then_inc(inverse_ready, 1)

            def norm_apply(c):
                r = PS[c["root_use"] % SLOTS][:, :]
                dve.wait_ge(root_spread, c["index"] + 1)
                for t in range(c["tiles"] + (1 if c["parts"] else 0)):
                    if t < c["tiles"]:
                        g = par(c["gain"], t + (4 if c is n_na else 0))
                        if c["parts"] and t >= 3:
                            dve.wait_ge(xlo_ready, c["lo0"] + t - 2)
                        dve.scalar_tensor_tensor(out=c["dst"][t], in0=c["src"][t], scalar=g, in1=r,
                                                 op0=ALU.mult, op1=ALU.mult).then_inc(xn_ready, 1)
                    if c["parts"] and t >= 1:
                        dve.wait_ge(xn_ready, c["xn0"] + t)
                        dve.wait_ge(xhi_ready, c["lo0"] + t)
                        dve.tensor_tensor(c["parts"][1][t - 1], c["dst"][t - 1], c["parts"][0][t - 1].bitcast(f32),
                                          ALU.subtract).then_inc(xlo_ready, 1)
                if c["parts"]:
                    dve.wait_ge(xlo_ready, c["lo0"] + c["tiles"])
                dve.wait_ge(xn_ready, c["xn0"] + c["tiles"])
                dve.sem_inc(normed, 1)

            def norm(c):
                norm_inverse(c)
                norm_apply(c)

            dve.wait_ge(cst_loaded, 16)
            norm(n_mix)

            dve.wait_ge(cst_loaded, 16)
            free = list(range(40))

            def tmp():
                return small[:, free.pop(0), :]

            def ts(out, a, s1, s2, op0, op1=ALU.bypass):
                if s2 is None:
                    link(dve.tensor_scalar(out, a, s1, None, op0))
                else:
                    link(dve.tensor_scalar(out, a, s1, s2, op0, op1))

            def tt(out, a, b, op):
                link(dve.tensor_tensor(out, a, b, op))

            def tt_(out, a, b, op, signal=None):
                ins = dve.tensor_tensor(out, a, b, op)
                if signal is None:
                    link(ins)
                else:
                    ins.then_inc(signal, 1)
                    dve.wait_ge(signal, 1)

            def stt(out, a, s, b, op0, op1):
                link(dve.scalar_tensor_tensor(out=out, in0=a, scalar=s, in1=b, op0=op0, op1=op1))

            MAGIC = 12582912.0

            def exp_parts(x, w):
                k, r, p, t, ki = (tmp()[:, 0:w] for _ in range(5))
                ts(k, x, 1.4426950408889634, 1000.0, ALU.mult, ALU.min)
                ts(k, k, -1000.0, MAGIC, ALU.max, ALU.add)
                ts(k, k, MAGIC, None, ALU.subtract)
                stt(r, k, -0.693145751953125, x, ALU.mult, ALU.add)
                stt(r, k, -1.42860682030941723e-6, r, ALU.mult, ALU.add)
                ts(r, r, 0.5, -0.5, ALU.min, ALU.max)
                ts(p, r, 1.0 / 40320, 1.0 / 5040, ALU.mult, ALU.add)
                for c in (1.0 / 720, 1.0 / 120, 1.0 / 24, 1.0 / 6, 0.5, 1.0):
                    tt(p, p, r, ALU.mult)
                    ts(p, p, c, None, ALU.add)
                tt(p, p, r, ALU.mult)
                ts(t, k, 127.0, 0.0, ALU.add, ALU.max)
                ts(t, t, 254.0, 8388608.0, ALU.min, ALU.mult)
                link(dve.tensor_copy(ki.bitcast(i32), t))
                tt(p, p, ki, ALU.mult)
                return ki, p

            def keep(n):
                del free[:]
                free.extend(range(n, 40))

            lre, lim = par("lam_re", 0, 8), par("lam_im", 0, 8)
            dt, a, b = tmp(), tmp(), tmp()
            two_k, part = exp_parts(par("log_dt", 0, 8), 8)
            tt(dt, two_k, part, ALU.add)
            tt(a, lre, dt, ALU.mult)
            tt(b, lim, dt, ALU.mult)
            keep(3)
            em1, hs, hc = tmp(), tmp(), tmp()
            two_k, part = exp_parts(a, 8)
            tt(s5p[:, 0, :], two_k, part, ALU.add)
            ts(em1, two_k, -1.0, None, ALU.add)
            tt(em1, em1, part, ALU.add)
            keep(6)
            k, r, x2, s, c = tmp(), tmp(), tmp(), tmp(), tmp()
            ts(k, b, 0.15915494309189535, MAGIC, ALU.mult, ALU.add)
            ts(k, k, MAGIC, None, ALU.subtract)
            stt(r, k, -6.28125, b, ALU.mult, ALU.add)
            stt(r, k, -0.0019350051879882812, r, ALU.mult, ALU.add)
            stt(r, k, -3.019916050561733e-07, r, ALU.mult, ALU.add)
            ts(r, r, 0.5, None, ALU.mult)
            tt(x2, r, r, ALU.mult)

            def series(out, first, coefs):
                ts(out, x2, first, coefs[0], ALU.mult, ALU.add)
                for q in coefs[1:]:
                    tt(out, out, x2, ALU.mult)
                    ts(out, out, q, None, ALU.add)
            series(s, 1.0 / 6227020800, (-1.0 / 39916800, 1.0 / 362880, -1.0 / 5040, 1.0 / 120, -1.0 / 6, 1.0))
            tt(hs, s, r, ALU.mult)
            series(hc, 1.0 / 479001600, (-1.0 / 3628800, 1.0 / 40320, -1.0 / 720, 1.0 / 24, -0.5, 1.0))
            cm1, cosb, sinb, ere, eim, t1, l2, fre, fim = (tmp() for _ in range(9))
            tt(cm1, hs, hs, ALU.mult)
            ts(cm1, cm1, -2.0, None, ALU.mult)
            ts(s5p[:, 1, :], cm1, 1.0, None, ALU.add)
            tt(t1, hs, hc, ALU.mult)
            ts(s5p[:, 2, :], t1, 2.0, None, ALU.mult)
            tt(ere, em1, s5p[:, 1, :], ALU.mult)
            tt(ere, ere, cm1, ALU.add)
            tt(eim, s5p[:, 0, :], s5p[:, 2, :], ALU.mult)
            tt(l2, lre, lre, ALU.mult)
            tt(t1, lim, lim, ALU.mult)
            tt(l2, l2, t1, ALU.add)
            link(dve.reciprocal(l2, l2))
            tt(fre, ere, lre, ALU.mult)
            tt(t1, eim, lim, ALU.mult)
            tt(fre, fre, t1, ALU.add)
            tt(s5p[:, 3, :], fre, l2, ALU.mult)
            tt(fim, eim, lre, ALU.mult)
            tt(t1, ere, lim, ALU.mult)
            tt(fim, fim, t1, ALU.subtract)
            tt(s5p[:, 4, :], fim, l2, ALU.mult)
            ts(s5p[:, 25, :], s5p[:, 4, :], -1.0, None, ALU.mult)
            tt(s5p[:, 5, :], s5p[:, 1, :], s5p[:, 1, :], ALU.bypass) if False else link(dve.tensor_copy(s5p[:, 5, :], s5p[:, 1, :]))
            link(dve.tensor_copy(s5p[:, 6, :], s5p[:, 2, :]))
            for k2 in range(1, 10):
                c0, s0 = s5p[:, 3 + 2 * k2, :], s5p[:, 4 + 2 * k2, :]
                tt(t1, s0, s0, ALU.mult)
                ts(s5p[:, 5 + 2 * k2, :], t1, -2.0, 1.0, ALU.mult, ALU.add)
                tt(t1, c0, s0, ALU.mult)
                ts(s5p[:, 6 + 2 * k2, :], t1, 2.0, None, ALU.mult)
            keep(0)
            lam = par("rg_lam", 0, 2)
            na_, mx_, z, z2 = (tmp()[:, 0:2] for _ in range(4))
            ts(na_, lam, -1.0, None, ALU.mult)
            tt(na_, na_, lam, ALU.min)
            ts(mx_, lam, -1.0, 0.0, ALU.mult, ALU.max)
            two_k, part = exp_parts(na_, 2)
            tt(z, two_k, part, ALU.add)
            ts(z2, z, 2.0, None, ALU.add)
            link(dve.reciprocal(z2, z2))
            tt(z, z, z2, ALU.mult)
            tt(z2, z, z, ALU.mult)
            lg = tmp()[:, 0:2]
            ts(lg, z2, 2.0 / 17, 2.0 / 15, ALU.mult, ALU.add)
            for q in (13, 11, 9, 7, 5, 3, 1):
                tt(lg, lg, z2, ALU.mult)
                ts(lg, lg, 2.0 / q, None, ALU.add)
            tt(lg, lg, z, ALU.mult)
            tt(lg, lg, mx_, ALU.add)
            ts(sp4[:], lg, 4.0, None, ALU.mult)

            def biased(u):
                h, i = u // NT, u % NT
                k0, k1 = key_tiles(h, i)
                nk = (k1 - k0) * P
                n = use_s[u]
                if i == 0:
                    dve.wait_ge(strip_loaded[h % 2], 16 * (h // 2 + 1))
                dve.wait_ge(mm_done, done(n))
                if u >= 3:
                    dve.wait_ge(mm_done, done(use_t[u - 3]))
                st = STRIPS[h % 2]
                if h < 8:
                    bias = st[:, 896 - P * i:896 - P * i + nk]
                elif 2 <= i <= 5:
                    bias = st[:, NF:NF + NI]
                else:
                    bias = st[:, (3 + k0 - i) * P:(3 + k0 - i) * P + nk]
                w = nk if nk <= HALF else nk // 2

                def banks(ap):
                    return ap if w == nk else ap.rearrange("p (b w) -> p b w", w=w)
                scores = PS[n % SLOTS][:, 0:nk] if w == nk else PS[n % SLOTS][:, :].rearrange("p (b w) -> p b w", w=HALF)[:, :, 0:w]
                dve.tensor_tensor_reduce(out=banks(SB[u % 3][:, 0:nk]), in0=scores, in1=banks(bias), scale=-1.0,
                                         scalar=3.0e38, op0=ALU.add, op1=ALU.min,
                                         accum_out=negm[:, u % 4:u % 4 + 1]).then_inc(scores_ready, 1)

            def head_out(u):
                h, i = u // NT, u % NT
                rd = rden[:, u % 8:u % 8 + 1]
                dve.wait_ge(exp_done, u + 1)
                link(dve.reciprocal(rd, den[:, u % 8:u % 8 + 1]))
                dve.wait_ge(mm_done, done(use_o[u]))
                dve.tensor_scalar(Bp[i][:, h * DH:(h + 1) * DH], PS[use_o[u] % SLOTS][:, 0:DH], rd, None, ALU.mult).then_inc(heads_done, 1)

            for t in range(NU + LAG_O + 1):
                if t < NU:
                    biased(t)
                if 0 <= t - LAG_O - 1 < NU:
                    head_out(t - LAG_O - 1)
            norm_inverse(n_dil)
            norm_inverse(n_na)
            norm_apply(n_dil)
            norm_apply(n_na)

            def add_to_h(n0, base):
                for m in range(8):
                    dve.wait_ge(mm_done, done(n0 + m))
                    dve.tensor_tensor(Hp[m], PS[(n0 + m) % SLOTS][:, :], Hp[m], ALU.add).then_inc(h_ready, 1)

            dve.wait_ge(x_again, 16)
            add_to_h(P_OUT, 0)
            norm(n_ffn)

            def v3(name, n):
                return R(name).rearrange("p (t n) -> p t n", n=n)

            def bc(name, n):
                return R(name).unsqueeze(2).to_broadcast([P, NT, n])

            tie = mat("tie", 0, 4).unsqueeze(1).to_broadcast([P, NT, 4])
            dve.wait_ge(mm_done, done(P_ROUTE))
            link(dve.tensor_tensor(v3("L", 20), PS[P_ROUTE % SLOTS][:, 0:160].rearrange("p (t n) -> p t n", n=20),
                                   mat("bias20", 0, 20).unsqueeze(1).to_broadcast([P, NT, 20]), ALU.add))
            g4 = v3("L", 20)[:, :, 0:4]
            link(dve.tensor_reduce(R("gm"), g4, AX.X, ALU.max))
            dve.tensor_tensor(v3("gd", 4), g4, bc("gm", 4), ALU.subtract).then_inc(gdiff_ready, 1)

            def first_of_max(oh, vals, mx, t4):
                link(dve.tensor_tensor(v3(t4, 4), vals, bc(mx, 4), ALU.is_equal))
                link(dve.tensor_tensor(v3(t4, 4), v3(t4, 4), tie, ALU.mult))
                link(dve.tensor_reduce(R("tm"), v3(t4, 4), AX.X, ALU.max))
                link(dve.tensor_tensor(v3(oh, 4), v3(t4, 4), bc("tm", 4), ALU.is_equal))
            first_of_max("oh", g4, "gm", "t4")
            for g in range(N_GRP):
                sel = v3("oh", 4)[:, :, g:g + 1].to_broadcast([P, NT, 4])
                link(dve.tensor_tensor(v3("t5" if g else "v4", 4), v3("L", 20)[:, :, 4 + 4 * g:8 + 4 * g], sel, ALU.mult))
                if g:
                    link(dve.tensor_tensor(R("v4"), R("v4"), R("t5"), ALU.add))
            link(dve.tensor_reduce(R("m1"), v3("v4", 4), AX.X, ALU.max))
            first_of_max("o1", v3("v4", 4), "m1", "t4")
            link(dve.scalar_tensor_tensor(out=R("v4b"), in0=R("o1"), scalar=-3.0e38, in1=R("v4"), op0=ALU.mult, op1=ALU.add))
            link(dve.tensor_reduce(R("m2"), v3("v4b", 4), AX.X, ALU.max))
            first_of_max("o2", v3("v4b", 4), "m2", "t4")
            dve.tensor_tensor(R("d1"), R("m2"), R("m1"), ALU.subtract).then_inc(tdiff_ready, 1)
            for g in range(N_GRP):
                sel = v3("oh", 4)[:, :, g:g + 1].to_broadcast([P, NT, 4])
                dve.tensor_tensor(v3("s1", 16)[:, :, 4 * g:4 * g + 4], v3("o1", 4), sel, ALU.mult)
                last = dve.tensor_tensor(v3("s2", 16)[:, :, 4 * g:4 * g + 4], v3("o2", 4), sel, ALU.mult)
            link(last)
            dve.tensor_tensor(R("member"), R("s1"), R("s2"), ALU.add).then_inc(member_ready, 1)
            dve.wait_ge(gexp_done, 1)
            link(dve.tensor_reduce(R("gs"), v3("gd", 4), AX.X, ALU.add))
            dve.wait_ge(texp_done, 1)
            link(dve.tensor_scalar(R("w1"), R("d1"), 1.0, None, ALU.add))
            link(dve.tensor_tensor(R("w1"), R("w1"), R("gs"), ALU.mult))
            link(dve.reciprocal(R("w1"), R("w1")))
            link(dve.tensor_tensor(R("w2"), R("w1"), R("d1"), ALU.mult))

            def by_tile(name):
                return v3(name, 16)
            dve.wait_ge(mm_done, done(P_RANK))
            rank = PS[P_RANK % SLOTS][:, 0:P].rearrange("p (t e) -> p t e", e=16)
            link(dve.tensor_copy(R("tot"), PS[P_RANK % SLOTS][:, HALF:HALF + P]))
            base = R("base")
            link(dve.memset(base[:, 0:16], 0.0))
            for tt in range(NT):
                link(dve.tensor_tensor(base[:, 16 * tt + 16:16 * tt + 32], base[:, 16 * tt:16 * tt + 16],
                                       R("tot")[:, 16 * tt:16 * tt + 16], ALU.add))
            ts(R("nblk"), base[:, 128:144], 1.0 / P, 127.0 / 256, ALU.mult, ALU.add)
            ts(R("nblk"), R("nblk"), MAGIC, None, ALU.add)
            ts(R("nblk"), R("nblk"), MAGIC, None, ALU.subtract)
            link(dve.tensor_tensor_scan(R("ends"), ones[:, 0:16], R("nblk"), 0.0, ALU.mult, ALU.add))
            tt_(R("start"), R("ends"), R("nblk"), ALU.subtract)
            ts(R("start"), R("start"), float(P), None, ALU.mult)
            tt_(by_tile("tot"), rank, base[:, 0:128].rearrange("p (t e) -> p t e", e=16), ALU.add, rank_read)
            tt_(by_tile("tot"), by_tile("tot"), R("start").unsqueeze(1).to_broadcast([P, NT, 16]), ALU.add)
            for sel, p, pi in (("s1", "p1", "p1i"), ("s2", "p2", "p2i")):
                tt_(R(sel), R(sel), R("tot"), ALU.mult)
                link(dve.tensor_reduce(R(p), by_tile(sel), AX.X, ALU.add))
                link(dve.tensor_copy(R(pi).bitcast(i32), R(p)))
            cmp3 = R("cmp").rearrange("p (b e) -> p b e", e=16)
            tt_(cmp3, R("ends").unsqueeze(1).to_broadcast([P, NBLK, 16]),
                mat("blk", 0, NBLK).unsqueeze(2).to_broadcast([P, NBLK, 16]), ALU.is_le)
            link(dve.tensor_reduce(R("fe"), cmp3, AX.X, ALU.add))
            ts(R("fe"), R("fe"), float(N_EXP - 1), None, ALU.min)
            ts(R("fq"), R("fe"), 1.0, None, ALU.add)
            link(dve.tensor_copy(R("wait_i").bitcast(i32), R("fq")))
            ts(R("fq"), R("fe"), 1.0 / XBUF, -1.0 / XBUF, ALU.mult, ALU.add)
            ts(R("fq"), R("fq"), MAGIC, None, ALU.add)
            ts(R("fq"), R("fq"), MAGIC, None, ALU.subtract)
            stt(R("fq"), R("fq"), -float(XBUF), R("fe"), ALU.mult, ALU.add)
            ts(R("fq"), R("fq"), float(XPG * S), None, ALU.mult)
            link(dve.tensor_copy(R("page_i").bitcast(i32), R("fq")))
            ts(R("nblk"), R("ends"), 1.0, None, ALU.add)
            dve.tensor_copy(R("ends_i").bitcast(i32), R("nblk")).then_inc(dispatch_ready, 1)
            dve.sem_inc(blocks_done, 1)

            dve.wait_ge(x_scattered, 16 * 2 * NT)

            def block_up(b):
                dve.wait_ge(silu_ready, b + 1)
                if b >= 2:
                    dve.wait_ge(mm_done, done(use_h[b - 2]))
                dve.tensor_tensor(HA[b % 2], PS[use_g[b] % SLOTS][:, F_EXP:2 * F_EXP], SG[b % 2], ALU.mult).then_inc(up_ready, 1)

            def block_hT(b):
                dve.wait_ge(mm_done, done(use_h[b]))
                if b >= 2:
                    dve.wait_ge(mm_done, done(use_y[b - 2]))
                dve.tensor_copy(HAT[b % 2], PS[use_h[b] % SLOTS][:, 0:F_EXP]).then_inc(hT_ready, 1)

            def block_y(b):
                dve.wait_ge(mm_done, done(use_y[b]))
                dve.sem_inc(blocks_done, 1)
                if b >= 3:
                    dve.wait_ge(y_stored[b % 3], 16 * (b // 3))
                dve.tensor_copy(YB[b % 3], PS[use_y[b] % SLOTS][:, :]).then_inc(y_ready, 1)

            for t in range(1, NBLK + 2):
                for lag, stage in ((1, block_up), (2, block_y), (1, block_hT)):
                    if 0 <= t - lag < NBLK:
                        stage(t - lag)
            for tt in range(NT):
                k = (2 * tt) % 4
                a, b = YG[k], YG[k + 1]
                dve.wait_ge(y_gathered[k], 16 * (tt // 2 + 1))
                link(dve.tensor_scalar(a, a, R("w1")[:, tt:tt + 1], None, ALU.mult))
                dve.wait_ge(y_gathered[k + 1], 16 * (tt // 2 + 1))
                dve.scalar_tensor_tensor(out=b, in0=b, scalar=R("w2")[:, tt:tt + 1], in1=a, op0=ALU.mult,
                                         op1=ALU.add).then_inc(ysum_added, 1)
                dve.wait_ge(mm_done, done(P_YSUM + tt))
                cols = hT[:, :, tt * P:(tt + 1) * P]
                dve.tensor_tensor(cols, PS[(P_YSUM + tt) % SLOTS][:, :].rearrange("p (k n) -> p k n", n=P), cols,
                                  ALU.add).then_inc(ysum_ready, 1)
            norm(n_fin1)
            norm(n_att2)

            dve.wait_ge(s5_loaded, 32)
            bm, br = [Wp[10], Wp[11]], [Wp[12], Wp[13]]
            for j in range(8):
                cols = slice(j * P, (j + 1) * P)
                dve.tensor_scalar(br[0][:, cols], bm[0][:, cols], s5p[:, 4, j:j + 1], None, ALU.mult)
                last = dve.tensor_scalar(br[1][:, cols], bm[1][:, cols], s5p[:, 25, j:j + 1], None, ALU.mult)
            link(last)
            for j in range(8):
                cols = slice(j * P, (j + 1) * P)
                fr = s5p[:, 3, j:j + 1]
                dve.scalar_tensor_tensor(out=bm[0][:, cols], in0=bm[0][:, cols], scalar=fr, in1=br[1][:, cols],
                                         op0=ALU.mult, op1=ALU.add)
                last = dve.scalar_tensor_tensor(out=bm[1][:, cols], in0=bm[1][:, cols], scalar=fr, in1=br[0][:, cols],
                                                op0=ALU.mult, op1=ALU.add)
            last.then_inc(s5b_ready, 1)
            dve.tensor_scalar(Wp[18][:, 256:512], Wp[18][:, 256:512], -1.0, None, ALU.mult).then_inc(s5c_ready, 1)

            for c in range(2):
                x, y = Wp[PG_RX + c], Wp[19 + c]
                dve.wait_ge(in2_ready, c + 1)
                link(dve.tensor_scalar(y, x, par("rg_w", 6 + c), par("rg_cb", c), ALU.mult, ALU.add))
                for s_ in range(1, 4):
                    ins = dve.scalar_tensor_tensor(out=y[:, s_:S], in0=x[:, 0:S - s_], scalar=par("rg_w", 2 * (3 - s_) + c),
                                                   in1=y[:, s_:S], op0=ALU.mult, op1=ALU.add)
                    if s_ < 3:
                        link(ins)
                    else:
                        ins.then_inc(conv_ready, 1)
            dve.wait_ge(conv_ready, 2)
            for c in range(2):
                xc, th, ix, rc = Wp[19 + c], Wp[21 + c], Wp[23 + c], Wp[25 + c]
                dve.wait_ge(tanh_ready, c + 1)
                dve.tensor_scalar(rc, th, 1.0, None, ALU.add).then_inc(onep_ready, 1)
                dve.wait_ge(onep_ready, c + 1)
                link(dve.reciprocal(rc, rc))
                link(dve.tensor_tensor(ix, ix, xc, ALU.mult))
                link(dve.tensor_scalar(xc, rc, 2.0, -1.0, ALU.mult, ALU.add))
                dve.wait_ge(root_ready, c + 1)
                link(dve.tensor_tensor(rc, rc, th, ALU.mult))
                link(dve.tensor_tensor(ix, ix, rc, ALU.mult))
                link(dve.tensor_tensor_scan(Wp[PG_RX + c], xc, ix, 0.0, ALU.mult, ALU.add))

            dve.wait_ge(in2_ready, 4)

            def rg_out():
                for c in range(2):
                    dve.wait_ge(ggate_ready, c + 1)
                    dve.tensor_tensor(Wp[PG_RX + c], Wp[PG_RX + c], Wp[PG_RG + c], ALU.mult).then_inc(rg_ready, 1)
                dve.wait_ge(rg_ready, 2)
                for c in range(2):
                    last = dve.tensor_scalar(YS[c], Wp[PG_U + c], par("s5_d", c), None, ALU.mult)
                link(last)

            def s5_out(j):
                r = slice(32 * (j % 4), 32 * (j % 4) + 32)
                dve.wait_ge(mm_done, done(P_CX[j]))
                dve.tensor_tensor(YS[j // 4][r, :], PS[P_CX[j] % SLOTS][r, :], YS[j // 4][r, :], ALU.add).then_inc(s5y_ready, 1)

            for j in range(8):
                rr = s5p[:, 0, j:j + 1]
                ec, es, vr, vi = EC[j % 2], ES[j % 2], VR[j % 2], VI[j % 2]
                if j >= 2:
                    dve.wait_ge(s5x_ready, j - 1)
                dve.memset(ec[:, 0:1], 1.0)
                link(dve.memset(es[:, 0:1], 0.0))
                for k2 in range(10):
                    n = 1 << k2
                    wc, ws = s5p[:, 5 + 2 * k2, j:j + 1], s5p[:, 6 + 2 * k2, j:j + 1]
                    dve.tensor_scalar(TA[:, 0:n], es[:, 0:n], ws, None, ALU.mult)
                    link(dve.tensor_scalar(TB[:, 0:n], ec[:, 0:n], ws, None, ALU.mult))
                    dve.scalar_tensor_tensor(out=ec[:, n:2 * n], in0=ec[:, 0:n], scalar=wc, in1=TA[:, 0:n],
                                             op0=ALU.mult, op1=ALU.subtract)
                    link(dve.scalar_tensor_tensor(out=es[:, n:2 * n], in0=es[:, 0:n], scalar=wc, in1=TB[:, 0:n],
                                                  op0=ALU.mult, op1=ALU.add))
                dve.wait_ge(mm_done, done(P_BU[j] + 1))
                if j >= 2:
                    dve.wait_ge(mm_done, done(P_CX[j - 2]))
                bre, bim = PS[P_BU[j] % SLOTS][:, :], PS[(P_BU[j] + 1) % SLOTS][:, :]
                dve.tensor_tensor(vr, bre, ec, ALU.mult)
                dve.tensor_tensor(TA, bim, es, ALU.mult)
                dve.tensor_tensor(vi, bim, ec, ALU.mult)
                dve.tensor_tensor(TB, bre, es, ALU.mult).then_inc(s5in_ready, 1)
                dve.wait_ge(s5in_ready, j + 1)
                dve.tensor_tensor(vr, vr, TA, ALU.add)
                link(dve.tensor_tensor(vi, vi, TB, ALU.subtract))
                dve.tensor_tensor_scan(vr, rr.to_broadcast([P, S]), vr, 0.0, ALU.mult, ALU.add)
                dve.tensor_tensor_scan(vi, rr.to_broadcast([P, S]), vi, 0.0, ALU.mult, ALU.add).then_inc(s5v_ready, 1)
                if j == 0:
                    rg_out()
                else:
                    s5_out(j - 1)
            s5_out(7)
            dve.wait_ge(s5s_ready, 2)
            for c in range(2):
                dve.tensor_tensor(Wp[c], Wp[c], Wp[22 - c], ALU.mult).then_inc(s5_ready, 1)
            norm_inverse(n_rg)
            norm_inverse(n_s5)
            norm_apply(n_rg)
            norm_apply(n_s5)

            bcp, ex = pair(25), pair(27)
            for m in range(2):
                n = P_GK + m
                dve.wait_ge(mm_done, done(n))
                x = PS[n % SLOTS][:, :]
                dve.tensor_scalar(Wp[25 + m], x, par("gk_bias", m), None, ALU.add).then_inc(gk_biased, 1)
                dve.wait_ge(gk_biased, m + 1)
                dve.scalar_tensor_tensor(out=Wp[27 + m], in0=Wp[25 + m], scalar=-1.0, in1=Wp[25 + m], op0=ALU.mult, op1=ALU.max).then_inc(gk_abs, 1)
                link(dve.tensor_scalar(Wp[25 + m], Wp[25 + m], 0.0, 1.0 / 16, ALU.min, ALU.mult))
            link(dve.memset(Wp[4], 1.0))
            link(dve.memset(Wp[4].rearrange("p (n c) -> p n c", c=CH)[:, :, 0:1], 0.0))
            dve.wait_ge(gk_ln, 1)
            link(dve.scalar_tensor_tensor(out=bcp, in0=ex, scalar=-1.0 / 16, in1=bcp, op0=ALU.mult, op1=ALU.add))
            for m in range(2):
                last = dve.tensor_tensor_scan(Wp[25 + m], Wp[4], Wp[25 + m], 0.0, ALU.mult, ALU.add)
            link(last)
            q, k = pair(PG_Q), pair(PG_K)

            def chunks(ap):
                return ap.rearrange("p a (n c) -> p (a n) c", c=CH)
            b3 = chunks(bcp)
            mid = b3[:, :, CH // 2 - 1:CH // 2].to_broadcast([P, 2 * NCH, CH])
            end = b3[:, :, CH - 1:CH].to_broadcast([P, 2 * NCH, CH])
            dve.tensor_tensor(chunks(ex), b3, mid, ALU.subtract).then_inc(bc_ready, 1)
            dve.wait_ge(gexps, 1)
            link(dve.tensor_tensor(pair(4), q, ex, ALU.mult))
            dve.tensor_tensor(chunks(ex), mid, b3, ALU.subtract).then_inc(gexps_used, 1)
            dve.wait_ge(gexps, 2)
            link(dve.tensor_tensor(pair(19), k, ex, ALU.mult))
            dve.tensor_tensor(chunks(ex), end, b3, ALU.subtract).then_inc(gexps_used, 1)
            dve.wait_ge(gexps, 3)
            dve.tensor_tensor(k, k, ex, ALU.mult).then_inc(gprods, 1)
            dve.wait_ge(gexps, 4)
            dve.tensor_tensor(q, q, ex, ALU.mult).then_inc(gprods, 1)
            dve.wait_ge(gprods, 2)
            dve.wait_ge(decay_ready, 1)
            st = [pair(23).rearrange("p a (b c) -> p (a b) c", c=P), pair(8).rearrange("p a (b c) -> p (a b) c", c=P)]
            for m in range(2):
                for q4 in range(4):
                    n_ = P_KV + 4 * m + q4
                    dve.wait_ge(mm_done, done(n_))
                    for j in range(4):
                        n = 4 * q4 + j
                        if n == NCH - 1:
                            continue
                        for hh in range(2):
                            r = slice(hh * DH, (hh + 1) * DH)
                            c0 = (j % 2) * HALF + (j // 2) * 256 + hh * P
                            kv = PS[n_ % SLOTS][r, c0:c0 + P]
                            if n == 0:
                                last = dve.tensor_copy(st[m][r, 1, :], kv)
                            else:
                                last = dve.scalar_tensor_tensor(out=st[m][r, n + 1, :], in0=st[m][r, n, :],
                                                                scalar=decay[r, m, n:n + 1], in1=kv,
                                                                op0=ALU.mult, op1=ALU.add)
                        if j < 3 and n < NCH - 2:
                            link(last)
                    last.then_inc(state_ready, 1)
                    dve.wait_ge(state_ready, 4 * m + q4 + 1)
            causal = mat("causal").bitcast(i32)
            for h in range(4):
                n = P_SC + h
                if h == 3:
                    dve.wait_ge(mm_done, done(P_KV + 7))
                link(dve.memset(Mp[h], 0.0))
                dve.wait_ge(mm_done, done(n))
                for tt_ in range(NT):
                    cols = slice(tt_ * P, (tt_ + 1) * P)
                    last = dve.copy_predicated(Mp[h][:, cols], causal, PS[n % SLOTS][:, cols])
                last.then_inc(intra_ready, 1)
            for h in range(4):
                norm_c = n_gla[h]
                norm(norm_c)
                dve.wait_ge(gsilu, h + 1)
                dve.tensor_tensor(Bp[h], Bp[h], Wp[PG_G + h], ALU.mult).then_inc(gla_ready, 1)
            add_to_h(P_OUT2, 8)
            norm(n_mlp)

            for what, i in FFN_STEPS:
                if what == "down":
                    add_to_h(P_DOWN[i], 16 + 8 * i)
                    continue
                j, n = i, P_UP[i]
                y, x = Wp[22 + j % 3], PS[n % SLOTS]
                dve.wait_ge(conv0_ready, j + 1)
                link(dve.scalar_tensor_tensor(out=y[:, 1:S], in0=x[:, 0:S - 1], scalar=par("ff_w", FF + j), in1=y[:, 1:S],
                                              op0=ALU.mult, op1=ALU.add))
                dve.scalar_tensor_tensor(out=y[:, 2:S], in0=x[:, 0:S - 2], scalar=par("ff_w", j), in1=y[:, 2:S],
                                         op0=ALU.mult, op1=ALU.add).then_inc(conv1_ready, 1)
                dve.wait_ge(gelu_ready, j + 1)
                dve.wait_ge(mm_done, done(n + 1))
                dve.tensor_tensor(y, PS[(n + 1) % SLOTS][:, :], y, ALU.mult).then_inc(prod_ready, 1)
                dve.wait_ge(prod_ready, j + 1)
                dve.wait_ge(ffhi_ready, j + 1)
                dve.tensor_tensor(FLO[j % FF_KEEP], y, FHI_F[j % FF_KEEP], ALU.subtract).then_inc(ffact_ready, 1)
            norm(n_fin2)


def dilated_strips():
    d = np.arange(STRIP)[None, :] - 896 - np.arange(P)[:, None]
    ad = np.abs(d)
    count = ((ad <= 64).astype(int) + ((d % 4 == 0) & (ad <= 256)) + (d % 16 == 0))
    base = np.where(count > 0, np.log(np.maximum(count, 1)), NEG)
    slopes = 2.0 ** -np.arange(1, 9)
    return np.stack([np.where(count > 0, base - s * ad, NEG) for s in slopes]).astype(np.float32)


def neighbourhood_strips(rpb):
    q, k = np.arange(P), np.arange(NF)
    qr, qc = (q // 64)[:, None], (q % 64)[:, None]
    kr, kc = (k // 64 - 6)[None, :], (k % 64)[None, :]
    dr, dc = kr - qr + 7, kc - qc + 15
    cs = np.clip(qc - 8, 0, 48)
    col_ok = (kc >= cs) & (kc < cs + 16)
    ok = col_ok & (dr >= 0) & (dr <= 14)
    full = np.where(ok, rpb[:, np.clip(dr, 0, 14), np.clip(dc, 0, 30)], np.float32(NEG))
    rows = (kr >= qr - 4) & (kr < qr + 4)
    inner = np.where(rows, full, np.float32(NEG))[:, :, P:P + NI]
    return np.ascontiguousarray(np.concatenate([full, inner], axis=2))


def column_units(w):
    k, m = w.shape
    return np.ascontiguousarray(w.reshape(k // P, P, m // P, P).transpose(2, 1, 0, 3).reshape(m // P, P, (k // P) * P))


def pack(i):
    f = np.float32

    def tiles(v):
        return np.asarray(v, f).reshape(-1, P).T
    x = np.asarray(i["x"])[0]
    cst = np.zeros((P, NCOL), f)

    def put(name, a, cols=PCOLS):
        a = np.asarray(a, f)
        cst[:a.shape[0], cols[name]:cols[name] + a.shape[1]] = a
    put("norm_mix", tiles(i["norm_mix_g"][0]))
    put("g_out", np.concatenate([tiles(i["g_out_dil"][0]), tiles(i["g_out_na"][0])], 1))
    put("norm_ffn", tiles(i["norm_ffn_g"][0]))
    put("norm_final", tiles(i["norm_final_g"]))
    put("attn_norm", tiles(i["attn_norm_2"][0]))
    put("gk_bias", tiles(i["gla_b_gk_2"][0]))
    put("gla_norm", tiles(i["gla_norm_2"][0]))
    put("lam_re", tiles(i["s5_lambda_re_2"][0].reshape(-1)))
    put("lam_im", tiles(i["s5_lambda_im_2"][0].reshape(-1)))
    put("log_dt", tiles(np.repeat(i["s5_log_dt_2"][0], 64)))
    put("s5_d", tiles(i["s5_d_2"][0]))
    put("b_glu", tiles(i["s5_b_glu_2"][0]))
    put("s5_norm", tiles(i["s5_norm_2"][0]))
    put("rg_w", np.concatenate([tiles(i["rg_conv_w_2"][0][t]) for t in range(4)], 1))
    put("rg_cb", tiles(i["rg_conv_b_2"][0]))
    put("rg_ba", tiles(i["rg_b_a_2"][0]))
    put("rg_bx", tiles(i["rg_b_x_2"][0]))
    put("rg_lam", tiles(i["rg_lambda_2"][0]))
    put("rg_norm", tiles(i["rg_norm_2"][0]))
    put("mlp_norm", tiles(i["mlp_norm_2"][0]))
    put("ff_w", np.concatenate([tiles(i["mlp_conv_w_2"][0][t]) for t in range(3)], 1))
    put("ff_cb", tiles(i["mlp_conv_b_2"][0]))
    put("final_norm", tiles(i["final_norm_2"]))
    put("ones", np.ones((P, P)), MCOLS)
    put("ident", np.eye(P), MCOLS)
    s, c = np.arange(P)[:, None], np.arange(P)[None, :]
    put("causal", ((c >= s) & (c // CH == s // CH)).astype(f), MCOLS)
    route = np.concatenate([i["w_group"][0], i["w_router"][0]], 1)
    put("route", route.reshape(NT, P, 20).transpose(1, 0, 2).reshape(P, -1), MCOLS)
    w2 = np.asarray(i["w_in_2"][0])
    put("low", w2[:, 1536:1552].reshape(NT, P, 16).transpose(1, 0, 2).reshape(P, -1), MCOLS)
    rg = np.zeros((P, 4, P), f)
    for j, name in enumerate(("rg_w_a_2", "rg_w_x_2")):
        for h in range(4):
            r = (h % 2) * 64
            rg[r:r + 64, 2 * j + h // 2, r:r + 64] = i[name][0][h]
    put("rg", rg.reshape(P, -1), MCOLS)
    put("glu", np.asarray(i["s5_w_glu_2"][0]).reshape(2, P, 256).transpose(1, 0, 2).reshape(P, -1), MCOLS)
    put("gkup", i["gla_w_gk_up_2"][0], MCOLS)
    put("bias20", np.broadcast_to(np.concatenate([i["b_group"][0], i["b_router"][0]])[None], (P, 20)), MCOLS)
    put("before", (s < c).astype(f), MCOLS)
    put("blk", np.broadcast_to(np.arange(NBLK)[None], (P, NBLK)), MCOLS)
    put("tie", np.broadcast_to(np.array([4.0, 3.0, 2.0, 1.0])[None], (P, 4)), MCOLS)

    w = np.asarray(i["w_in"][0])
    cols = {"dil": [w[:, 512 * n:512 * (n + 1)] for n in range(3)], "na": [w[:, 1536 + 512 * n:1536 + 512 * (n + 1)] for n in range(3)]}
    w_in = column_units(np.concatenate([cols["dil"][0], cols["na"][0], cols["dil"][1], cols["na"][1], cols["dil"][2], cols["na"][2]], 1))
    gate, up = (np.asarray(i[n][0]).reshape(N_EXP, NT, P, F_EXP) for n in ("w_gate", "w_up"))
    gu = np.concatenate([gate, up], 3).transpose(0, 2, 1, 3).reshape(N_EXP, P, 4 * S)
    dn = np.asarray(i["w_down"][0]).reshape(N_EXP, 2, P, D).transpose(0, 2, 1, 3).reshape(N_EXP, P, 2 * S)
    moe = np.concatenate([gu, dn], 2)
    w_in2 = column_units(np.concatenate([w2[:, 1808:2064], w2[:, 1552:1808], w2[:, 2064:2320], w2[:, 0:512], w2[:, 1024:1536], w2[:, 512:1024]], 1))
    up_u = column_units(i["w_up_2"][0])
    w_up = np.stack([up_u[j // 2 + (j % 2) * FF] for j in range(2 * FF)])
    down = column_units(np.concatenate([i["w_down_2"][0], np.zeros((2 * P, D), f)], 0))
    w_down = np.ascontiguousarray(down.reshape(8, P, 4, 6 * P).transpose(2, 0, 1, 3).reshape(32, P, 6 * P))
    bm, cm = np.zeros((P, 2, 8, P), f), np.zeros((P, 2, 8, 32), f)
    for g in range(16):
        r, j, c0 = (g % 2) * 64, g // 2, (g % 8) * 16
        for n, part in enumerate(("re", "im")):
            bm[r:r + 64, n, j, c0:c0 + 16] = i[f"s5_b_{part}_2"][0][g]
            cm[r:r + 64, n, j, (g % 2) * 16:(g % 2) * 16 + 16] = i[f"s5_c_{part}_2"][0][g].T
    return {
        "xT": np.ascontiguousarray(x.T.reshape(NT, P, S).transpose(1, 0, 2)),
        "params": cst, "w_in_units": w_in, "w_out_units": column_units(i["w_out"][0]), "w_moe": moe,
        "w_in2_units": w_in2, "w_out2_units": column_units(i["w_out_2"][0]), "w_up_units": w_up, "w_down_units": w_down,
        "dil_strip": dilated_strips(), "na_strip": neighbourhood_strips(np.asarray(i["rpb"][0])),
        "s5_b": bm.reshape(P, 2, 8 * P), "s5_c": cm.reshape(P, 512),
    }


def kernel(**inputs):
    import concourse.bacc as bacc
    from concourse.bass_utils import run_bass_kernel_spmd

    nc = bacc.Bacc("TRN2", target_bir_lowering=False, num_devices=1)
    arrays = pack({k: np.asarray(v) for k, v in inputs.items()})
    args = [nc.dram_tensor(k, a.shape, mybir.dt.from_np(a.dtype), kind="ExternalInput").ap() for k, a in arrays.items()]
    args.append(nc.dram_tensor("outT", (P, NT, S), mybir.dt.float32, kind="ExternalOutput").ap())
    build(nc, *args)
    r = run_bass_kernel_spmd(nc, [arrays], core_ids=[0])
    got = r.results[0]["outT"]
    return np.ascontiguousarray(got.transpose(1, 0, 2).reshape(D, S).T).reshape(1, S, D)
```
